# Optimizing a Trainium2 kernel written in Bass

```python
import math
import jax, jax.numpy as jnp
from jax import lax
import numpy as np

D_MODEL = 1024
BATCH = 1
SEQ = 512
DEPTH = 1
DEC_BATCH = 8
DEC_SEQ = 8
PAST_LEN = 4096
PAGE_SIZE = 128

N_META = 16
D_MIX = D_MODEL
N_HEADS_DN = 4
DK = 128
DV = 128
DK_TOT = N_HEADS_DN * DK
DV_TOT = N_HEADS_DN * DV
QKV_DIM = 2 * DK_TOT + DV_TOT
SHORT_CONV = 4
CHUNK = 64
C_CONV = D_MIX - DV_TOT
CONV_WIDTH = 31
D_FF = 2816
D_IN = QKV_DIM + DV_TOT + 2 * N_HEADS_DN + 2 * C_CONV
EPS = 1e-6

kernel_name = 'hybrid_gdn_conformer_conv_decoder_step'

def rmsnorm(x, g):
    x32 = x.astype(jnp.float32)
    y = x32 * lax.rsqrt(jnp.mean(x32 * x32, axis=-1, keepdims=True) + EPS)
    return (y * g.astype(jnp.float32)).astype(x.dtype)

def l2norm(x):
    return x * lax.rsqrt(jnp.sum(x * x, axis=-1, keepdims=True) + EPS)

def swiglu_half(h, g, w1, w3, w2):
    u = rmsnorm(h, g)
    return h + 0.5 * ((jax.nn.silu(u @ w1) * (u @ w3)) @ w2)

def causal_dwconv(x_ext, w):
    c = x_ext.shape[-1]
    return lax.conv_general_dilated(x_ext, w[:, None, :].astype(x_ext.dtype), window_strides=(1,),
                                    padding='VALID', dimension_numbers=('NWC', 'WIO', 'NWC'),
                                    feature_group_count=c)

def gated_delta_chunked(q, k, v, g, beta, s0, chunk):
    b, L, h, _ = q.shape
    pad = (-L) % chunk
    if pad:
        pz = lambda t: jnp.pad(t, [(0, 0), (0, pad)] + [(0, 0)] * (t.ndim - 2))
        q, k, v, g, beta = pz(q), pz(k), pz(v), pz(g), pz(beta)
    n = (L + pad) // chunk
    blk = lambda t: t.reshape(b, n, chunk, h, t.shape[-1]).transpose(0, 3, 1, 2, 4)
    q, k, v = blk(q), blk(k), blk(v)
    g = g.reshape(b, n, chunk, h).transpose(0, 3, 1, 2)
    beta = beta.reshape(b, n, chunk, h).transpose(0, 3, 1, 2)
    gc = jnp.cumsum(g, axis=-1)
    idx = jnp.arange(chunk)
    causal = idx[:, None] >= idx[None, :]
    strict = (idx[:, None] > idx[None, :]).astype(jnp.float32)
    decay = jnp.exp(jnp.where(causal, gc[..., :, None] - gc[..., None, :], -jnp.inf))
    kb = k * beta[..., None]
    vb = v * beta[..., None]
    a_mat = jnp.einsum('bhncd,bhnsd->bhncs', kb, k) * decay * strict
    m_mat = jnp.eye(chunk, dtype=jnp.float32) + a_mat
    rhs = jnp.concatenate([vb, kb * jnp.exp(gc)[..., None]], axis=-1)
    sol = lax.linalg.triangular_solve(m_mat, rhs, left_side=True, lower=True, unit_diagonal=True)
    u_c, w_c = sol[..., :DV], sol[..., DV:]
    att = jnp.einsum('bhncd,bhnsd->bhncs', q, k) * decay

    def step(s, xs):
        q_i, k_i, u_i, w_i, att_i, gc_i = xs
        v_new = u_i - jnp.einsum('bhck,bhkv->bhcv', w_i, s)
        o = (jnp.einsum('bhck,bhkv->bhcv', q_i * jnp.exp(gc_i)[..., None], s)
             + jnp.einsum('bhcs,bhsv->bhcv', att_i, v_new))
        g_last = gc_i[..., -1]
        s = (s * jnp.exp(g_last)[..., None, None]
             + jnp.einsum('bhck,bhcv->bhkv', k_i * jnp.exp(g_last[..., None] - gc_i)[..., None], v_new))
        return s, o

    first = lambda t: jnp.moveaxis(t, 2, 0)
    s_fin, o = lax.scan(step, s0, (first(q), first(k), first(u_c), first(w_c), first(att), first(gc)))
    o = o.transpose(1, 0, 3, 2, 4).reshape(b, n * chunk, h, DV)[:, :L]
    return o, s_fin

def hybrid_mixer(h, s_delta, s_qkv, s_conv, n_lead, norm_g, w_in, qkv_conv_w, a_log, dt_bias,
                 o_norm_g, conv_w, conv_b, conv_norm_g, w_out):
    f32 = jnp.float32
    bn, L, _ = h.shape
    u = rmsnorm(h, norm_g)
    p = u @ w_in
    cut = np.cumsum([QKV_DIM, DV_TOT, N_HEADS_DN, N_HEADS_DN]).tolist()
    qkv_pre, z, b_raw, a_raw, glu = jnp.split(p, cut, axis=-1)
    qkv_ext = jnp.concatenate([s_qkv.astype(p.dtype), qkv_pre], axis=1)
    new_s_qkv = qkv_ext[:, -(SHORT_CONV - 1):]
    qkv = jax.nn.silu(causal_dwconv(qkv_ext, qkv_conv_w)).astype(f32)
    q, k, v = jnp.split(qkv, [DK_TOT, 2 * DK_TOT], axis=-1)
    q = l2norm(q.reshape(bn, L, N_HEADS_DN, DK)) * (DK ** -0.5)
    k = l2norm(k.reshape(bn, L, N_HEADS_DN, DK))
    v = v.reshape(bn, L, N_HEADS_DN, DV)
    beta = jax.nn.sigmoid(b_raw.astype(f32))
    g = -jnp.exp(a_log.astype(f32)) * jax.nn.softplus(a_raw.astype(f32) + dt_bias.astype(f32))
    s = s_delta.astype(f32)
    segments = [(0, n_lead), (n_lead, L)] if n_lead > 0 else [(0, L)]
    outs = []
    for lo, hi in segments:
        o_seg, s = gated_delta_chunked(q[:, lo:hi], k[:, lo:hi], v[:, lo:hi], g[:, lo:hi], beta[:, lo:hi],
                                       s, min(CHUNK, hi - lo))
        outs.append(o_seg)
    o = jnp.concatenate(outs, axis=1)
    o = rmsnorm(o, o_norm_g) * jax.nn.silu(z.astype(f32).reshape(bn, L, N_HEADS_DN, DV))
    o = o.reshape(bn, L, DV_TOT).astype(h.dtype)
    val, gate = jnp.split(glu, 2, axis=-1)
    c_in = val * jax.nn.sigmoid(gate)
    c_ext = jnp.concatenate([s_conv.astype(c_in.dtype), c_in], axis=1)
    new_s_conv = c_ext[:, -(CONV_WIDTH - 1):]
    c = causal_dwconv(c_ext, conv_w) + conv_b
    c = jax.nn.silu(rmsnorm(c, conv_norm_g))
    mix = jnp.concatenate([o, c], axis=-1) @ w_out
    return h + mix, s.astype(h.dtype), new_s_qkv, new_s_conv

def decoder_layer(h, s_delta, s_qkv, s_conv, n_lead, ffn1, mixp, ffn2):
    h = swiglu_half(h, *ffn1)
    h, sd, sq, sc = hybrid_mixer(h, s_delta, s_qkv, s_conv, n_lead, *mixp)
    h = swiglu_half(h, *ffn2)
    return h, sd, sq, sc

def setup_inputs(seed: int = 0) -> dict:
    key = jax.random.key(seed)
    ks = jax.random.split(key, 25)
    f32 = jnp.float32
    nrm = lambda i, shape, scale: jax.random.normal(ks[i], shape, f32) * scale
    gain = lambda i, shape: 1.0 + 0.05 * jax.random.normal(ks[i], shape, f32)
    a_log = jnp.log(jax.random.uniform(ks[13], (DEPTH, N_HEADS_DN), f32, 1.0, 16.0))
    dt = jnp.exp(jax.random.uniform(ks[14], (DEPTH, N_HEADS_DN), f32, math.log(1e-3), math.log(1e-1)))
    dt_bias = dt + jnp.log(-jnp.expm1(-dt))
    return {
        'x_prompt': nrm(0, (BATCH, SEQ, D_MODEL), 1.0),
        'x_sample': nrm(1, (DEC_BATCH, DEC_SEQ, D_MODEL), 1.0),
        'state_delta': nrm(2, (DEPTH, DEC_BATCH, N_HEADS_DN, DK, DV), 0.5),
        'state_qkv_conv': nrm(3, (DEPTH, DEC_BATCH, SHORT_CONV - 1, QKV_DIM), 1.0),
        'state_conv': nrm(4, (DEPTH, DEC_BATCH, CONV_WIDTH - 1, C_CONV), 1.0),
        'meta_tokens': nrm(5, (N_META, D_MODEL), 1.0),
        'ffn1_norm': gain(6, (DEPTH, D_MODEL)),
        'ffn1_w1': nrm(7, (DEPTH, D_MODEL, D_FF), D_MODEL ** -0.5),
        'ffn1_w3': nrm(8, (DEPTH, D_MODEL, D_FF), D_MODEL ** -0.5),
        'ffn1_w2': nrm(9, (DEPTH, D_FF, D_MODEL), D_FF ** -0.5),
        'mix_norm': gain(10, (DEPTH, D_MODEL)),
        'w_in': nrm(11, (DEPTH, D_MODEL, D_IN), D_MODEL ** -0.5),
        'qkv_conv_w': nrm(12, (DEPTH, SHORT_CONV, QKV_DIM), SHORT_CONV ** -0.5),
        'a_log': a_log,
        'dt_bias': dt_bias,
        'o_norm': gain(15, (DEPTH, DV)),
        'conv_w': nrm(16, (DEPTH, CONV_WIDTH, C_CONV), CONV_WIDTH ** -0.5),
        'conv_b': nrm(17, (DEPTH, C_CONV), 0.02),
        'conv_norm': gain(18, (DEPTH, C_CONV)),
        'w_out': nrm(19, (DEPTH, D_MIX, D_MODEL), D_MIX ** -0.5),
        'ffn2_norm': gain(20, (DEPTH, D_MODEL)),
        'ffn2_w1': nrm(21, (DEPTH, D_MODEL, D_FF), D_MODEL ** -0.5),
        'ffn2_w3': nrm(22, (DEPTH, D_MODEL, D_FF), D_MODEL ** -0.5),
        'ffn2_w2': nrm(23, (DEPTH, D_FF, D_MODEL), D_FF ** -0.5),
        'final_norm': gain(24, (D_MODEL,)),
    }

def reference(x_prompt, x_sample, state_delta, state_qkv_conv, state_conv, meta_tokens,
              ffn1_norm, ffn1_w1, ffn1_w3, ffn1_w2, mix_norm, w_in, qkv_conv_w, a_log, dt_bias,
              o_norm, conv_w, conv_b, conv_norm, w_out, ffn2_norm, ffn2_w1, ffn2_w3, ffn2_w2, final_norm):
    dt = x_prompt.dtype
    bp = x_prompt.shape[0]
    meta = jnp.broadcast_to(meta_tokens.astype(dt)[None], (bp, N_META, D_MODEL))
    hp = jnp.concatenate([meta, x_prompt], axis=1)
    hs = x_sample
    dp, qp, cp, ds, qs, cs = [], [], [], [], [], []
    for l in range(DEPTH):
        ffn1 = (ffn1_norm[l], ffn1_w1[l], ffn1_w3[l], ffn1_w2[l])
        ffn2 = (ffn2_norm[l], ffn2_w1[l], ffn2_w3[l], ffn2_w2[l])
        mixp = (mix_norm[l], w_in[l], qkv_conv_w[l], a_log[l], dt_bias[l], o_norm[l],
                conv_w[l], conv_b[l], conv_norm[l], w_out[l])
        zd = jnp.zeros((bp, N_HEADS_DN, DK, DV), dt)
        zq = jnp.zeros((bp, SHORT_CONV - 1, QKV_DIM), dt)
        zc = jnp.zeros((bp, CONV_WIDTH - 1, C_CONV), dt)
        hp, sd, sq, sc = decoder_layer(hp, zd, zq, zc, N_META, ffn1, mixp, ffn2)
        dp.append(sd); qp.append(sq); cp.append(sc)
        hs, sd, sq, sc = decoder_layer(hs, state_delta[l], state_qkv_conv[l], state_conv[l], 0, ffn1, mixp, ffn2)
        ds.append(sd); qs.append(sq); cs.append(sc)
    y_prompt = rmsnorm(hp, final_norm)[:, N_META:]
    y_sample = rmsnorm(hs, final_norm)
    return (y_prompt, y_sample, jnp.stack(dp), jnp.stack(qp), jnp.stack(cp),
            jnp.stack(ds), jnp.stack(qs), jnp.stack(cs))


_drawn_inputs = setup_inputs


def setup_inputs(seed=0):
    import zlib

    import numpy as np

    out = dict(_drawn_inputs(seed))
    spreads = {}
    factors = {'o_norm': 3.228, 'conv_b': 4.252, 'conv_norm': 2.72, 'ffn2_norm': 3.381}
    for name, (base, spread) in spreads.items():
        noise = np.random.default_rng([zlib.crc32(name.encode()), seed]).standard_normal(out[name].shape)
        drawn = base * np.exp(spread * noise) if base else spread * noise
        out[name] = __import__('jax').numpy.asarray(drawn.astype(out[name].dtype))
    for name, factor in factors.items():
        out[name] = (out[name] * factor).astype(out[name].dtype)
    return out
```

```python
from contextlib import ExitStack

import numpy as np
import concourse.bass as bass
from concourse import mybir

F32 = mybir.dt.float32
F32R = mybir.dt.float32r
ACT = mybir.ActivationFunctionType
ALU = mybir.AluOpType

P = 128
D = 1024
KT = D // P
SEQ_LEN, N_META = 512, 16
L = SEQ_LEN + N_META
NB, LB = 8, 8
TOK = L + NB * LB
HALF = TOK // 2
FT = 2816 // P
PARTS = [8, 8, 6]
H = 4
NQ = 3 * H
NC_ = 4
SC, CW = 4, 31
POOL_TAPS = 3 * (CW - 1)
EPS = 1e-6

U_FFN1 = 0
FFN_UNITS = 2 * FT + 8 * len(PARTS)
U_GLU = U_FFN1 + FFN_UNITS
U_QKV = U_GLU + 2 * NC_
U_Z = U_QKV + NQ
U_OUT = U_Z + H
U_FFN2 = U_OUT + 8
U_END = U_FFN2 + FFN_UNITS
assert all(u % 4 == 0 for u in (U_FFN1, U_GLU, U_QKV, U_Z, U_OUT, U_FFN2, U_END))

QP = SC - 1 + L
QS = SC - 1 + LB
QE = QP + NB * QS
QO = QE - (SC - 1)
CP = CW - 1 + L
CS = CW - 1 + LB
CE = CP + NB * CS

TILES = [(128 * t, 128) for t in range(4)] + [(512, 80)]
NT = len(TILES)
NG = 1 + NB
GROUPS = [(0, 16)] + [(16 + LB * b, LB) for b in range(NB)]
LEVELS = [7, 7, 7, 7, 4]

VEC = {}
_at = 0
for _n, _w in (("ffn1_norm", 8), ("mix_norm", 8), ("ffn2_norm", 8), ("final_norm", 8), ("qkv_conv_w", NQ * SC),
               ("conv_w", NC_ * CW), ("conv_b", NC_), ("conv_norm", NC_), ("o_norm", 1), ("dt_bias", H),
               ("a_log", H), ("w_ba", KT * 2 * H)):
    VEC[_n] = slice(_at, _at + _w)
    _at += _w
NV = _at

MASK = {}
_at = 0
for _n, _w in (("ident", P), ("incl", P), ("strict", P), ("incl4", P), ("strict4", P), ("same4", P),
               ("levels", 7 * P), ("group", NG)):
    MASK[_n] = slice(_at, _at + _w)
    _at += _w
NM = _at


def shape_masks():
    m = np.zeros((P, NM), np.float32)
    s, c = np.arange(P)[:, None], np.arange(P)[None, :]
    seq = np.where(np.arange(P) < 16, 0, 1 + (np.arange(P) - 16) // LB)
    seq[80:] = 99
    same = (seq[:, None] == seq[None, :]) & (s < 80) & (c < 80)
    m[:, MASK["ident"]] = s == c
    m[:, MASK["incl"]] = s <= c
    m[:, MASK["strict"]] = s < c
    m[:, MASK["incl4"]] = (s <= c) & same
    m[:, MASK["strict4"]] = (s < c) & same
    m[:, MASK["same4"]] = same
    for l in range(7):
        w = 1 << l
        a = MASK["levels"].start + l * P
        m[:, a:a + P] = (s // (2 * w) == c // (2 * w)) & (s % (2 * w) < w) & (c % (2 * w) >= w)
    m[:, MASK["group"]] = seq[:, None] == np.arange(NG)[None, :]
    return m


def build(nc, weights, x_t, vecs, masks, hist_q, hist_c, states, y_t, new_state, last_q, last_c):
    ctx = ExitStack()
    with ctx:
        def sb(name, shape, dt=F32, where=ctx):
            return where.enter_context(nc.sbuf_tensor(name, shape, dt))

        def sem(name):
            return ctx.enter_context(nc.semaphore(name))

        h = sb("h", [P, KT, TOK])
        raw = sb("raw", [P, 2, KT, P])
        w_hi = sb("w_hi", [P, 4, KT, P], F32R)
        w_lo = sb("w_lo", [P, 4, KT, P], F32R)
        rstd = sb("rstd", [P, TOK])
        ssum = sb("ssum", [P, TOK])
        sq = sb("sq", [P, 2, TOK])
        work = sb("work", [P, 8, QE])
        vec = sb("vec", [P, NV])
        mask = sb("mask", [P, NM])
        mean_d = sb("mean_d", [P, P])
        mean_c = sb("mean_c", [P, P])
        mean_v = sb("mean_v", [P, P])
        ones = sb("ones", [P, P])
        eps = sb("eps", [P, 1])
        c_ext = sb("c_ext", [P, NC_, CE])
        hq = sb("hq", [P, NQ, NB * (SC - 1)])
        lastq = sb("lastq", [P, NQ, (1 + NB) * (SC - 1)])
        wba_hi = sb("wba_hi", [P, KT, 2 * H], F32R)
        wba_lo = sb("wba_lo", [P, KT, 2 * H], F32R)
        gate = {n: sb("gate_" + n, [P, NT, H]) for n in ("beta", "g", "t1", "t2", "t3")}
        ba = sb("ba", [P, NT, 2 * H])
        rtok = sb("rtok", [P, 8])
        rjunk = sb("rjunk", [P, P])
        expa = sb("expa", [P, H])
        gcs = sb("gcs", [P, 2 * H + H * NG])
        fac = sb("fac", [P, 4, H * NG])
        gx = sb("gx", [P, H, NG])
        zone = ExitStack()
        x_hi = sb("x_hi", [P, KT, TOK], F32R, zone)
        x_lo = sb("x_lo", [P, KT, TOK], F32R, zone)
        zone.close()
        zone = ExitStack()
        G_B, B_B, E_, EG, EM, ES, AT, ATT, BM0, BM1, X_, Y_, T1, NWT, VB, KBG, KG, VN = [
            sb("d_" + n, [P, H, P], F32, zone) for n in
            ("g_b", "beta_b", "decay", "egrow", "decay_incl", "decay_strict", "a_t", "att_t", "b0", "b1", "inv",
             "inv_t", "t1", "neg_w_t", "vb", "kbg", "kg", "v_new")]
        hold1 = sb("hold1", [P, 2 * KT * TOK - 18 * H * P], F32, zone)
        ctx.enter_context(zone)
        zone2 = ExitStack()
        g_hi = sb("g_hi", [P, 8, TOK], F32R, zone2)
        g_lo = sb("g_lo", [P, 8, TOK], F32R, zone2)
        zone2.close()
        qkv = sb("qkv", [P, NQ, TOK], F32, zone2)
        S = sb("S", [P, H, NG, P], F32, zone2)
        z = sb("z", [P, H, TOK], F32, zone2)
        ctx.enter_context(zone2)

        ps = ctx.enter_context(nc.psum_tensor("ps", [P, 4, 2, 512], F32))

        def bank(j):
            return ps[:, j // 2, j % 2, :]

        def heads(j, n):
            return bank(j).rearrange("p (h c) -> p h c", h=H)[:, :, 0:n]

        def v(name, i=0, n=1):
            return vec[:, VEC[name].start + i:VEC[name].start + i + n]

        def m(name, n=P, i=0):
            a = MASK[name].start + i * P
            return mask[0:n, a:a + n]

        def over_heads(ap, n):
            return ap.unsqueeze(1).to_broadcast([n, H, ap.shape[1]])

        def over_cols(ap, c):
            return ap.unsqueeze(2).to_broadcast([ap.shape[0], ap.shape[1], c])

        raw_in = [sem(f"raw_in{i}") for i in range(2)]
        w_hi_ready = sem("w_hi_ready")
        w_lo_ready = sem("w_lo_ready")
        unit_done = sem("unit_done")
        psum_free = sem("psum_free")
        x_in = sem("x_in"); vec_in = sem("vec_in"); hist_in = sem("hist_in"); state_in = sem("state_in")
        ones_set = sem("ones_set")
        sq_ready = sem("sq_ready"); ssum_step = sem("ssum_step"); stats_done = sem("stats_done")
        rstd_ready = sem("rstd_ready")
        x_hi_ready = sem("x_hi_ready"); x_ready = sem("x_ready")
        silu_done = sem("silu_done"); sr_ready = sem("sr_ready")
        g_hi_ready = sem("g_hi_ready"); g_ready = sem("g_ready")
        wba_hi_ready = sem("wba_hi_ready"); wba_ready = sem("wba_ready")
        pads_set = sem("pads_set")
        link_s = sem("dve_link")
        pool_s = sem("pool_link")
        ab_ready = sem("ab_ready"); gate_act = sem("gate_act"); gates_ready = sem("gates_ready")
        gate_in = sem("gate_in"); sig_ready = sem("sig_ready"); c_in_ready = sem("c_in_ready")
        tap_ready = sem("tap_ready"); tap_added = sem("tap_added"); conv3_step = sem("conv3_step")
        lastq_saved = sem("lastq_saved"); q_conv = sem("q_conv"); q_ready = sem("q_ready")
        names = ("qk_sq norms_ps qk_log qk_factor o_log o_factor qk_normed gates_b gates_ps gcs_ready d_diff e_ready eg_ready bs_ready em_ready "
                 "es_ready qg_ready facs diffs tok_ps tok_ready gram_ps at_ready att_ready b_ready y_ready x1_ps "
                 "x_inv t1_ps t1_ready p_ps wt_ps nwt_ready vn_ps vn_ready o_ps o_evac s_ps s_ready osq_ready on_ps "
                 "o_ready vnt_ps vnt_ready os_ps os_ready vn4_ps att4_ps gx_ready vx_ready s4_ps s_scaled").split()
        s = {n: sem(n) for n in names}
        z_ready = sem("z_ready"); mix_ready = sem("mix_ready")
        csq_ready = sem("csq_ready"); cn_ps = sem("cn_ps"); c_factor = sem("c_factor"); root_done = sem("root_done"); c_scaled = sem("c_scaled"); c_act = sem("c_act")
        y_ready = sem("y_out_ready"); y_gain = sem("y_gain")
        out_s = sem("out_s"); state_out = sem("state_out")

        block = ctx.enter_context(nc.Block())

        def parts(base, g0):
            u, g = base, g0
            for n in PARTS:
                yield u, n, g
                u += 2 * n + 8
                g += n

        @block.sync
        def _(sp):
            sp.dma_start(vec[:], vecs).then_inc(vec_in, 16)
            sp.dma_start(h[:, 0:4], x_t[:, 0:4]).then_inc(x_in, 16)
            sp.dma_start(raw[:, 0], weights[0]).then_inc(raw_in[0], 16)
            sp.wait_ge(x_in, 16)
            sp.dma_start(h[:, 4:8], x_t[:, 4:8]).then_inc(x_in, 16)
            sp.dma_start(raw[:, 1], weights[1]).then_inc(raw_in[1], 16)
            sp.dma_start(mask[:], masks).then_inc(hist_in, 16)
            sp.dma_start(hq[:], hist_q).then_inc(hist_in, 16)
            for c in range(NC_):
                sp.dma_start(c_ext[:, c, CP:CE].rearrange("p (b w) -> p b w", b=NB)[:, :, 0:CW - 1],
                             hist_c[:, c]).then_inc(hist_in, 16)

            def load_pair(u):
                for j in range(2):
                    sp.wait_ge(w_lo_ready, u + j - 1)
                    sp.dma_start(raw[:, j], weights[u + j]).then_inc(raw_in[j], 16)

            with sp.Fori(0, (U_QKV + 4 - 2) // 2) as i:
                load_pair(2 * i + 2)
            sp.wait_ge(unit_done, U_GLU)
            sp.dma_start(S[:, :, 1:NG, :], states).then_inc(state_in, 16)
            with sp.Fori(0, (U_END - U_QKV - 4) // 2) as i:
                load_pair(2 * i + U_QKV + 4)
            sp.wait_ge(lastq_saved, NQ)
            sp.dma_start(last_q, lastq[:]).then_inc(out_s, 16)
            sp.wait_ge(c_in_ready, NC_)
            for c in range(NC_):
                sp.dma_start(last_c[:, c, 0:30], c_ext[:, c, L:L + 30]).then_inc(out_s, 16)
                sp.dma_start(last_c[:, c, 30:270].rearrange("p (b w) -> p b w", b=NB),
                             c_ext[:, c, CP:CE].rearrange("p (b w) -> p b w", b=NB)[:, :, LB:CS]).then_inc(out_s, 16)
            for k in range(KT):
                sp.wait_ge(y_ready, k + 1)
                sp.dma_start(y_t[:, k], h[:, k]).then_inc(out_s, 16)
            sp.wait_ge(out_s, 16 * (1 + 2 * NC_ + KT))

        @block.tensor
        def _(pe):
            def product(u, slot, kt, xh, xl, k_sem=None, k_base=0):
                pe.wait_ge(w_lo_ready, u + 1)
                for k in range(kt):
                    if k_sem is not None:
                        pe.wait_ge(k_sem, k_base + k + 1)
                    for n, (w, x) in enumerate(((w_hi, xh), (w_hi, xl), (w_lo, xh))):
                        for half in range(2):
                            last = nc.tensor.matmul(ps[:, slot, half, 0:HALF], w[:, slot, k, :],
                                                    x[:, k, half * HALF:(half + 1) * HALF],
                                                    start=(k == 0 and n == 0), stop=(k == kt - 1 and n == 2))
                last.then_inc(unit_done, 1)

            def mean_square(stage, u):
                pe.wait_ge(ssum_step, 8 * (stage + 1))
                if u:
                    pe.wait_ge(psum_free, u)
                for half in range(2):
                    last = nc.tensor.matmul(ps[:, 3, half, 0:HALF], mean_d[:], ssum[:, half * HALF:(half + 1) * HALF],
                                            start=True, stop=True)
                return last

            def ffn(stage, base, g0, k_base):
                for p, (u0, n, g) in enumerate(parts(base, g0)):
                    if p == 0:
                        for j in range(4):
                            u = u0 + j
                            if j == 3:
                                pe.wait_ge(rstd_ready, stage + 1)
                            elif u >= 4:
                                pe.wait_ge(psum_free, u - 3)
                            product(u, j, KT, x_hi, x_lo, x_ready if j == 0 else None, k_base)
                            if j == 0:
                                mean_square(stage, u0).then_inc(stats_done, 1)
                    with pe.Fori(1 if p == 0 else 0, n // 2) as i:
                        for j in range(4):
                            pe.wait_ge(psum_free, 4 * i + (u0 + j - 3))
                            product(4 * i + (u0 + j), j, KT, x_hi, x_lo)
                    d0 = u0 + 2 * n
                    with pe.Fori(0, 2) as i:
                        for j in range(4):
                            pe.wait_ge(psum_free, 4 * i + (d0 + j - 3))
                            product(4 * i + (d0 + j), j, n, g_hi, g_lo, g_ready if j == 0 else None, g)

            pe.wait_ge(ones_set, 1)
            ffn(0, U_FFN1, 0, 0)

            for j in range(4):
                u = U_GLU + j
                if j == 3:
                    pe.wait_ge(ab_ready, 1)
                else:
                    pe.wait_ge(psum_free, u - 3)
                product(u, j, KT, x_hi, x_lo, x_ready if j == 0 else None, 8)
                if j == 0:
                    mean_square(1, U_GLU)
                    pe.wait_ge(wba_ready, 1)
                    for t, (c0, n) in enumerate(TILES):
                        for k in range(KT):
                            for r, (a, b) in enumerate(((x_hi, wba_hi), (x_lo, wba_hi), (x_hi, wba_lo))):
                                last = nc.tensor.matmul(ps[0:n, 3, 0, 304 + 8 * t:312 + 8 * t], a[:, k, c0:c0 + n],
                                                        b[:, k, :], start=(k == 0 and r == 0), stop=(k == 7 and r == 2))
                    last.then_inc(stats_done, 1)
            with pe.Fori(1, (U_Z - U_GLU) // 4) as i:
                for j in range(4):
                    pe.wait_ge(psum_free, 4 * i + (U_GLU + j - 3))
                    product(4 * i + (U_GLU + j), j, KT, x_hi, x_lo)
            for j in range(4):
                pe.wait_ge(psum_free, U_Z + j - 3)
                product(U_Z + j, j, KT, x_hi, x_lo)

            def mm(out, lhsT, rhs, start=True, stop=True):
                return nc.tensor.matmul(out, lhsT, rhs, start=start, stop=stop, skip_group_check=True)

            pe.wait_ge(psum_free, U_OUT)
            lv = 0
            for t, (c0, n) in enumerate(TILES):
                cols = slice(c0, c0 + n)
                ident = m("ident")
                incl = m("incl4" if t == 4 else "incl", n)
                pe.wait_ge(s["qk_sq"], t + 1)
                if t:
                    pe.wait_ge(s["s_ready"], t)
                    pe.wait_ge(s["o_ready"], t)
                mm(heads(0, n), ones[:], sq[:, 0, 0:H * n].rearrange("p (h c) -> p h c", h=H))
                mm(heads(1, n), ones[:], sq[:, 1, 0:H * n].rearrange("p (h c) -> p h c", h=H)).then_inc(s["norms_ps"], 1)
                pe.wait_ge(s["gates_b"], t + 1)
                mm(bank(6)[0:n, 0:H], incl, gate["g"][0:n, t, :])
                mm(bank(6)[:, H:2 * H] if t < 4 else bank(6)[0:n, H:2 * H], ones[:] if t < 4 else m("same4", n),
                   gate["g"][0:n, t, :])
                if t == 4:
                    mm(bank(6)[:, 2 * H:2 * H + H * NG], ones[0:n, :], gx[0:n].rearrange("p h g -> p (h g)"))
                for hd in range(H):
                    mm(heads(4, n)[:, hd, :], G_B[0:n, hd, :], incl)
                for hd in range(H):
                    last = mm(heads(5, n)[:, hd, :], B_B[0:n, hd, :], m("ident", n))
                last.then_inc(s["gates_ps"], 1)
                pe.wait_ge(s["qk_normed"], t + 1)
                for hd in range(H):
                    nc.tensor.transpose(bank(2)[0:n, hd * P:(hd + 1) * P], qkv[:, H + hd, cols], ident)
                for hd in range(H):
                    last = nc.tensor.transpose(bank(3)[0:n, hd * P:(hd + 1) * P], qkv[:, 2 * H + hd, cols], ident)
                last.then_inc(s["tok_ps"], 1)
                for hd in range(H):
                    mm(heads(0, n)[0:n, hd, :], qkv[:, H + hd, cols], qkv[:, H + hd, cols])
                for hd in range(H):
                    last = mm(heads(1, n)[0:n, hd, :], qkv[:, H + hd, cols], qkv[:, hd, cols])
                last.then_inc(s["gram_ps"], 1)
                pe.wait_ge(s["y_ready"], lv + 1)
                pe.wait_ge(s["bs_ready"], t + 1)
                for hd in range(H):
                    last = nc.tensor.transpose(bank(5)[0:n, hd * P:hd * P + n], Y_[0:n, hd, 0:n], m("ident", n))
                last.then_inc(s["x1_ps"], 1)
                pe.wait_ge(s["tok_ready"], t + 1)
                pe.wait_ge(s["eg_ready"], t + 1)
                for l in range(1, LEVELS[t]):
                    BM = (BM0, BM1)[l % 2]
                    pe.wait_ge(s["b_ready"], lv - t + l)
                    pe.wait_ge(s["x_inv"], lv - t + l)
                    pe.wait_ge(s["y_ready"], lv + l)
                    for hd in range(H):
                        last = mm(heads(2, n)[0:n, hd, :], BM[0:n, hd, 0:n], X_[0:n, hd, 0:n])
                    last.then_inc(s["t1_ps"], 1)
                    pe.wait_ge(s["t1_ready"], lv - t + l)
                    for hd in range(H if l < LEVELS[t] - 1 else 0):
                        mm(heads(3, n)[0:n, hd, :], Y_[0:n, hd, 0:n], T1[0:n, hd, 0:n])
                    for hd in range(H):
                        last = mm(heads(4, n)[0:n, hd, :], T1[0:n, hd, 0:n], Y_[0:n, hd, 0:n])
                    last.then_inc(s["p_ps"], 1)
                lv += LEVELS[t]
                pe.wait_ge(s["y_ready"], lv)
                pe.wait_ge(s["gcs_ready"], t + 1)
                for hd in range(H):
                    last = mm(heads(6, n)[:, hd, :], KBG[0:n, hd, :], Y_[0:n, hd, 0:n])
                last.then_inc(s["wt_ps"], 1)
                pe.wait_ge(s["att_ready"], t + 1)
                if t < 4:
                    if t:
                        pe.wait_ge(s["nwt_ready"], t + 1)
                    for hd in range(H):
                        last = mm(bank(7)[0:n, hd * P:(hd + 1) * P], Y_[0:n, hd, 0:n], VB[0:n, hd, :], stop=(t == 0))
                        if t:
                            last = mm(bank(7)[0:n, hd * P:(hd + 1) * P], NWT[:, hd, 0:n], S[:, hd, 0, :], start=False)
                    last.then_inc(s["vn_ps"], 1)
                    pe.wait_ge(s["vn_ready"], t + 1)
                    pe.wait_ge(s["qg_ready"], t + 1)
                    for hd in range(H):
                        if t:
                            mm(heads(0, n)[:, hd, :], S[:, hd, 0, :], EG[:, hd, 0:n], stop=False)
                        last = mm(heads(0, n)[:, hd, :], VN[0:n, hd, :], ATT[0:n, hd, 0:n], start=(t == 0))
                    last.then_inc(s["o_ps"], 1)
                    for hd in range(H):
                        last = mm(bank(1)[:, hd * P:(hd + 1) * P], KG[0:n, hd, :], VN[0:n, hd, :])
                    last.then_inc(s["s_ps"], 1)
                else:
                    pe.wait_ge(s["nwt_ready"], t + 1)
                    pe.wait_ge(state_in, 16)
                    for hd in range(H):
                        mm(heads(7, n)[:, hd, :], VB[0:n, hd, :], Y_[0:n, hd, 0:n], stop=False)
                        for gi, (a, w) in enumerate(GROUPS):
                            last = mm(heads(7, n)[:, hd, a:a + w], S[:, hd, gi, :], NWT[:, hd, a:a + w], start=False,
                                      stop=(gi == NG - 1))
                    last.then_inc(s["vnt_ps"], 1)
                    pe.wait_ge(s["qg_ready"], t + 1)
                    for hd in range(H):
                        for gi, (a, w) in enumerate(GROUPS):
                            last = mm(heads(0, n)[:, hd, a:a + w], S[:, hd, gi, :], EG[:, hd, a:a + w])
                    last.then_inc(s["os_ps"], 1)
                    pe.wait_ge(s["vnt_ready"], 1)
                    for hd in range(H):
                        last = nc.tensor.transpose(bank(2)[0:n, hd * P:(hd + 1) * P],
                                                   work[:, 3, hd * n:(hd + 1) * n], ident)
                    last.then_inc(s["vn4_ps"], 1)
                    pe.wait_ge(s["vn_ready"], t + 1)
                    for hd in range(H):
                        last = mm(heads(3, n)[:, hd, :], VN[0:n, hd, :], ATT[0:n, hd, 0:n])
                    last.then_inc(s["att4_ps"], 1)
                    for hd in range(H):
                        pe.wait_ge(s["vx_ready"], hd + 1)
                        if hd:
                            pe.wait_ge(s["s_ready"], 4 + hd)
                        VX = work[0:n, 0:2, :].rearrange("p a b -> p (a b)")
                        for j, (a, w) in enumerate(((0, 512), (512, 512), (1024, 128))):
                            last = mm(bank(4 + j)[:, 0:w], KG[0:n, hd, :], VX[:, a:a + w])
                        last.then_inc(s["s4_ps"], 1)
                pe.wait_ge(s["osq_ready"], t + 1)
                mm(heads(2, n), mean_v[:], sq[:, 0, 0:H * n].rearrange("p (h c) -> p h c", h=H)).then_inc(s["on_ps"], 1)

            pe.wait_ge(s["o_ready"], NT)
            for c in range(NC_):
                pe.wait_ge(csq_ready, c + 1)
                for half in range(2):
                    last = nc.tensor.matmul(ps[:, 0, half, 0:HALF], mean_c[:],
                                            sq[:, c % 2, half * HALF:(half + 1) * HALF], start=(c == 0),
                                            stop=(c == NC_ - 1))
                last.then_inc(cn_ps, 1)

            pe.wait_ge(s["s_ready"], 4 + H)
            for j in range(4):
                if j == 0:
                    pe.wait_ge(c_factor, 1)
                product(U_OUT + j, j, KT, x_hi, x_lo, x_ready if j == 0 else None, 16)
            for j in range(4):
                pe.wait_ge(psum_free, U_OUT + 1 + j)
                product(U_OUT + 4 + j, j, KT, x_hi, x_lo)

            ffn(2, U_FFN2, FT, 24)
            pe.wait_ge(ssum_step, 32)
            pe.wait_ge(psum_free, U_END - 3)
            for half in range(2):
                last = nc.tensor.matmul(ps[:, 0, half, 0:HALF], mean_d[:], ssum[:, half * HALF:(half + 1) * HALF],
                                        start=True, stop=True)
            last.then_inc(stats_done, 1)

        def tap_place(t):
            return (ssum, sq[:, 0, :], sq[:, 1, :])[t % 3]

        def both(slot):
            return ps[:, slot, :, 0:HALF]

        def two(ap):
            return ap.rearrange("p (a b) -> p a b", a=2)

        @block.scalar
        def _(act):
            def split_hi(u, slot, first=False):
                if not isinstance(u, int):
                    act.wait_ge(raw_in[slot % 2], u * 8 + (16 - 8 * (slot % 2)))
                else:
                    act.wait_ge(raw_in[slot % 2], 16 * (u // 2 + 1))
                if not first:
                    act.wait_ge(unit_done, u - 3)
                nc.scalar.copy(w_hi[:, slot], raw[:, slot % 2]).then_inc(w_hi_ready, 1)

            def prepare(stage, norm, ready, split=True):
                for k in range(KT):
                    ready(k)
                    if 8 * stage + k >= 2:
                        act.wait_ge(ssum_step, 8 * stage + k - 1)
                    nc.scalar.activation(sq[:, k % 2, :], h[:, k, :], ACT.Square).then_inc(sq_ready, 1)
                    if split:
                        nc.scalar.activation(x_hi[:, k, :], h[:, k, :], ACT.Copy, scale=v(norm, k)).then_inc(x_hi_ready, 1)

            def root(stage, slot=3):
                act.wait_ge(stats_done, stage + 1)
                nc.scalar.activation(two(rstd[:]), both(slot), ACT.Sqrt, bias=eps[:]).then_inc(root_done, 1)

            def hidden(ua, f, gslot, j):
                act.wait_ge(psum_free, ua + 1)
                nc.scalar.activation(work[:, 2 + j, 0:TOK], work[:, j, 0:TOK], ACT.Silu).then_inc(silu_done, 1)
                split_hi(ua + 4, (2 * j) % 4)
                act.wait_ge(psum_free, ua + 2)
                nc.scalar.copy(g_hi[:, gslot, :], work[:, 6 + j, 0:TOK]).then_inc(g_hi_ready, 1)
                split_hi(ua + 5, (2 * j + 1) % 4)

            def ffn(base, g0, finish):
                for p, (u0, n, g) in enumerate(parts(base, g0)):
                    with act.Fori(0, n // 2) as i:
                        for j in range(2):
                            hidden(4 * i + (u0 + 2 * j), 2 * i + (g + j), 2 * i + j, j)
                    d0 = u0 + 2 * n
                    if p < len(PARTS) - 1:
                        with act.Fori(0, 2) as i:
                            for j in range(4):
                                split_hi(4 * i + (d0 + j + 4), j)
                    else:
                        finish(d0)

            act.wait_ge(vec_in, 16)
            act.wait_ge(ones_set, 1)
            nc.scalar.copy(wba_hi[:], v("w_ba", 0, KT * 2 * H).rearrange("p (k c) -> p k c", k=KT)).then_inc(wba_hi_ready, 1)
            nc.scalar.activation(expa[:], v("a_log", 0, H), ACT.Exp)

            def x_tile(k):
                act.wait_ge(x_in, 16 * (1 + k // 4))

            split_hi(0, 0, True)
            prepare(0, "ffn1_norm", x_tile)
            split_hi(1, 1, True)
            split_hi(2, 2, True)
            split_hi(3, 3, True)
            root(0)

            def finish_with(stage, norm, lookahead):
                def finish(d0):
                    def ready(k):
                        if d0 + k + 4 < U_END:
                            split_hi(d0 + k + 4, k % 4)
                        act.wait_ge(psum_free, d0 + k + 1)
                    prepare(stage, norm, ready, norm is not None)
                return finish

            ffn(U_FFN1, 0, finish_with(1, "mix_norm", True))

            root(1)
            act.wait_ge(ab_ready, 1)
            nc.scalar.activation(gate["beta"][:], ba[:, :, 0:H], ACT.Sigmoid).then_inc(gate_act, 1)
            nc.scalar.activation(gate["t2"][:], gate["t1"][:], ACT.Exp, scale=-1.0).then_inc(gate_act, 1)
            act.wait_ge(gate_act, 2)
            nc.scalar.activation(gate["t3"][:], gate["t2"][:], ACT.Ln, bias=1.0).then_inc(gate_act, 1)

            taps = [0]

            def conv_taps(n):
                for t in range(taps[0], min(taps[0] + n, POOL_TAPS)):
                    c, j = t // (CW - 1), 1 + t % (CW - 1)
                    act.wait_ge(c_in_ready, c + 1)
                    if t >= 3:
                        act.wait_ge(tap_added, t - 2)
                    o = tap_place(t)
                    nc.scalar.activation(o[:, 0:L], c_ext[:, c, j:j + L], ACT.Copy, scale=v("conv_w", CW * c + j))
                    nc.scalar.activation(o[:, L:TOK].rearrange("p (b w) -> p b w", b=NB),
                                         c_ext[:, c, CP:CE].rearrange("p (b w) -> p b w", b=NB)[:, :, j:j + LB],
                                         ACT.Copy, scale=v("conv_w", CW * c + j)).then_inc(tap_ready, 1)
                taps[0] += n

            act.wait_ge(pads_set, 1)
            act.wait_ge(hist_in, 16 * (2 + NC_))
            for c in range(NC_):
                u = U_GLU + 2 * c
                split_hi(u + 4, (u + 4) % 4)
                if c:
                    conv_taps(8)
                act.wait_ge(psum_free, u + 2)
                nc.scalar.activation(work[:, 1 + 2 * (c % 2), 0:TOK], work[:, 1 + 2 * (c % 2), 0:TOK],
                                     ACT.Sigmoid).then_inc(sig_ready, 1)
                split_hi(u + 5, (u + 5) % 4)
            for i in range(NQ):
                u = U_QKV + i
                split_hi(u + 4, (u + 4) % 4)
                conv_taps(4)
                act.wait_ge(psum_free, u + 1)
                e = work[:, i % 2, :]
                nc.scalar.copy(lastq[:, i, 0:3], e[:, L:L + 3])
                nc.scalar.copy(lastq[:, i, 3:27].rearrange("p (b w) -> p b w", b=NB),
                               e[:, QP:QE].rearrange("p (b w) -> p b w", b=NB)[:, :, LB:QS]).then_inc(lastq_saved, 1)
                act.wait_ge(q_conv, i + 1)
                a = work[:, 2 + i % 2, :]
                nc.scalar.activation(qkv[:, i, 0:L], a[:, 0:L], ACT.Silu)
                nc.scalar.activation(qkv[:, i, L:TOK].rearrange("p (b w) -> p b w", b=NB),
                                     a[:, QP:QE].rearrange("p (b w) -> p b w", b=NB)[:, :, 0:LB],
                                     ACT.Silu).then_inc(q_ready, 1)
            for i in range(H):
                u = U_Z + i
                split_hi(u + 4, (u + 4) % 4)
                conv_taps(5)
                act.wait_ge(psum_free, u + 1)
                nc.scalar.activation(z[:, i, :], z[:, i, :], ACT.Silu).then_inc(z_ready, 1)

            lv = 0
            for t, (c0, n) in enumerate(TILES):
                cols = slice(c0, c0 + n)
                if t == 0:
                    act.wait_ge(q_ready, NQ)
                    act.wait_ge(tap_added, POOL_TAPS)
                    act.wait_ge(stats_done, 2)
                else:
                    act.wait_ge(s["o_ready"], t)
                for i in range(2):
                    last = nc.scalar.activation(sq[:, i, 0:H * n].rearrange("p (h c) -> p h c", h=H),
                                                qkv[:, H * i:H * (i + 1), cols], ACT.Square)
                last.then_inc(s["qk_sq"], 1)
                act.wait_ge(s["norms_ps"], t + 1)
                for i in range(2):
                    last = nc.scalar.activation(work[:, i, 0:H * n].rearrange("p (h c) -> p h c", h=H), heads(i, n),
                                                ACT.Ln, bias=eps[:])
                last.then_inc(s["qk_log"], 1)
                act.wait_ge(s["qk_log"], t + 1)
                nc.scalar.activation(work[:, 0:2, 0:H * n], work[:, 0:2, 0:H * n], ACT.Exp,
                                     scale=-0.5).then_inc(s["qk_factor"], 1)
                act.wait_ge(s["diffs"], t + 1)
                nc.scalar.activation(fac[0:n, 0, 0:H], gcs[0:n, 0:H], ACT.Exp)
                nc.scalar.activation(fac[0:n, 1, 0:H], fac[0:n, 3, 0:H], ACT.Exp)
                if t < 4:
                    nc.scalar.activation(fac[:, 2, 0:H], gcs[:, H:2 * H], ACT.Exp).then_inc(s["facs"], 1)
                else:
                    nc.scalar.activation(fac[:, 2, :], gcs[:, 2 * H:2 * H + H * NG], ACT.Exp).then_inc(s["facs"], 1)
                act.wait_ge(s["d_diff"], t + 1)
                nc.scalar.activation(E_[0:n, :, 0:n], E_[0:n, :, 0:n], ACT.Exp).then_inc(s["e_ready"], 1)
                nc.scalar.activation(EG[:, :, 0:n], heads(4, n), ACT.Exp).then_inc(s["eg_ready"], 1)
                act.wait_ge(s["x1_ps"], t + 1)
                nc.scalar.copy(X_[0:n, :, 0:n], heads(5, n)[0:n]).then_inc(s["x_inv"], 1)
                for l in range(1, LEVELS[t]):
                    act.wait_ge(s["t1_ps"], lv - t + l)
                    nc.scalar.copy(T1[0:n, :, 0:n], heads(2, n)[0:n]).then_inc(s["t1_ready"], 1)
                lv += LEVELS[t]
                act.wait_ge(s["wt_ps"], t + 1)
                nc.scalar.activation(NWT[:, :, 0:n], heads(6, n), ACT.Copy, scale=-1.0).then_inc(s["nwt_ready"], 1)
                if t < 4:
                    act.wait_ge(s["o_ps"], t + 1)
                    nc.scalar.copy(qkv[:, 0:H, cols], heads(0, n)).then_inc(s["o_evac"], 1)
                    act.wait_ge(s["o_evac"], t + 1)
                else:
                    act.wait_ge(s["vnt_ps"], 1)
                    nc.scalar.copy(work[:, 3, 0:H * n].rearrange("p (h c) -> p h c", h=H),
                                   heads(7, n)).then_inc(s["vnt_ready"], 1)
                    act.wait_ge(s["os_ps"], 1)
                    nc.scalar.copy(work[:, 2, 0:H * n].rearrange("p (h c) -> p h c", h=H),
                                   heads(0, n)).then_inc(s["os_ready"], 1)
                    act.wait_ge(s["o_evac"], NT)
                nc.scalar.activation(sq[:, 0, 0:H * n].rearrange("p (h c) -> p h c", h=H), qkv[:, 0:H, cols],
                                     ACT.Square).then_inc(s["osq_ready"], 1)
                act.wait_ge(s["on_ps"], t + 1)
                r = work[:, 0, 0:H * n].rearrange("p (h c) -> p h c", h=H)
                nc.scalar.activation(r, heads(2, n), ACT.Ln, bias=eps[:]).then_inc(s["o_log"], 1)
                act.wait_ge(s["o_log"], t + 1)
                nc.scalar.activation(r, r, ACT.Exp, scale=-0.5).then_inc(s["o_factor"], 1)

            act.wait_ge(s["s_ready"], 4 + H)
            act.dma_start(new_state, S[:]).then_inc(state_out, 16)
            for c in range(NC_):
                if c < 3:
                    act.wait_ge(tap_added, (CW - 1) * (c + 1))
                else:
                    act.wait_ge(conv3_step, CW)
                if c == 0:
                    act.wait_ge(s["o_ready"], NT)
                if c >= 2:
                    act.wait_ge(cn_ps, c - 1)
                nc.scalar.activation(sq[:, c % 2, :], work[:, 4 + c, 0:TOK], ACT.Square).then_inc(csq_ready, 1)
            act.wait_ge(cn_ps, NC_)
            nc.scalar.activation(two(ssum[:]), both(0), ACT.Ln, bias=eps[:]).then_inc(c_factor, 1)
            act.wait_ge(c_factor, 1)
            nc.scalar.activation(ssum[:], ssum[:], ACT.Exp, scale=-0.5).then_inc(c_factor, 1)
            for i in range(H):
                act.wait_ge(mix_ready, i + 1)
                nc.scalar.copy(x_hi[:, i, :], qkv[:, i, :]).then_inc(x_hi_ready, 1)
            for c in range(NC_):
                act.wait_ge(c_scaled, c + 1)
                nc.scalar.activation(work[:, 4 + c, 0:TOK], work[:, 4 + c, 0:TOK], ACT.Silu,
                                     scale=v("conv_norm", c)).then_inc(c_act, 1)
                act.wait_ge(c_act, c + 1)
                nc.scalar.copy(x_hi[:, H + c, :], work[:, 4 + c, 0:TOK]).then_inc(x_hi_ready, 1)

            for k in range(8):
                split_hi(U_OUT + 4 + k, k % 4)

            def out_tile(k):
                act.wait_ge(psum_free, U_OUT + k + 1)
                act.wait_ge(unit_done, U_FFN2)
            prepare(2, "ffn2_norm", out_tile)
            root(2)
            act.wait_ge(state_out, 16)
            ffn(U_FFN2, FT, finish_with(3, None, False))
            root(3, 0)
            for k in range(KT):
                nc.scalar.activation(h[:, k, :], h[:, k, :], ACT.Copy, scale=v("final_norm", k)).then_inc(y_gain, 1)

        @block.vector
        def _(dve):
            V = nc.vector
            count = [0]

            def link(ins):
                count[0] += 1
                ins.then_inc(link_s, 1)
                dve.wait_ge(link_s, count[0])

            def split_lo(u, slot):
                dve.wait_ge(w_hi_ready, u + 1)
                V.tensor_tensor(w_lo[:, slot], raw[:, slot % 2], w_hi[:, slot].bitcast(F32),
                                ALU.subtract).then_inc(w_lo_ready, 1)

            def rest_of_x(k, norm, at):
                dve.wait_ge(x_hi_ready, at + k + 1)
                V.scalar_tensor_tensor(x_lo[:, k, :], h[:, k, :], v(norm, k), x_hi[:, k, :].bitcast(F32),
                                       ALU.mult, ALU.subtract).then_inc(x_ready, 1)

            def rms_factor(stage):
                dve.wait_ge(root_done, stage + 1)
                V.reciprocal(rstd[:], rstd[:]).then_inc(rstd_ready, 1)
                dve.wait_ge(rstd_ready, stage + 1)

            def scaled(out, u, slot):
                dve.wait_ge(unit_done, u + 1)
                return V.tensor_tensor(two(out), both(slot), two(rstd[:]), ALU.mult)

            def hidden(ua, f, gslot, j):
                scaled(work[:, j, 0:TOK], ua, 2 * j).then_inc(psum_free, 1)
                split_lo(ua + 4, 2 * j)
                dve.wait_ge(silu_done, f + 1)
                V.tensor_tensor(work[:, 4 + j, 0:TOK], work[:, 2 + j, 0:TOK], rstd[:], ALU.mult).then_inc(sr_ready, 1)
                dve.wait_ge(sr_ready, f + 1)
                dve.wait_ge(unit_done, ua + 2)
                V.tensor_tensor(two(work[:, 6 + j, 0:TOK]), both(2 * j + 1), two(work[:, 4 + j, 0:TOK]),
                                ALU.mult).then_inc(psum_free, 1)
                split_lo(ua + 5, 2 * j + 1)
                dve.wait_ge(g_hi_ready, f + 1)
                V.tensor_tensor(g_lo[:, gslot, :], work[:, 6 + j, 0:TOK], g_hi[:, gslot, :].bitcast(F32),
                                ALU.subtract).then_inc(g_ready, 1)

            def add_to_h(u, slot, k, factor):
                dve.wait_ge(unit_done, u + 1)
                dve.wait_ge(psum_free, u - 7)
                V.scalar_tensor_tensor(two(h[:, k, :]), both(slot), factor, two(h[:, k, :]), ALU.mult,
                                       ALU.add).then_inc(psum_free, 1)

            def ffn(base, g0, norm, at):
                for p, (u0, n, g) in enumerate(parts(base, g0)):
                    with dve.Fori(0, n // 2) as i:
                        for j in range(2):
                            hidden(4 * i + (u0 + 2 * j), 2 * i + (g + j), 2 * i + j, j)
                    d0 = u0 + 2 * n
                    if p < len(PARTS) - 1:
                        with dve.Fori(0, 2) as i:
                            for j in range(4):
                                add_to_h(4 * i + (d0 + j), j, 4 * i + j, 0.5)
                                split_lo(4 * i + (d0 + j + 4), j)
                    else:
                        for k in range(KT):
                            add_to_h(d0 + k, k % 4, k, 0.5)
                            if d0 + k + 4 < U_END:
                                split_lo(d0 + k + 4, k % 4)
                            if norm is not None:
                                rest_of_x(k, norm, at)

            V.memset(mean_d[:], 1.0 / D)
            V.memset(mean_c[:], 1.0 / (NC_ * P))
            V.memset(mean_v[:], 1.0 / P)
            V.memset(eps[:], EPS)
            V.memset(ones[:], 1.0).then_inc(ones_set, 1)
            V.memset(c_ext[:, :, 0:CW - 1], 0.0)
            V.memset(ba[:], 0.0)
            V.memset(rtok[:], 0.0).then_inc(pads_set, 1)
            dve.wait_ge(wba_hi_ready, 1)
            V.tensor_tensor(wba_lo[:], v("w_ba", 0, KT * 2 * H).rearrange("p (k c) -> p k c", k=KT),
                            wba_hi[:].bitcast(F32), ALU.subtract).then_inc(wba_ready, 1)
            split_lo(0, 0)
            for k in range(KT):
                rest_of_x(k, "ffn1_norm", 0)
            for u in range(1, 4):
                split_lo(u, u)
            rms_factor(0)
            ffn(U_FFN1, 0, "mix_norm", 8)

            rms_factor(1)
            dve.wait_ge(pads_set, 1)
            dve.wait_ge(hist_in, 16 * (2 + NC_))
            for t, (c0, n) in enumerate(TILES):
                link(V.tensor_tensor_reduce(rjunk[0:n, 0:n], rstd[0:n, c0:c0 + n], m("ident", n), 1.0, 0.0, ALU.mult, ALU.add,
                                            rtok[0:n, t:t + 1]))
                link(V.tensor_scalar(ba[0:n, t, :], ps[0:n, 3, 0, 304 + 8 * t:312 + 8 * t], rtok[0:n, t:t + 1], None,
                                     ALU.mult))
            link(V.tensor_tensor(gate["g"][:], ba[:, :, H:2 * H], v("dt_bias", 0, H).unsqueeze(1).to_broadcast([P, NT, H]),
                                 ALU.add))
            V.scalar_tensor_tensor(gate["t1"][:], gate["g"][:], -1.0, gate["g"][:], ALU.mult, ALU.max).then_inc(ab_ready, 1)

            for c in range(NC_):
                u = U_GLU + 2 * c
                a, b = work[:, 2 * (c % 2), :], work[:, 1 + 2 * (c % 2), :]
                scaled(a[:, 0:TOK], u, u % 4).then_inc(psum_free, 1)
                split_lo(u + 4, (u + 4) % 4)
                scaled(b[:, 0:TOK], u + 1, (u + 1) % 4).then_inc(psum_free, 1)
                split_lo(u + 5, (u + 5) % 4)
                dve.wait_ge(sig_ready, c + 1)
                dve.wait_ge(psum_free, u + 2)
                V.tensor_tensor(c_ext[:, c, CW - 1:CP], a[:, 0:L], b[:, 0:L], ALU.mult)
                V.tensor_tensor(c_ext[:, c, CP:CE].rearrange("p (b w) -> p b w", b=NB)[:, :, CW - 1:CS],
                                a[:, L:TOK].rearrange("p (b w) -> p b w", b=NB),
                                b[:, L:TOK].rearrange("p (b w) -> p b w", b=NB), ALU.mult).then_inc(c_in_ready, 1)
                if c == 0:
                    dve.wait_ge(gate_act, 3)
                    link(V.scalar_tensor_tensor(gate["t2"][:], gate["g"][:], 0.0, gate["t3"][:], ALU.max, ALU.add))
                    V.scalar_tensor_tensor(gate["g"][:], gate["t2"][:], -1.0,
                                           expa[:].unsqueeze(1).to_broadcast([P, NT, H]), ALU.mult,
                                           ALU.mult).then_inc(gates_ready, 1)

            dve.wait_ge(c_in_ready, NC_)
            for i in range(2):
                last = V.memset(work[:, i, 0:SC - 1], 0.0)
            link(last)
            for i in range(NQ):
                u = U_QKV + i
                e, a = work[:, i % 2, :], work[:, 2 + i % 2, :]
                if i >= 2:
                    dve.wait_ge(lastq_saved, i - 1)
                dve.wait_ge(unit_done, u + 1)
                V.tensor_copy(e[:, QP:QE].rearrange("p (b w) -> p b w", b=NB)[:, :, 0:SC - 1],
                              hq[:, i, :].rearrange("p (b w) -> p b w", b=NB))
                V.tensor_tensor(e[:, 3:3 + HALF], ps[:, u % 4, 0, 0:HALF], rstd[:, 0:HALF], ALU.mult)
                V.tensor_tensor(e[:, 3 + HALF:QP], ps[:, u % 4, 1, 0:L - HALF], rstd[:, HALF:L], ALU.mult)
                V.tensor_tensor(e[:, QP:QE].rearrange("p (b w) -> p b w", b=NB)[:, :, SC - 1:QS],
                                ps[:, u % 4, 1, L - HALF:HALF].rearrange("p (b w) -> p b w", b=NB),
                                rstd[:, L:TOK].rearrange("p (b w) -> p b w", b=NB), ALU.mult).then_inc(psum_free, 1)
                split_lo(u + 4, (u + 4) % 4)
                dve.wait_ge(psum_free, u + 1)
                if i >= 2:
                    dve.wait_ge(q_ready, i - 1)
                link(V.tensor_scalar(a[:, 0:QO], e[:, 0:QO], v("qkv_conv_w", SC * i), None, ALU.mult))
                for j in range(1, SC):
                    ins = V.scalar_tensor_tensor(a[:, 0:QO], e[:, j:j + QO], v("qkv_conv_w", SC * i + j), a[:, 0:QO],
                                                 ALU.mult, ALU.add)
                    if j < SC - 1:
                        link(ins)
                    else:
                        ins.then_inc(q_conv, 1)

            for i in range(H):
                u = U_Z + i
                scaled(z[:, i, :], u, u % 4).then_inc(psum_free, 1)
                split_lo(u + 4, (u + 4) % 4)

            taps = [0]

            def conv_taps(n):
                out, c = work[:, 7, :], 3
                parts = ((out[:, 0:L], lambda j: c_ext[:, c, j:j + L]),
                         (out[:, L:TOK].rearrange("p (b w) -> p b w", b=NB),
                          lambda j: c_ext[:, c, CP:CE].rearrange("p (b w) -> p b w", b=NB)[:, :, j:j + LB]))
                for j in range(taps[0], min(taps[0] + n, CW)):
                    if j:
                        dve.wait_ge(conv3_step, j)
                    for o, x in parts:
                        if j:
                            last = V.scalar_tensor_tensor(o, x(j), v("conv_w", CW * c + j), o, ALU.mult, ALU.add)
                        else:
                            last = V.tensor_scalar(o, x(j), v("conv_w", CW * c), v("conv_b", c), ALU.mult, ALU.add)
                    last.then_inc(conv3_step, 1)
                taps[0] += n

            lv = 0
            for t, (c0, n) in enumerate(TILES):
                cols = slice(c0, c0 + n)
                dve.wait_ge(s["qk_factor"], t + 1)
                r = [work[:, i, 0:H * n].rearrange("p (h c) -> p h c", h=H) for i in range(2)]
                V.scalar_tensor_tensor(qkv[:, 0:H, cols], qkv[:, 0:H, cols], float(P) ** -0.5, r[0], ALU.mult, ALU.mult)
                V.tensor_tensor(qkv[:, H:2 * H, cols], qkv[:, H:2 * H, cols], r[1], ALU.mult).then_inc(s["qk_normed"], 1)
                dve.wait_ge(s["gates_ps"], t + 1)
                if t == 4:
                    V.tensor_copy(gcs[:, 2 * H:], bank(6)[:, 2 * H:2 * H + H * NG])
                V.tensor_copy(gcs[0:n, 0:2 * H], bank(6)[0:n, 0:2 * H]).then_inc(s["gcs_ready"], 1)
                dve.wait_ge(s["gcs_ready"], t + 1)
                V.tensor_tensor(fac[0:n, 3, 0:H], gcs[0:n, H:2 * H], gcs[0:n, 0:H], ALU.subtract).then_inc(s["diffs"], 1)
                for hd in range(H):
                    last = V.tensor_scalar(E_[0:n, hd, 0:n], heads(4, n)[0:n, hd, :], gcs[0:n, hd:hd + 1], 0.0,
                                           ALU.subtract, ALU.min)
                last.then_inc(s["d_diff"], 1)
                V.tensor_tensor(ES[0:n, :, 0:n], heads(5, n)[0:n], over_heads(m("strict4" if t == 4 else "strict", n), n),
                                ALU.mult).then_inc(s["bs_ready"], 1)
                dve.wait_ge(s["tok_ps"], t + 1)
                dve.wait_ge(s["facs"], t + 1)
                link(V.tensor_tensor(fac[0:n, 3, 0:H], gate["beta"][0:n, t, :], fac[0:n, 0, 0:H], ALU.mult))
                V.tensor_tensor(VB[0:n], heads(3, P)[0:n], over_cols(gate["beta"][0:n, t, :], P), ALU.mult)
                V.tensor_tensor(KBG[0:n], heads(2, P)[0:n], over_cols(fac[0:n, 3, 0:H], P), ALU.mult)
                V.tensor_tensor(KG[0:n], heads(2, P)[0:n], over_cols(fac[0:n, 1, 0:H], P), ALU.mult).then_inc(s["tok_ready"], 1)
                dve.wait_ge(s["gram_ps"], t + 1)
                dve.wait_ge(s["es_ready"], t + 1)
                V.tensor_tensor(AT[0:n, :, 0:n], heads(0, n)[0:n], ES[0:n, :, 0:n], ALU.mult).then_inc(s["at_ready"], 1)
                V.tensor_tensor(ATT[0:n, :, 0:n], heads(1, n)[0:n], EM[0:n, :, 0:n], ALU.mult).then_inc(s["att_ready"], 1)
                dve.wait_ge(s["at_ready"], t + 1)
                link(V.tensor_tensor(VN[0:n, :, 0:n], AT[0:n, :, 0:n], over_heads(m("levels", n, 0), n), ALU.mult))
                V.tensor_tensor(Y_[0:n, :, 0:n], over_heads(m("ident", n), n), VN[0:n, :, 0:n],
                                ALU.subtract).then_inc(s["y_ready"], 1)
                for l in range(1, LEVELS[t]):
                    dve.wait_ge(s["p_ps"], lv - t + l)
                    dve.wait_ge(s["x_inv"], lv - t + l)
                    if l < LEVELS[t] - 1:
                        V.tensor_tensor(X_[0:n, :, 0:n], X_[0:n, :, 0:n], heads(3, n)[0:n],
                                        ALU.subtract).then_inc(s["x_inv"], 1)
                    dve.wait_ge(s["y_ready"], lv + l)
                    V.tensor_tensor(Y_[0:n, :, 0:n], Y_[0:n, :, 0:n], heads(4, n)[0:n], ALU.subtract).then_inc(s["y_ready"], 1)
                    conv_taps(1)
                lv += LEVELS[t]
                if t < 4:
                    dve.wait_ge(s["vn_ps"], t + 1)
                    V.tensor_copy(VN[:], heads(7, P)).then_inc(s["vn_ready"], 1)
                    dve.wait_ge(s["s_ps"], t + 1)
                    if t == 0:
                        V.tensor_copy(S[:, :, 0, :], heads(1, P)).then_inc(s["s_ready"], 1)
                    else:
                        dve.wait_ge(s["s_ready"], t)
                        for hd in range(H):
                            last = V.scalar_tensor_tensor(S[:, hd, 0, :], S[:, hd, 0, :], fac[:, 2, hd:hd + 1],
                                                          heads(1, P)[:, hd, :], ALU.mult, ALU.add)
                        last.then_inc(s["s_ready"], 1)
                else:
                    dve.wait_ge(s["vn4_ps"], 1)
                    V.tensor_copy(VN[0:n], heads(2, P)[0:n]).then_inc(s["vn_ready"], 1)
                    dve.wait_ge(s["os_ready"], 1)
                    dve.wait_ge(s["att4_ps"], 1)
                    V.tensor_tensor(qkv[:, 0:H, cols], heads(3, n), work[:, 2, 0:H * n].rearrange("p (h c) -> p h c", h=H),
                                    ALU.add).then_inc(s["o_evac"], 1)
                    VX = work[0:n, 0:2, :].rearrange("p a b -> p (a b)")[:, 0:NG * P].rearrange("p (g c) -> p g c", g=NG)
                    dve.wait_ge(s["vn_ready"], t + 1)
                    for hd in range(H):
                        if hd:
                            dve.wait_ge(s["s4_ps"], hd)
                        V.tensor_tensor(VX, VN[0:n, hd, :].unsqueeze(1).to_broadcast([n, NG, P]),
                                        mask[0:n, MASK["group"]].unsqueeze(2).to_broadcast([n, NG, P]),
                                        ALU.mult).then_inc(s["vx_ready"], 1)
                        dve.wait_ge(s["s_ready"], 4)
                        V.tensor_tensor(S[:, hd], S[:, hd], over_cols(fac[:, 2, NG * hd:NG * (hd + 1)], P),
                                        ALU.mult).then_inc(s["s_scaled"], 1)
                        dve.wait_ge(s["s_scaled"], hd + 1)
                        dve.wait_ge(s["s4_ps"], hd + 1)
                        V.tensor_tensor(S[:, hd, 0:8, :], S[:, hd, 0:8, :],
                                        ps[:, 2].rearrange("p a (g c) -> p (a g) c", g=4), ALU.add)
                        V.tensor_tensor(S[:, hd, 8, :], S[:, hd, 8, :], bank(6)[:, 0:P], ALU.add).then_inc(s["s_ready"], 1)
                dve.wait_ge(s["o_factor"], t + 1)
                V.tensor_tensor(qkv[:, 0:H, cols], qkv[:, 0:H, cols], r[0], ALU.mult).then_inc(s["o_ready"], 1)

            conv_taps(CW)
            dve.wait_ge(z_ready, H)
            dve.wait_ge(s["o_ready"], NT)
            for i in range(H):
                V.scalar_tensor_tensor(qkv[:, i, :], qkv[:, i, :], v("o_norm"), z[:, i, :], ALU.mult,
                                       ALU.mult).then_inc(mix_ready, 1)
            dve.wait_ge(c_factor, 2)
            for c in range(NC_):
                V.tensor_tensor(work[:, 4 + c, 0:TOK], work[:, 4 + c, 0:TOK], ssum[:], ALU.mult).then_inc(c_scaled, 1)
            for i in range(2 * H):
                dve.wait_ge(x_hi_ready, 16 + i + 1)
                src = qkv[:, i, :] if i < H else work[:, i, 0:TOK]
                V.tensor_tensor(x_lo[:, i, :], src, x_hi[:, i, :].bitcast(F32), ALU.subtract).then_inc(x_ready, 1)

            for k in range(KT):
                add_to_h(U_OUT + k, k % 4, k, 1.0)
                split_lo(U_OUT + k + 4, k % 4)
            for k in range(KT):
                rest_of_x(k, "ffn2_norm", 24)
            rms_factor(2)
            ffn(U_FFN2, FT, None, 0)
            rms_factor(3)
            for k in range(KT):
                dve.wait_ge(y_gain, k + 1)
                V.tensor_tensor(h[:, k, :], h[:, k, :], rstd[:], ALU.mult).then_inc(y_ready, 1)

        @block.gpsimd
        def _(pool):
            G = nc.gpsimd
            count = [0]

            def link(ins):
                count[0] += 1
                ins.then_inc(pool_s, 1)
                pool.wait_ge(pool_s, count[0])

            def sum_squares(stage):
                for k in range(KT):
                    pool.wait_ge(sq_ready, 8 * stage + k + 1)
                    if k == 0:
                        if stage:
                            pool.wait_ge(stats_done, stage)
                        G.tensor_copy(ssum[:], sq[:, 0, :]).then_inc(ssum_step, 1)
                    else:
                        pool.wait_ge(ssum_step, 8 * stage + k)
                        G.tensor_tensor(ssum[:], ssum[:], sq[:, k % 2, :], ALU.add).then_inc(ssum_step, 1)

            sum_squares(0)
            sum_squares(1)

            pool.wait_ge(vec_in, 16)
            pool.wait_ge(hist_in, 16 * (2 + NC_))
            pool.wait_ge(pads_set, 1)
            pool.wait_ge(stats_done, 2)
            for c in range(3):
                pool.wait_ge(c_in_ready, c + 1)
                out = work[:, 4 + c, :]
                G.tensor_scalar(out[:, 0:L], c_ext[:, c, 0:L], v("conv_w", CW * c), v("conv_b", c), ALU.mult, ALU.add)
                link(G.tensor_scalar(out[:, L:TOK].rearrange("p (b w) -> p b w", b=NB),
                                     c_ext[:, c, CP:CE].rearrange("p (b w) -> p b w", b=NB)[:, :, 0:LB],
                                     v("conv_w", CW * c), v("conv_b", c), ALU.mult, ALU.add))
                for j in range(1, CW):
                    t = (CW - 1) * c + j - 1
                    pool.wait_ge(tap_ready, t + 1)
                    if j > 1:
                        pool.wait_ge(tap_added, t)
                    last = G.tensor_tensor(out[:, 0:TOK], out[:, 0:TOK], tap_place(t)[:, 0:TOK], ALU.add)
                    last.then_inc(tap_added, 1)

            lv = 0
            pool.wait_ge(gates_ready, 1)
            pool.wait_ge(psum_free, U_OUT)
            for t, (c0, n) in enumerate(TILES):
                cols = slice(c0, c0 + n)
                if t:
                    pool.wait_ge(s["gates_ps"], t)
                G.tensor_copy(G_B[0:n], over_cols(gate["g"][0:n, t, :], P))
                if t == 4:
                    G.tensor_tensor(gx[0:n], over_cols(gate["g"][0:n, t, :], NG), over_heads(mask[0:n, MASK["group"]], n),
                                    ALU.mult)
                G.tensor_copy(B_B[0:n], over_cols(gate["beta"][0:n, t, :], P)).then_inc(s["gates_b"], 1)
                pool.wait_ge(s["e_ready"], t + 1)
                G.tensor_tensor(EM[0:n, :, 0:n], E_[0:n, :, 0:n], over_heads(m("incl4" if t == 4 else "incl", n), n),
                                ALU.mult).then_inc(s["em_ready"], 1)
                pool.wait_ge(s["em_ready"], t + 1)
                pool.wait_ge(s["bs_ready"], t + 1)
                G.tensor_tensor(ES[0:n, :, 0:n], ES[0:n, :, 0:n], EM[0:n, :, 0:n], ALU.mult).then_inc(s["es_ready"], 1)
                pool.wait_ge(s["at_ready"], t + 1)
                for l in range(1, LEVELS[t]):
                    if l == 3:
                        pool.wait_ge(s["eg_ready"], t + 1)
                        pool.wait_ge(s["qk_normed"], t + 1)
                        G.tensor_tensor(EG[:, :, 0:n], EG[:, :, 0:n], qkv[:, 0:H, cols], ALU.mult).then_inc(s["qg_ready"], 1)
                    if l >= 3:
                        pool.wait_ge(s["t1_ps"], lv - t + l - 2)
                    G.tensor_tensor((BM0, BM1)[l % 2][0:n, :, 0:n], AT[0:n, :, 0:n], over_heads(m("levels", n, l), n),
                                    ALU.mult).then_inc(s["b_ready"], 1)
                lv += LEVELS[t]
            sum_squares(2)
            sum_squares(3)


_OUTS = {"y_t": (P, KT, TOK), "new_state": (P, H, NG, P), "last_q": (P, NQ, 27), "last_c": (P, NC_, 270)}


def feature_tiles(a):
    return np.ascontiguousarray(a.T.reshape(-1, P, a.shape[0]).transpose(1, 0, 2))


def unit_list(i):
    w_in = i["w_in"][0]
    qkv_z = NQ * P + H * P
    glu = qkv_z + 2 * H
    units = np.zeros((U_END, P, KT, P), np.float32)
    at = [0]

    def add(w, r0, rows, c0):
        block = w[r0 * P:(r0 + rows) * P, c0:c0 + P]
        units[at[0], :, 0:rows, :] = block.reshape(rows, P, P).transpose(1, 0, 2)
        at[0] += 1

    def ffn(w1, w3, w2):
        g = 0
        for n in PARTS:
            for f in range(g, g + n):
                add(w1, 0, KT, f * P)
                add(w3, 0, KT, f * P)
            for k in range(KT):
                add(w2, g, n, k * P)
            g += n

    ffn(i["ffn1_w1"][0], i["ffn1_w3"][0], i["ffn1_w2"][0])
    for c in range(NC_):
        add(w_in, 0, KT, glu + c * P)
        add(w_in, 0, KT, glu + (NC_ + c) * P)
    for c in range(NQ + H):
        add(w_in, 0, KT, c * P)
    for k in range(KT):
        add(i["w_out"][0], 0, KT, k * P)
    ffn(i["ffn2_w1"][0], i["ffn2_w3"][0], i["ffn2_w2"][0])
    assert at[0] == U_END
    return units


def kernel(**inputs):
    import concourse.bacc as bacc
    from concourse.bass_utils import run_bass_kernel_spmd

    i = {k: np.asarray(a) for k, a in inputs.items()}
    x = np.concatenate([i["meta_tokens"], i["x_prompt"][0], i["x_sample"].reshape(NB * LB, D)])
    vecs = np.zeros((P, NV), np.float32)
    for name in ("ffn1_norm", "mix_norm", "ffn2_norm", "conv_b", "conv_norm", "o_norm"):
        vecs[:, VEC[name]] = i[name][0].reshape(-1, P).T
    vecs[:, VEC["final_norm"]] = i["final_norm"].reshape(-1, P).T
    for name, w in (("qkv_conv_w", SC), ("conv_w", CW)):
        vecs[:, VEC[name]] = i[name][0].T.reshape(-1, P, w).transpose(1, 0, 2).reshape(P, -1)
    vecs[:, VEC["dt_bias"]] = i["dt_bias"][0]
    vecs[:, VEC["a_log"]] = i["a_log"][0]
    ba = i["w_in"][0][:, (NQ + H) * P:(NQ + H) * P + 2 * H]
    vecs[:, VEC["w_ba"]] = ba.reshape(KT, P, 2 * H).transpose(1, 0, 2).reshape(P, -1)
    arrays = {
        "weights": unit_list(i),
        "x_t": feature_tiles(x),
        "vecs": vecs,
        "masks": shape_masks(),
        "hist_q": feature_tiles(i["state_qkv_conv"][0].reshape(NB * (SC - 1), NQ * P)),
        "hist_c": np.ascontiguousarray(
            feature_tiles(i["state_conv"][0].reshape(NB * (CW - 1), NC_ * P)).reshape(P, NC_, NB, CW - 1)),
        "states": np.ascontiguousarray(i["state_delta"][0].transpose(2, 1, 0, 3)),
    }
    nc = bacc.Bacc("TRN2", target_bir_lowering=False, num_devices=1)
    args = [nc.dram_tensor(n, a.shape, mybir.dt.from_np(a.dtype), kind="ExternalInput").ap() for n, a in arrays.items()]
    args += [nc.dram_tensor(n, shape, F32, kind="ExternalOutput").ap() for n, shape in _OUTS.items()]
    build(nc, *args)
    r = run_bass_kernel_spmd(nc, [arrays], core_ids=[0]).results[0]
    y = r["y_t"].transpose(2, 1, 0).reshape(TOK, D)
    st = r["new_state"].transpose(1, 2, 0, 3)
    lq = r["last_q"].transpose(2, 1, 0).reshape(27, NQ * P)
    lc = r["last_c"].transpose(2, 1, 0).reshape(270, NC_ * P)
    c = np.ascontiguousarray
    return (c(y[N_META:L][None]), c(y[L:].reshape(NB, LB, D)), c(st[:, 0][None, None]),
            c(lq[0:3][None, None]), c(lc[0:30][None, None]), c(st[:, 1:].transpose(1, 0, 2, 3)[None]),
            c(lq[3:].reshape(1, NB, SC - 1, NQ * P)), c(lc[30:].reshape(1, NB, CW - 1, NC_ * P)))
```

```python
from contextlib import ExitStack

import numpy as np
import concourse.bass as bass
from concourse import mybir

F32 = mybir.dt.float32
F32R = mybir.dt.float32r
ACT = mybir.ActivationFunctionType
ALU = mybir.AluOpType

P = 128
D = 1024
KT = D // P
SEQ_LEN, N_META = 512, 16
L = SEQ_LEN + N_META
NB, LB = 8, 8
TOK = L + NB * LB
HALF = TOK // 2
FT = 2816 // P
PARTS = [8, 8, 6]
H = 4
NQ = 3 * H
NC_ = 4
SC, CW = 4, 31
POOL_TAPS = 3 * (CW - 1)
EPS = 1e-6

U_FFN1 = 0
FFN_UNITS = 2 * FT + 8 * len(PARTS)
U_GLU = U_FFN1 + FFN_UNITS
U_QKV = U_GLU + 2 * NC_
U_Z = U_QKV + NQ
U_OUT = U_Z + H
U_FFN2 = U_OUT + 8
U_END = U_FFN2 + FFN_UNITS
assert all(u % 4 == 0 for u in (U_FFN1, U_GLU, U_QKV, U_Z, U_OUT, U_FFN2, U_END))

QP = SC - 1 + L
QS = SC - 1 + LB
QE = QP + NB * QS
QO = QE - (SC - 1)
CP = CW - 1 + L
CS = CW - 1 + LB
CE = CP + NB * CS

TILES = [(128 * t, 128) for t in range(4)] + [(512, 80)]
NT = len(TILES)
NG = 1 + NB
GROUPS = [(0, 16)] + [(16 + LB * b, LB) for b in range(NB)]
LEVELS = [7, 7, 7, 7, 4]
LVO = [0, 0, 7, 7, 14]


def merge(a, b):
    if len(b) > len(a):
        a, b = b, a
    out, taken = [], 0
    for i, x in enumerate(a):
        out.append(x)
        while taken * len(a) < (i + 1) * len(b):
            out.append(b[taken])
            taken += 1
    return out


def delta_schedule():
    prep = [[("prep", t, i) for i in range(9)] for t in range(NT)]
    tok = [[("tok", t, i) for i in range(2)] for t in range(NT)]
    scan = [[("scan", t, i) for i in range(7)] for t in range(4)]
    chain = [[("start", t, i) for i in range(2)] + [("level", t, 2 * l + i) for l in range(1, LEVELS[t]) for i in range(2)]
             + [("end", t, 0)] for t in range(NT)]
    final = [("final", 4, i) for i in range(8)]
    out = [("gates", 0, i) for i in range(3)] + merge(prep[0], prep[1])
    out += merge(merge(chain[0], chain[1]), tok[0] + tok[1] + prep[2] + prep[3])
    out += merge(merge(chain[2], chain[3]), merge(scan[0] + scan[1], prep[4]) + tok[2] + tok[3])
    out += merge(merge(scan[2] + tok[4] + scan[3], chain[4]), [("conv", c, 0) for c in range(NC_)])
    out += merge(final, [("weights", j, 0) for j in range(4)] + [("conv", 4, 0)])
    return out

VEC = {}
_at = 0
for _n, _w in (("ffn1_norm", 8), ("mix_norm", 8), ("ffn2_norm", 8), ("final_norm", 8), ("qkv_conv_w", NQ * SC),
               ("conv_w", NC_ * CW), ("conv_b", NC_), ("conv_norm", NC_), ("o_norm", 1), ("dt_bias", H),
               ("a_log", H), ("w_ba", KT * 2 * H)):
    VEC[_n] = slice(_at, _at + _w)
    _at += _w
NV = _at

MASK = {}
_at = 0
for _n, _w in (("ident", P), ("incl", P), ("strict", P), ("incl4", P), ("strict4", P), ("same4", P),
               ("levels", 7 * P), ("group", NG)):
    MASK[_n] = slice(_at, _at + _w)
    _at += _w
NM = _at


def shape_masks():
    m = np.zeros((P, NM), np.float32)
    s, c = np.arange(P)[:, None], np.arange(P)[None, :]
    seq = np.where(np.arange(P) < 16, 0, 1 + (np.arange(P) - 16) // LB)
    seq[80:] = 99
    same = (seq[:, None] == seq[None, :]) & (s < 80) & (c < 80)
    m[:, MASK["ident"]] = s == c
    m[:, MASK["incl"]] = s <= c
    m[:, MASK["strict"]] = s < c
    m[:, MASK["incl4"]] = (s <= c) & same
    m[:, MASK["strict4"]] = (s < c) & same
    m[:, MASK["same4"]] = same
    for l in range(7):
        w = 1 << l
        a = MASK["levels"].start + l * P
        m[:, a:a + P] = (s // (2 * w) == c // (2 * w)) & (s % (2 * w) < w) & (c % (2 * w) >= w)
    m[:, MASK["group"]] = seq[:, None] == np.arange(NG)[None, :]
    return m


def build(nc, weights, x_t, vecs, masks, hist_q, hist_c, states, y_t, new_state, last_q, last_c):
    ctx = ExitStack()
    with ctx:
        def sb(name, shape, dt=F32, where=ctx):
            return where.enter_context(nc.sbuf_tensor(name, shape, dt))

        def sem(name):
            return ctx.enter_context(nc.semaphore(name))

        h = sb("h", [P, KT, TOK])
        raw = sb("raw", [P, 2, KT, P])
        rstd = sb("rstd", [P, TOK])
        ssum = sb("ssum", [P, TOK])
        sq = sb("sq", [P, 2, TOK])
        work = sb("work", [P, 8, QE])
        vec = sb("vec", [P, NV])
        mask = sb("mask", [P, NM])
        mean_d = sb("mean_d", [P, P])
        mean_c = sb("mean_c", [P, P])
        ones = sb("ones", [P, P])
        eps = sb("eps", [P, 1])
        c_ext = sb("c_ext", [P, NC_, CE])
        hq = sb("hq", [P, NQ, NB * (SC - 1)])
        lastq = sb("lastq", [P, NQ, (1 + NB) * (SC - 1)])
        wba_hi = sb("wba_hi", [P, KT, 2 * H], F32R)
        wba_lo = sb("wba_lo", [P, KT, 2 * H], F32R)
        gate = {n: sb("gate_" + n, [P, NT, H]) for n in ("beta", "g", "t1", "t2", "t3")}
        ba = sb("ba", [P, NT, 2 * H])
        rtok = sb("rtok", [P, 8])
        expa = sb("expa", [P, H])
        gcs = sb("gcs", [P, 2 * NT * H + H * NG])
        f_cum, f_rest, f_all, f_kbg = [sb("f_" + n, [P, NT, H]) for n in ("cum", "rest", "all", "kbg")]
        f_group = sb("f_group", [P, H * NG])
        gx = sb("gx", [P, H, NG])
        zone = ExitStack()
        w_hi = sb("w_hi", [P, 4, KT, P], F32R, zone)
        w_lo = sb("w_lo", [P, 4, KT, P], F32R, zone)
        x_hi = sb("x_hi", [P, KT, TOK], F32R, zone)
        x_lo = sb("x_lo", [P, KT, TOK], F32R, zone)
        zone.close()
        zone = ExitStack()

        def ring(name, n):
            return [sb(f"d_{name}{i}", [P, H, P], F32, zone) for i in range(n)]

        G_B, B_B, E_, ES, AT, BM, X_, T1 = [ring(n, 2) for n in ("g_b", "beta_b", "decay", "decay_strict", "a_t", "b",
                                                                  "inv", "t1")]
        Y_ = ring("inv_t", 2)
        ATT, EG = ring("att_t", 4), ring("egrow", 4)
        NWT, U_, KBG = ring("neg_w_t", 2), ring("u", 2), ring("kbg", 2)
        KG = ring("kg", 2)
        VN = ring("v_new", 1)[0]
        if 2 * KT * TOK + 8 * KT * P > 35 * H * P:
            sb("hold1", [P, 2 * KT * TOK + 8 * KT * P - 35 * H * P], F32, zone)
        ctx.enter_context(zone)
        zone2 = ExitStack()
        g_hi = sb("g_hi", [P, 8, TOK], F32R, zone2)
        g_lo = sb("g_lo", [P, 8, TOK], F32R, zone2)
        zone2.close()
        qkv = sb("qkv", [P, NQ, TOK], F32, zone2)
        S = sb("S", [P, H, NG, P], F32, zone2)
        z = sb("z", [P, H, TOK], F32, zone2)
        ctx.enter_context(zone2)

        ps = ctx.enter_context(nc.psum_tensor("ps", [P, 4, 2, 512], F32))

        def bank(j):
            return ps[:, j // 2, j % 2, :]

        def heads(j, n):
            return bank(j).rearrange("p (h c) -> p h c", h=H)[:, :, 0:n]

        def v(name, i=0, n=1):
            return vec[:, VEC[name].start + i:VEC[name].start + i + n]

        def m(name, n=P, i=0):
            a = MASK[name].start + i * P
            return mask[0:n, a:a + n]

        def chain_at(t):
            p = t % 2
            return p, 2 * p, 2 * p + 1, LVO[t], LVO[t] - t // 2

        def side_banks(t):
            return (6, 7) if t == 1 else (4, 5)

        def tile_mask(name, t, i=0, cols=None):
            n = TILES[t][1]
            a = MASK[name + "4" if t == 4 and name in ("incl", "strict") else name].start + i * P
            return mask[0:n, a:a + (cols or n)]

        def h4(ap, n):
            return ap[:, 0:H * n].rearrange("p (h c) -> p h c", h=H)

        n4 = TILES[4][1]
        VX = work[0:n4, 0:2, :].rearrange("p a b -> p (a b)")[:, 0:NG * P]
        VX3 = VX.rearrange("p (g c) -> p g c", g=NG)

        def over_heads(ap, n):
            return ap.unsqueeze(1).to_broadcast([n, H, ap.shape[1]])

        def over_cols(ap, c):
            return ap.unsqueeze(2).to_broadcast([ap.shape[0], ap.shape[1], c])

        raw_in = [sem(f"raw_in{i}") for i in range(2)]
        w_hi_ready = sem("w_hi_ready")
        w_lo_ready = sem("w_lo_ready")
        unit_done = sem("unit_done")
        psum_free = sem("psum_free")
        x_in = sem("x_in"); vec_in = sem("vec_in"); hist_in = sem("hist_in"); state_in = sem("state_in")
        ones_set = sem("ones_set")
        sq_ready = sem("sq_ready"); ssum_step = sem("ssum_step"); stats_done = sem("stats_done")
        rstd_ready = sem("rstd_ready")
        x_hi_ready = sem("x_hi_ready"); x_ready = sem("x_ready")
        silu_done = sem("silu_done"); sr_ready = sem("sr_ready")
        g_hi_ready = sem("g_hi_ready"); g_ready = sem("g_ready")
        wba_hi_ready = sem("wba_hi_ready"); wba_ready = sem("wba_ready")
        pads_set = sem("pads_set")
        link_s = sem("dve_link")
        pool_s = sem("pool_link")
        ab_ready = sem("ab_ready"); gate_act = sem("gate_act"); gates_ready = sem("gates_ready")
        gate_in = sem("gate_in"); sig_ready = sem("sig_ready"); c_in_ready = sem("c_in_ready")
        tap_ready = sem("tap_ready"); tap_added = sem("tap_added"); conv3_step = sem("conv3_step")
        lastq_saved = sem("lastq_saved"); q_conv = sem("q_conv"); q_ready = sem("q_ready")
        names = ("qk_sq norms_ps qk_log qk_factor o_log o_factor qk_normed gates_b gates_ps d_diff e_ready eg_ready "
                 "bs_ready em_ready es_ready qg_ready diffs facs f_ready tok_ps tok_ready gram_ps kk_ps at_ready "
                 "att_ready x1_ps wt_ps u_ps nwt_ready u_ready vn_ps vn_ready o_ps o_evac s_ps s_ready osq_ready on_ps "
                 "o_ready vnt_ps vnt_ready os_ps os_ready vn4_ps att4_ps gx_ready gsum_ps vx_ready s4_ps s4_ready "
                 "s_scaled").split()
        s = {n: sem(n) for n in names}
        for n in ("b_ready", "y_ready", "x_inv", "t1_ps", "t1_ready", "p_ps"):
            s[n] = [sem(f"{n}{i}") for i in range(2)]
        z_ready = sem("z_ready"); mix_ready = sem("mix_ready")
        csq_ready = sem("csq_ready"); cn_ps = sem("cn_ps"); c_factor = sem("c_factor"); root_done = sem("root_done"); c_scaled = sem("c_scaled"); c_act = sem("c_act")
        y_ready = sem("y_out_ready"); y_gain = sem("y_gain")
        out_s = sem("out_s"); state_out = sem("state_out")

        block = ctx.enter_context(nc.Block())

        def parts(base, g0):
            u, g = base, g0
            for n in PARTS:
                yield u, n, g
                u += 2 * n + 8
                g += n

        @block.sync
        def _(sp):
            sp.dma_start(vec[:], vecs).then_inc(vec_in, 16)
            sp.dma_start(h[:, 0:4], x_t[:, 0:4]).then_inc(x_in, 16)
            sp.dma_start(raw[:, 0], weights[0]).then_inc(raw_in[0], 16)
            sp.wait_ge(x_in, 16)
            sp.dma_start(h[:, 4:8], x_t[:, 4:8]).then_inc(x_in, 16)
            sp.dma_start(raw[:, 1], weights[1]).then_inc(raw_in[1], 16)
            sp.dma_start(mask[:], masks).then_inc(hist_in, 16)
            sp.dma_start(hq[:], hist_q).then_inc(hist_in, 16)
            for c in range(NC_):
                sp.dma_start(c_ext[:, c, CP:CE].rearrange("p (b w) -> p b w", b=NB)[:, :, 0:CW - 1],
                             hist_c[:, c]).then_inc(hist_in, 16)

            def load_pair(u):
                for j in range(2):
                    sp.wait_ge(w_lo_ready, u + j - 1)
                    sp.dma_start(raw[:, j], weights[u + j]).then_inc(raw_in[j], 16)

            with sp.Fori(0, (U_QKV + 4 - 2) // 2) as i:
                load_pair(2 * i + 2)
            sp.wait_ge(unit_done, U_GLU)
            sp.dma_start(S[:, :, 1:NG, :], states).then_inc(state_in, 16)
            with sp.Fori(0, (U_END - U_QKV - 4) // 2) as i:
                load_pair(2 * i + U_QKV + 4)
            sp.wait_ge(lastq_saved, NQ)
            sp.dma_start(last_q, lastq[:]).then_inc(out_s, 16)
            sp.wait_ge(c_in_ready, NC_)
            for c in range(NC_):
                sp.dma_start(last_c[:, c, 0:30], c_ext[:, c, L:L + 30]).then_inc(out_s, 16)
                sp.dma_start(last_c[:, c, 30:270].rearrange("p (b w) -> p b w", b=NB),
                             c_ext[:, c, CP:CE].rearrange("p (b w) -> p b w", b=NB)[:, :, LB:CS]).then_inc(out_s, 16)
            for k in range(KT):
                sp.wait_ge(y_ready, k + 1)
                sp.dma_start(y_t[:, k], h[:, k]).then_inc(out_s, 16)
            sp.wait_ge(out_s, 16 * (1 + 2 * NC_ + KT))

        @block.tensor
        def _(pe):
            def product(u, slot, kt, xh, xl, k_sem=None, k_base=0):
                pe.wait_ge(w_lo_ready, u + 1)
                for k in range(kt):
                    if k_sem is not None:
                        pe.wait_ge(k_sem, k_base + k + 1)
                    for n, (w, x) in enumerate(((w_hi, xh), (w_hi, xl), (w_lo, xh))):
                        for half in range(2):
                            last = nc.tensor.matmul(ps[:, slot, half, 0:HALF], w[:, slot, k, :],
                                                    x[:, k, half * HALF:(half + 1) * HALF],
                                                    start=(k == 0 and n == 0), stop=(k == kt - 1 and n == 2))
                last.then_inc(unit_done, 1)

            def mean_square(stage, u):
                pe.wait_ge(ssum_step, 8 * (stage + 1))
                if u:
                    pe.wait_ge(psum_free, u)
                for half in range(2):
                    last = nc.tensor.matmul(ps[:, 3, half, 0:HALF], mean_d[:], ssum[:, half * HALF:(half + 1) * HALF],
                                            start=True, stop=True)
                return last

            def ffn(stage, base, g0, k_base):
                for p, (u0, n, g) in enumerate(parts(base, g0)):
                    if p == 0:
                        for j in range(4):
                            u = u0 + j
                            if j == 3:
                                pe.wait_ge(rstd_ready, stage + 1)
                            elif u >= 4:
                                pe.wait_ge(psum_free, u - 3)
                            product(u, j, KT, x_hi, x_lo, x_ready if j == 0 else None, k_base)
                            if j == 0:
                                mean_square(stage, u0).then_inc(stats_done, 1)
                    with pe.Fori(1 if p == 0 else 0, n // 2) as i:
                        for j in range(4):
                            pe.wait_ge(psum_free, 4 * i + (u0 + j - 3))
                            product(4 * i + (u0 + j), j, KT, x_hi, x_lo)
                    d0 = u0 + 2 * n
                    with pe.Fori(0, 2) as i:
                        for j in range(4):
                            pe.wait_ge(psum_free, 4 * i + (d0 + j - 3))
                            product(4 * i + (d0 + j), j, n, g_hi, g_lo, g_ready if j == 0 else None, g)

            pe.wait_ge(ones_set, 1)
            ffn(0, U_FFN1, 0, 0)

            for j in range(4):
                u = U_GLU + j
                if j == 3:
                    pe.wait_ge(ab_ready, 1)
                else:
                    pe.wait_ge(psum_free, u - 3)
                product(u, j, KT, x_hi, x_lo, x_ready if j == 0 else None, 8)
                if j == 0:
                    mean_square(1, U_GLU)
                    pe.wait_ge(wba_ready, 1)
                    for t, (c0, n) in enumerate(TILES):
                        for k in range(KT):
                            for r, (a, b) in enumerate(((x_hi, wba_hi), (x_lo, wba_hi), (x_hi, wba_lo))):
                                last = nc.tensor.matmul(ps[0:n, 3, 0, 304 + 8 * t:312 + 8 * t], a[:, k, c0:c0 + n],
                                                        b[:, k, :], start=(k == 0 and r == 0), stop=(k == 7 and r == 2))
                    last.then_inc(stats_done, 1)
            with pe.Fori(1, (U_Z - U_GLU) // 4) as i:
                for j in range(4):
                    pe.wait_ge(psum_free, 4 * i + (U_GLU + j - 3))
                    product(4 * i + (U_GLU + j), j, KT, x_hi, x_lo)
            for j in range(4):
                pe.wait_ge(psum_free, U_Z + j - 3)
                product(U_Z + j, j, KT, x_hi, x_lo)

            def mm(out, lhsT, rhs, start=True, stop=True):
                return nc.tensor.matmul(out, lhsT, rhs, start=start, stop=stop, skip_group_check=True)

            ident = m("ident")

            def gates(_, i):
                if i:
                    return
                pe.wait_ge(psum_free, U_OUT)
                pe.wait_ge(s["gx_ready"], 1)
                for t, (c0, n) in enumerate(TILES):
                    g = gate["g"][0:n, t, :]
                    mm(bank(3)[:, H * t:H * (t + 1)], tile_mask("incl", t, cols=P), g)
                    mm(bank(3)[:, H * (NT + t):H * (NT + t + 1)], ones[:] if t < 4 else mask[0:n, MASK["same4"]], g)
                n = TILES[4][1]
                mm(bank(3)[:, 2 * NT * H:2 * NT * H + H * NG], ones[0:n, :],
                   gx[0:n].rearrange("p h g -> p (h g)")).then_inc(s["gsum_ps"], 1)

            def prep(t, i):
                c0, n = TILES[t]
                cols = slice(c0, c0 + n)
                b0, b1 = side_banks(t)
                if i == 1:
                    pe.wait_ge(s["qk_sq"], t + 1)
                    if t >= 2:
                        pe.wait_ge(s["att_ready"], t)
                        pe.wait_ge(s["eg_ready"], t)
                        pe.wait_ge(s["tok_ready"], 2)
                    mm(heads(b0, n), ones[:], h4(sq[:, 0, :], n))
                    mm(heads(b1, n), ones[:], h4(sq[:, 1, :], n)).then_inc(s["norms_ps"], 1)
                if i == 3:
                    pe.wait_ge(s["gates_b"], t + 1)
                    pe.wait_ge(s["qk_log"], t + 1)
                    for hd in range(H):
                        mm(heads(b0, n)[:, hd, :], G_B[t % 2][0:n, hd, :], tile_mask("incl", t))
                    for hd in range(H):
                        last = mm(heads(b1, n)[:, hd, :], B_B[t % 2][0:n, hd, :], m("ident", n))
                    last.then_inc(s["gates_ps"], 1)
                if i == 6:
                    pe.wait_ge(s["qk_normed"], t + 1)
                    pe.wait_ge(s["bs_ready"], t + 1)
                    for hd in range(H):
                        last = mm(heads(b1, n)[0:n, hd, :], qkv[:, H + hd, cols], qkv[:, hd, cols])
                    last.then_inc(s["gram_ps"], 1)

            def tok(t, i):
                if i:
                    return
                c0, n = TILES[t]
                cols = slice(c0, c0 + n)
                done = (2, 2, 5, 5, 5)[t]
                pe.wait_ge(s["qk_normed"], done)
                pe.wait_ge(s["att_ready"], done)
                pe.wait_ge(s["eg_ready"], done)
                if t:
                    pe.wait_ge(s["tok_ready"], t)
                for hd in range(H):
                    nc.tensor.transpose(bank(4)[0:n, hd * P:(hd + 1) * P], qkv[:, H + hd, cols], ident)
                for hd in range(H):
                    last = nc.tensor.transpose(bank(5)[0:n, hd * P:(hd + 1) * P], qkv[:, 2 * H + hd, cols], ident)
                last.then_inc(s["tok_ps"], 1)

            def start(t, i):
                c0, n = TILES[t]
                cols = slice(c0, c0 + n)
                p, a, b, ly, lx = chain_at(t)
                if i == 0:
                    pe.wait_ge(s["qk_normed"], t + 1)
                    if t >= 2:
                        pe.wait_ge(s["nwt_ready"], t - 1)
                    else:
                        pe.wait_ge(s["diffs"], 1)
                    for hd in range(H):
                        last = mm(heads(a, n)[0:n, hd, :], qkv[:, H + hd, cols], qkv[:, H + hd, cols])
                    last.then_inc(s["kk_ps"], 1)
                else:
                    pe.wait_ge(s["y_ready"][p], ly + 1)
                    if t >= 2:
                        pe.wait_ge(s["u_ready"], t - 1)
                    for hd in range(H):
                        last = nc.tensor.transpose(bank(b)[0:n, hd * P:hd * P + n], Y_[p][0:n, hd, 0:n], m("ident", n))
                    last.then_inc(s["x1_ps"], 1)

            def level(t, i):
                l, i = i // 2, i % 2
                n = TILES[t][1]
                p, a, b, ly, lx = chain_at(t)
                if i == 0:
                    pe.wait_ge(s["b_ready"][p], lx + l)
                    pe.wait_ge(s["x_inv"][p], lx + l)
                    pe.wait_ge(s["y_ready"][p], ly + l)
                    for hd in range(H):
                        last = mm(heads(a, n)[0:n, hd, :], BM[p][0:n, hd, 0:n], X_[p][0:n, hd, 0:n])
                    last.then_inc(s["t1_ps"][p], 1)
                else:
                    pe.wait_ge(s["t1_ready"][p], lx + l)
                    for hd in range(H if l < LEVELS[t] - 1 else 0):
                        mm(heads(b, n)[0:n, hd, :], Y_[p][0:n, hd, 0:n], T1[p][0:n, hd, 0:n])
                    for hd in range(H):
                        last = mm(heads(a, n)[0:n, hd, :], T1[p][0:n, hd, 0:n], Y_[p][0:n, hd, 0:n])
                    last.then_inc(s["p_ps"][p], 1)

            def end(t, i):
                n = TILES[t][1]
                p, a, b, ly, lx = chain_at(t)
                pe.wait_ge(s["y_ready"][p], ly + LEVELS[t])
                pe.wait_ge(s["tok_ready"], t + 1)
                for hd in range(H):
                    last = mm(heads(a, n)[:, hd, :], KBG[p][0:n, hd, :], Y_[p][0:n, hd, 0:n])
                last.then_inc(s["wt_ps"], 1)
                for hd in range(H if t < 4 else 0):
                    last = mm(bank(b)[0:n, hd * P:(hd + 1) * P], Y_[p][0:n, hd, 0:n], U_[p][0:n, hd, :])
                if t < 4:
                    last.then_inc(s["u_ps"], 1)

            def scan(t, i):
                n = TILES[t][1]
                p = t % 2
                if i == 0 and t:
                    pe.wait_ge(s["nwt_ready"], t + 1)
                    pe.wait_ge(s["s_ready"], t)
                    for hd in range(H):
                        last = mm(bank(6)[0:n, hd * P:(hd + 1) * P], NWT[p][:, hd, 0:n], S[:, hd, 0, :])
                    last.then_inc(s["vn_ps"], 1)
                if i == 2:
                    pe.wait_ge(s["vn_ready"], t + 1)
                    pe.wait_ge(s["qg_ready"], t + 1)
                    pe.wait_ge(s["att_ready"], max(t + 1, 2))
                    pe.wait_ge(s["eg_ready"], max(t + 1, 2))
                    if t:
                        pe.wait_ge(s["o_log"], t)
                    for hd in range(H):
                        if t:
                            mm(heads(7, n)[:, hd, :], S[:, hd, 0, :], EG[t % 4][:, hd, 0:n], stop=False)
                        last = mm(heads(7, n)[:, hd, :], VN[0:n, hd, :], ATT[t % 4][0:n, hd, 0:n], start=(t == 0))
                    last.then_inc(s["o_ps"], 1)
                    for hd in range(H):
                        last = mm(bank(6)[:, hd * P:(hd + 1) * P], KG[p][0:n, hd, :], VN[0:n, hd, :])
                    last.then_inc(s["s_ps"], 1)
                if i == 4:
                    pe.wait_ge(s["osq_ready"], t + 1)
                    mm(heads(7, n), ones[:], h4(work[:, 2, :], n)).then_inc(s["on_ps"], 1)

            def conv(c, _):
                if c == 4:
                    return
                pe.wait_ge(csq_ready, c + 1)
                if c == 0:
                    pe.wait_ge(s["nwt_ready"], 4)
                    pe.wait_ge(s["u_ready"], 4)
                for half in range(2):
                    last = mm(ps[:, 1, half, 0:HALF], mean_c[:], sq[:, c % 2, half * HALF:(half + 1) * HALF],
                              start=(c == 0), stop=(c == NC_ - 1))
                last.then_inc(cn_ps, 1)

            def final(_, i):
                t, n = 4, TILES[4][1]
                if i == 0:
                    pe.wait_ge(s["nwt_ready"], 5)
                    pe.wait_ge(s["s_ready"], 4)
                    pe.wait_ge(state_in, 16)
                    pe.wait_ge(s["o_log"], 4)
                    for hd in range(H):
                        mm(heads(7, n)[:, hd, :], U_[0][0:n, hd, :], Y_[0][0:n, hd, 0:n], stop=False)
                        for gi, (a, w) in enumerate(GROUPS):
                            last = mm(heads(7, n)[:, hd, a:a + w], S[:, hd, gi, :], NWT[0][:, hd, a:a + w], start=False,
                                      stop=(gi == NG - 1))
                    last.then_inc(s["vnt_ps"], 1)
                    pe.wait_ge(s["qg_ready"], 5)
                    for hd in range(H):
                        for gi, (a, w) in enumerate(GROUPS):
                            last = mm(heads(0, n)[:, hd, a:a + w], S[:, hd, gi, :], EG[0][:, hd, a:a + w])
                    last.then_inc(s["os_ps"], 1)
                if i == 1:
                    pe.wait_ge(s["vnt_ready"], 1)
                    pe.wait_ge(c_factor, 1)
                    for hd in range(H):
                        last = nc.tensor.transpose(bank(2)[0:n, hd * P:(hd + 1) * P],
                                                   work[:, 3, hd * n:(hd + 1) * n], ident)
                    last.then_inc(s["vn4_ps"], 1)
                if i == 2:
                    pe.wait_ge(s["vn_ready"], 5)
                    for hd in range(H):
                        last = mm(heads(3, n)[:, hd, :], VN[0:n, hd, :], ATT[0][0:n, hd, 0:n])
                    last.then_inc(s["att4_ps"], 1)
                if 3 <= i < 3 + H:
                    hd = i - 3
                    if hd == 1:
                        pe.wait_ge(s["osq_ready"], 5)
                        mm(heads(2, n), ones[:], h4(sq[:, 0, :], n)).then_inc(s["on_ps"], 1)
                    pe.wait_ge(s["vx_ready"], hd + 1)
                    if hd:
                        pe.wait_ge(s["s4_ready"], hd)
                    for j, (a, w) in enumerate(((0, 512), (512, 512), (1024, 128))):
                        last = mm(bank(4 + j)[:, 0:w], KG[0][0:n, hd, :], VX[:, a:a + w])
                    last.then_inc(s["s4_ps"], 1)

            def weights_split(j, _):
                pass

            steps = {"gates": gates, "prep": prep, "tok": tok, "start": start, "level": level, "end": end, "scan": scan,
                     "conv": conv, "final": final, "weights": weights_split}
            for name, t, i in delta_schedule():
                steps[name](t, i)

            for j in range(4):
                if j == 1:
                    pe.wait_ge(s["o_log"], 5)
                if j == 2:
                    pe.wait_ge(s["s4_ready"], H)
                product(U_OUT + j, j, KT, x_hi, x_lo, x_ready if j == 0 else None, 16)
            for j in range(4):
                pe.wait_ge(psum_free, U_OUT + 1 + j)
                product(U_OUT + 4 + j, j, KT, x_hi, x_lo)

            ffn(2, U_FFN2, FT, 24)
            pe.wait_ge(ssum_step, 32)
            pe.wait_ge(psum_free, U_END - 3)
            for half in range(2):
                last = nc.tensor.matmul(ps[:, 0, half, 0:HALF], mean_d[:], ssum[:, half * HALF:(half + 1) * HALF],
                                        start=True, stop=True)
            last.then_inc(stats_done, 1)

        def tap_place(t):
            return (ssum, sq[:, 0, :], sq[:, 1, :])[t % 3]

        def both(slot):
            return ps[:, slot, :, 0:HALF]

        def two(ap):
            return ap.rearrange("p (a b) -> p a b", a=2)

        @block.scalar
        def _(act):
            def split_hi(u, slot, first=False):
                if not isinstance(u, int):
                    act.wait_ge(raw_in[slot % 2], u * 8 + (16 - 8 * (slot % 2)))
                else:
                    act.wait_ge(raw_in[slot % 2], 16 * (u // 2 + 1))
                if not first:
                    act.wait_ge(unit_done, u - 3)
                nc.scalar.copy(w_hi[:, slot], raw[:, slot % 2]).then_inc(w_hi_ready, 1)

            def prepare(stage, norm, ready, split=True):
                for k in range(KT):
                    ready(k)
                    if 8 * stage + k >= 2:
                        act.wait_ge(ssum_step, 8 * stage + k - 1)
                    nc.scalar.activation(sq[:, k % 2, :], h[:, k, :], ACT.Square).then_inc(sq_ready, 1)
                    if split:
                        nc.scalar.activation(x_hi[:, k, :], h[:, k, :], ACT.Copy, scale=v(norm, k)).then_inc(x_hi_ready, 1)

            def root(stage, slot=3):
                act.wait_ge(stats_done, stage + 1)
                nc.scalar.activation(two(rstd[:]), both(slot), ACT.Sqrt, bias=eps[:]).then_inc(root_done, 1)

            def hidden(ua, f, gslot, j):
                act.wait_ge(psum_free, ua + 1)
                nc.scalar.activation(work[:, 2 + j, 0:TOK], work[:, j, 0:TOK], ACT.Silu).then_inc(silu_done, 1)
                split_hi(ua + 4, (2 * j) % 4)
                act.wait_ge(psum_free, ua + 2)
                nc.scalar.copy(g_hi[:, gslot, :], work[:, 6 + j, 0:TOK]).then_inc(g_hi_ready, 1)
                split_hi(ua + 5, (2 * j + 1) % 4)

            def ffn(base, g0, finish):
                for p, (u0, n, g) in enumerate(parts(base, g0)):
                    with act.Fori(0, n // 2) as i:
                        for j in range(2):
                            hidden(4 * i + (u0 + 2 * j), 2 * i + (g + j), 2 * i + j, j)
                    d0 = u0 + 2 * n
                    if p < len(PARTS) - 1:
                        with act.Fori(0, 2) as i:
                            for j in range(4):
                                split_hi(4 * i + (d0 + j + 4), j)
                    else:
                        finish(d0)

            act.wait_ge(vec_in, 16)
            act.wait_ge(ones_set, 1)
            nc.scalar.copy(wba_hi[:], v("w_ba", 0, KT * 2 * H).rearrange("p (k c) -> p k c", k=KT)).then_inc(wba_hi_ready, 1)
            nc.scalar.activation(expa[:], v("a_log", 0, H), ACT.Exp)

            def x_tile(k):
                act.wait_ge(x_in, 16 * (1 + k // 4))

            split_hi(0, 0, True)
            prepare(0, "ffn1_norm", x_tile)
            split_hi(1, 1, True)
            split_hi(2, 2, True)
            split_hi(3, 3, True)
            root(0)

            def finish_with(stage, norm, lookahead):
                def finish(d0):
                    def ready(k):
                        if d0 + k + 4 < U_END:
                            split_hi(d0 + k + 4, k % 4)
                        act.wait_ge(psum_free, d0 + k + 1)
                    prepare(stage, norm, ready, norm is not None)
                return finish

            ffn(U_FFN1, 0, finish_with(1, "mix_norm", True))

            root(1)
            act.wait_ge(ab_ready, 1)
            nc.scalar.activation(gate["beta"][:], ba[:, :, 0:H], ACT.Sigmoid).then_inc(gate_act, 1)
            nc.scalar.activation(gate["t2"][:], gate["t1"][:], ACT.Exp, scale=-1.0).then_inc(gate_act, 1)
            act.wait_ge(gate_act, 2)
            nc.scalar.activation(gate["t3"][:], gate["t2"][:], ACT.Ln, bias=1.0).then_inc(gate_act, 1)

            taps = [0]

            def conv_taps(n):
                for t in range(taps[0], min(taps[0] + n, POOL_TAPS)):
                    c, j = t // (CW - 1), 1 + t % (CW - 1)
                    act.wait_ge(c_in_ready, c + 1)
                    if t >= 3:
                        act.wait_ge(tap_added, t - 2)
                    o = tap_place(t)
                    nc.scalar.activation(o[:, 0:L], c_ext[:, c, j:j + L], ACT.Copy, scale=v("conv_w", CW * c + j))
                    nc.scalar.activation(o[:, L:TOK].rearrange("p (b w) -> p b w", b=NB),
                                         c_ext[:, c, CP:CE].rearrange("p (b w) -> p b w", b=NB)[:, :, j:j + LB],
                                         ACT.Copy, scale=v("conv_w", CW * c + j)).then_inc(tap_ready, 1)
                taps[0] += n

            act.wait_ge(pads_set, 1)
            act.wait_ge(hist_in, 16 * (2 + NC_))
            for c in range(NC_):
                u = U_GLU + 2 * c
                split_hi(u + 4, (u + 4) % 4)
                if c:
                    conv_taps(8)
                act.wait_ge(psum_free, u + 2)
                nc.scalar.activation(work[:, 1 + 2 * (c % 2), 0:TOK], work[:, 1 + 2 * (c % 2), 0:TOK],
                                     ACT.Sigmoid).then_inc(sig_ready, 1)
                split_hi(u + 5, (u + 5) % 4)
            for i in range(NQ):
                u = U_QKV + i
                split_hi(u + 4, (u + 4) % 4)
                conv_taps(4)
                act.wait_ge(psum_free, u + 1)
                e = work[:, i % 2, :]
                nc.scalar.copy(lastq[:, i, 0:3], e[:, L:L + 3])
                nc.scalar.copy(lastq[:, i, 3:27].rearrange("p (b w) -> p b w", b=NB),
                               e[:, QP:QE].rearrange("p (b w) -> p b w", b=NB)[:, :, LB:QS]).then_inc(lastq_saved, 1)
                act.wait_ge(q_conv, i + 1)
                a = work[:, 2 + i % 2, :]
                nc.scalar.activation(qkv[:, i, 0:L], a[:, 0:L], ACT.Silu)
                nc.scalar.activation(qkv[:, i, L:TOK].rearrange("p (b w) -> p b w", b=NB),
                                     a[:, QP:QE].rearrange("p (b w) -> p b w", b=NB)[:, :, 0:LB],
                                     ACT.Silu).then_inc(q_ready, 1)
            for i in range(H):
                u = U_Z + i
                conv_taps(5)
                act.wait_ge(psum_free, u + 1)
                nc.scalar.activation(z[:, i, :], z[:, i, :], ACT.Silu).then_inc(z_ready, 1)

            def gates(_, i):
                if i == 0:
                    nc.scalar.preload_act_table_set("natural_log_exp_and_others")
                if i == 2:
                    act.wait_ge(s["diffs"], 1)
                    nt = NT * H
                    nc.scalar.activation(f_cum[:].rearrange("p t h -> p (t h)"), gcs[:, 0:nt], ACT.Exp)
                    nc.scalar.activation(f_all[:].rearrange("p t h -> p (t h)"), gcs[:, nt:2 * nt], ACT.Exp)
                    nc.scalar.activation(f_group[:], gcs[:, 2 * nt:2 * nt + H * NG], ACT.Exp)
                    nc.scalar.activation(f_rest[:], f_kbg[:], ACT.Exp).then_inc(s["facs"], 1)

            def prep(t, i):
                c0, n = TILES[t]
                cols = slice(c0, c0 + n)
                p = t % 2
                b0, b1 = side_banks(t)
                r = work[:, 2 * p:2 * p + 2, 0:H * n]
                if i == 0:
                    if t == 0:
                        act.wait_ge(q_ready, NQ)
                        act.wait_ge(tap_added, POOL_TAPS)
                    else:
                        act.wait_ge(s["norms_ps"], t)
                    for q in range(2):
                        last = nc.scalar.activation(h4(sq[:, q, :], n), qkv[:, H * q:H * (q + 1), cols], ACT.Square)
                    last.then_inc(s["qk_sq"], 1)
                if i == 2:
                    act.wait_ge(s["norms_ps"], t + 1)
                    if t >= 2:
                        act.wait_ge(s["qk_normed"], t - 1)
                    for q, b in enumerate((b0, b1)):
                        last = nc.scalar.activation(h4(work[:, 2 * p + q, :], n), heads(b, n), ACT.Ln, bias=eps[:])
                    last.then_inc(s["qk_log"], 1)
                if i == 3:
                    act.wait_ge(s["qk_log"], t + 1)
                    nc.scalar.activation(r, r, ACT.Exp, scale=-0.5).then_inc(s["qk_factor"], 1)
                if i == 5:
                    act.wait_ge(s["d_diff"], t + 1)
                    nc.scalar.activation(E_[p][0:n, :, 0:n], E_[p][0:n, :, 0:n], ACT.Exp).then_inc(s["e_ready"], 1)
                    if t == 4:
                        act.wait_ge(s["o_ps"], 1)
                    nc.scalar.activation(EG[t % 4][:, :, 0:n], heads(b0, n), ACT.Exp).then_inc(s["eg_ready"], 1)

            def tok(t, i):
                pass

            def start(t, i):
                n = TILES[t][1]
                p, a, b, ly, lx = chain_at(t)
                if i == 1:
                    act.wait_ge(s["x1_ps"], t + 1)
                    nc.scalar.copy(X_[p][0:n, :, 0:n], heads(b, n)[0:n]).then_inc(s["x_inv"][p], 1)

            def level(t, i):
                l, i = i // 2, i % 2
                n = TILES[t][1]
                p, a, b, ly, lx = chain_at(t)
                if i == 0:
                    act.wait_ge(s["t1_ps"][p], lx + l)
                    nc.scalar.copy(T1[p][0:n, :, 0:n], heads(a, n)[0:n]).then_inc(s["t1_ready"][p], 1)

            def end(t, i):
                n = TILES[t][1]
                p, a, b, ly, lx = chain_at(t)
                act.wait_ge(s["wt_ps"], t + 1)
                if t >= 3:
                    act.wait_ge(s["vn_ps"], t - 2)
                nc.scalar.activation(NWT[p][:, :, 0:n], heads(a, n), ACT.Copy, scale=-1.0).then_inc(s["nwt_ready"], 1)

            def o_norm(t, b, n):
                r = h4(work[:, 3, :], n)
                act.wait_ge(s["on_ps"], t + 1)
                nc.scalar.activation(r, heads(b, n), ACT.Ln, bias=eps[:], scale=1.0 / P).then_inc(s["o_log"], 1)
                act.wait_ge(s["o_log"], t + 1)
                nc.scalar.activation(r, r, ACT.Exp, scale=-0.5).then_inc(s["o_factor"], 1)

            def scan(t, i):
                c0, n = TILES[t]
                cols = slice(c0, c0 + n)
                if i == 3:
                    act.wait_ge(s["o_ps"], t + 1)
                    nc.scalar.copy(qkv[:, 0:H, cols], heads(7, n)).then_inc(s["o_evac"], 1)
                    act.wait_ge(s["o_evac"], t + 1)
                    if t == 0:
                        act.wait_ge(s["qk_normed"], 4)
                    else:
                        act.wait_ge(s["on_ps"], t)
                    nc.scalar.activation(h4(work[:, 2, :], n), qkv[:, 0:H, cols], ACT.Square).then_inc(s["osq_ready"], 1)
                if i == 5:
                    if t:
                        act.wait_ge(s["o_ready"], t)
                    o_norm(t, 7, n)

            def conv(c, _):
                if c < 4:
                    if c == 0:
                        act.wait_ge(s["norms_ps"], NT)
                    if c < 3:
                        act.wait_ge(tap_added, (CW - 1) * (c + 1))
                    else:
                        act.wait_ge(conv3_step, CW)
                    if c >= 2:
                        act.wait_ge(cn_ps, c - 1)
                    nc.scalar.activation(sq[:, c % 2, :], work[:, 4 + c, 0:TOK], ACT.Square).then_inc(csq_ready, 1)
                    if c < 3:
                        return
                    act.wait_ge(cn_ps, NC_)
                    nc.scalar.activation(two(ssum[:]), both(1), ACT.Ln, bias=eps[:]).then_inc(c_factor, 1)
                    act.wait_ge(c_factor, 1)
                    nc.scalar.activation(ssum[:], ssum[:], ACT.Exp, scale=-0.5).then_inc(c_factor, 1)

            def final(_, i):
                t, (c0, n) = 4, TILES[4]
                if i == 0:
                    act.wait_ge(s["vnt_ps"], 1)
                    act.wait_ge(s["o_ready"], 4)
                    nc.scalar.copy(h4(work[:, 3, :], n), heads(7, n)).then_inc(s["vnt_ready"], 1)
                    act.wait_ge(s["os_ps"], 1)
                    nc.scalar.copy(h4(work[:, 2, :], n), heads(0, n)).then_inc(s["os_ready"], 1)
                if i == 3:
                    act.wait_ge(s["o_evac"], NT)
                    nc.scalar.activation(h4(sq[:, 0, :], n), qkv[:, 0:H, c0:c0 + n], ACT.Square).then_inc(s["osq_ready"], 1)
                if i == 4:
                    o_norm(4, 2, n)

            def weights_split(j, _):
                if j == 0:
                    act.wait_ge(s["wt_ps"], NT)
                split_hi(U_OUT + j, j)

            steps = {"gates": gates, "prep": prep, "tok": tok, "start": start, "level": level, "end": end, "scan": scan,
                     "conv": conv, "final": final, "weights": weights_split}
            for name, t, i in delta_schedule():
                steps[name](t, i)

            act.wait_ge(s["att4_ps"], 1)
            for i in range(H):
                act.wait_ge(mix_ready, i + 1)
                nc.scalar.copy(x_hi[:, i, :], qkv[:, i, :]).then_inc(x_hi_ready, 1)
            for c in range(NC_):
                act.wait_ge(c_scaled, c + 1)
                nc.scalar.activation(work[:, 4 + c, 0:TOK], work[:, 4 + c, 0:TOK], ACT.Silu,
                                     scale=v("conv_norm", c)).then_inc(c_act, 1)
                act.wait_ge(c_act, c + 1)
                nc.scalar.copy(x_hi[:, H + c, :], work[:, 4 + c, 0:TOK]).then_inc(x_hi_ready, 1)
            act.wait_ge(s["s4_ready"], H)
            act.dma_start(new_state, S[:]).then_inc(state_out, 16)

            for k in range(8):
                split_hi(U_OUT + 4 + k, k % 4)

            def out_tile(k):
                act.wait_ge(psum_free, U_OUT + k + 1)
                act.wait_ge(unit_done, U_FFN2)
            prepare(2, "ffn2_norm", out_tile)
            root(2)
            act.wait_ge(state_out, 16)
            ffn(U_FFN2, FT, finish_with(3, None, False))
            root(3, 0)
            for k in range(KT):
                nc.scalar.activation(h[:, k, :], h[:, k, :], ACT.Copy, scale=v("final_norm", k)).then_inc(y_gain, 1)

        @block.vector
        def _(dve):
            V = nc.vector
            count = [0]

            def link(ins):
                count[0] += 1
                ins.then_inc(link_s, 1)
                dve.wait_ge(link_s, count[0])

            def split_lo(u, slot):
                dve.wait_ge(w_hi_ready, u + 1)
                V.tensor_tensor(w_lo[:, slot], raw[:, slot % 2], w_hi[:, slot].bitcast(F32),
                                ALU.subtract).then_inc(w_lo_ready, 1)

            def rest_of_x(k, norm, at):
                dve.wait_ge(x_hi_ready, at + k + 1)
                V.scalar_tensor_tensor(x_lo[:, k, :], h[:, k, :], v(norm, k), x_hi[:, k, :].bitcast(F32),
                                       ALU.mult, ALU.subtract).then_inc(x_ready, 1)

            def rms_factor(stage):
                dve.wait_ge(root_done, stage + 1)
                V.reciprocal(rstd[:], rstd[:]).then_inc(rstd_ready, 1)
                dve.wait_ge(rstd_ready, stage + 1)

            def scaled(out, u, slot):
                dve.wait_ge(unit_done, u + 1)
                return V.tensor_tensor(two(out), both(slot), two(rstd[:]), ALU.mult)

            def hidden(ua, f, gslot, j):
                scaled(work[:, j, 0:TOK], ua, 2 * j).then_inc(psum_free, 1)
                split_lo(ua + 4, 2 * j)
                dve.wait_ge(silu_done, f + 1)
                V.tensor_tensor(work[:, 4 + j, 0:TOK], work[:, 2 + j, 0:TOK], rstd[:], ALU.mult).then_inc(sr_ready, 1)
                dve.wait_ge(sr_ready, f + 1)
                dve.wait_ge(unit_done, ua + 2)
                V.tensor_tensor(two(work[:, 6 + j, 0:TOK]), both(2 * j + 1), two(work[:, 4 + j, 0:TOK]),
                                ALU.mult).then_inc(psum_free, 1)
                split_lo(ua + 5, 2 * j + 1)
                dve.wait_ge(g_hi_ready, f + 1)
                V.tensor_tensor(g_lo[:, gslot, :], work[:, 6 + j, 0:TOK], g_hi[:, gslot, :].bitcast(F32),
                                ALU.subtract).then_inc(g_ready, 1)

            def add_to_h(u, slot, k, factor):
                dve.wait_ge(unit_done, u + 1)
                dve.wait_ge(psum_free, u - 7)
                V.scalar_tensor_tensor(two(h[:, k, :]), both(slot), factor, two(h[:, k, :]), ALU.mult,
                                       ALU.add).then_inc(psum_free, 1)

            def ffn(base, g0, norm, at):
                for p, (u0, n, g) in enumerate(parts(base, g0)):
                    with dve.Fori(0, n // 2) as i:
                        for j in range(2):
                            hidden(4 * i + (u0 + 2 * j), 2 * i + (g + j), 2 * i + j, j)
                    d0 = u0 + 2 * n
                    if p < len(PARTS) - 1:
                        with dve.Fori(0, 2) as i:
                            for j in range(4):
                                add_to_h(4 * i + (d0 + j), j, 4 * i + j, 0.5)
                                split_lo(4 * i + (d0 + j + 4), j)
                    else:
                        for k in range(KT):
                            add_to_h(d0 + k, k % 4, k, 0.5)
                            if d0 + k + 4 < U_END:
                                split_lo(d0 + k + 4, k % 4)
                            if norm is not None:
                                rest_of_x(k, norm, at)

            V.memset(mean_d[:], 1.0 / D)
            V.memset(mean_c[:], 1.0 / (NC_ * P))
            V.memset(eps[:], EPS)
            V.memset(ones[:], 1.0).then_inc(ones_set, 1)
            V.memset(c_ext[:, :, 0:CW - 1], 0.0)
            V.memset(ba[:], 0.0)
            V.memset(rtok[:], 0.0).then_inc(pads_set, 1)
            dve.wait_ge(wba_hi_ready, 1)
            V.tensor_tensor(wba_lo[:], v("w_ba", 0, KT * 2 * H).rearrange("p (k c) -> p k c", k=KT),
                            wba_hi[:].bitcast(F32), ALU.subtract).then_inc(wba_ready, 1)
            split_lo(0, 0)
            for k in range(KT):
                rest_of_x(k, "ffn1_norm", 0)
            for u in range(1, 4):
                split_lo(u, u)
            rms_factor(0)
            ffn(U_FFN1, 0, "mix_norm", 8)

            rms_factor(1)
            dve.wait_ge(pads_set, 1)
            dve.wait_ge(hist_in, 16 * (2 + NC_))
            for t, (c0, n) in enumerate(TILES):
                link(V.tensor_tensor_reduce(work[0:n, 7, 0:n], rstd[0:n, c0:c0 + n], m("ident", n), 1.0, 0.0, ALU.mult, ALU.add,
                                            rtok[0:n, t:t + 1]))
                link(V.tensor_scalar(ba[0:n, t, :], ps[0:n, 3, 0, 304 + 8 * t:312 + 8 * t], rtok[0:n, t:t + 1], None,
                                     ALU.mult))
            link(V.tensor_tensor(gate["g"][:], ba[:, :, H:2 * H], v("dt_bias", 0, H).unsqueeze(1).to_broadcast([P, NT, H]),
                                 ALU.add))
            V.scalar_tensor_tensor(gate["t1"][:], gate["g"][:], -1.0, gate["g"][:], ALU.mult, ALU.max).then_inc(ab_ready, 1)

            for c in range(NC_):
                u = U_GLU + 2 * c
                a, b = work[:, 2 * (c % 2), :], work[:, 1 + 2 * (c % 2), :]
                scaled(a[:, 0:TOK], u, u % 4).then_inc(psum_free, 1)
                split_lo(u + 4, (u + 4) % 4)
                scaled(b[:, 0:TOK], u + 1, (u + 1) % 4).then_inc(psum_free, 1)
                split_lo(u + 5, (u + 5) % 4)
                dve.wait_ge(sig_ready, c + 1)
                dve.wait_ge(psum_free, u + 2)
                V.tensor_tensor(c_ext[:, c, CW - 1:CP], a[:, 0:L], b[:, 0:L], ALU.mult)
                V.tensor_tensor(c_ext[:, c, CP:CE].rearrange("p (b w) -> p b w", b=NB)[:, :, CW - 1:CS],
                                a[:, L:TOK].rearrange("p (b w) -> p b w", b=NB),
                                b[:, L:TOK].rearrange("p (b w) -> p b w", b=NB), ALU.mult).then_inc(c_in_ready, 1)
                if c == 0:
                    dve.wait_ge(gate_act, 3)
                    link(V.scalar_tensor_tensor(gate["t2"][:], gate["g"][:], 0.0, gate["t3"][:], ALU.max, ALU.add))
                    V.scalar_tensor_tensor(gate["g"][:], gate["t2"][:], -1.0,
                                           expa[:].unsqueeze(1).to_broadcast([P, NT, H]), ALU.mult,
                                           ALU.mult).then_inc(gates_ready, 1)

            dve.wait_ge(c_in_ready, NC_)
            for i in range(2):
                last = V.memset(work[:, i, 0:SC - 1], 0.0)
            link(last)
            for i in range(NQ):
                u = U_QKV + i
                e, a = work[:, i % 2, :], work[:, 2 + i % 2, :]
                if i >= 2:
                    dve.wait_ge(lastq_saved, i - 1)
                dve.wait_ge(unit_done, u + 1)
                V.tensor_copy(e[:, QP:QE].rearrange("p (b w) -> p b w", b=NB)[:, :, 0:SC - 1],
                              hq[:, i, :].rearrange("p (b w) -> p b w", b=NB))
                V.tensor_tensor(e[:, 3:3 + HALF], ps[:, u % 4, 0, 0:HALF], rstd[:, 0:HALF], ALU.mult)
                V.tensor_tensor(e[:, 3 + HALF:QP], ps[:, u % 4, 1, 0:L - HALF], rstd[:, HALF:L], ALU.mult)
                V.tensor_tensor(e[:, QP:QE].rearrange("p (b w) -> p b w", b=NB)[:, :, SC - 1:QS],
                                ps[:, u % 4, 1, L - HALF:HALF].rearrange("p (b w) -> p b w", b=NB),
                                rstd[:, L:TOK].rearrange("p (b w) -> p b w", b=NB), ALU.mult).then_inc(psum_free, 1)
                split_lo(u + 4, (u + 4) % 4)
                dve.wait_ge(psum_free, u + 1)
                if i >= 2:
                    dve.wait_ge(q_ready, i - 1)
                link(V.tensor_scalar(a[:, 0:QO], e[:, 0:QO], v("qkv_conv_w", SC * i), None, ALU.mult))
                for j in range(1, SC):
                    ins = V.scalar_tensor_tensor(a[:, 0:QO], e[:, j:j + QO], v("qkv_conv_w", SC * i + j), a[:, 0:QO],
                                                 ALU.mult, ALU.add)
                    if j < SC - 1:
                        link(ins)
                    else:
                        ins.then_inc(q_conv, 1)

            for i in range(H):
                u = U_Z + i
                scaled(z[:, i, :], u, u % 4).then_inc(psum_free, 1)

            taps = [0]

            def conv_taps(n):
                out, c = work[:, 7, :], 3
                parts = ((out[:, 0:L], lambda j: c_ext[:, c, j:j + L]),
                         (out[:, L:TOK].rearrange("p (b w) -> p b w", b=NB),
                          lambda j: c_ext[:, c, CP:CE].rearrange("p (b w) -> p b w", b=NB)[:, :, j:j + LB]))
                for j in range(taps[0], min(taps[0] + n, CW)):
                    if j:
                        dve.wait_ge(conv3_step, j)
                    for o, x in parts:
                        if j:
                            last = V.scalar_tensor_tensor(o, x(j), v("conv_w", CW * c + j), o, ALU.mult, ALU.add)
                        else:
                            last = V.tensor_scalar(o, x(j), v("conv_w", CW * c), v("conv_b", c), ALU.mult, ALU.add)
                    last.then_inc(conv3_step, 1)
                taps[0] += n

            def gates(_, i):
                if i == 1:
                    dve.wait_ge(s["gsum_ps"], 1)
                    link(V.tensor_copy(gcs[:], bank(3)[:, 0:2 * NT * H + H * NG]))
                    nt = NT * H
                    V.tensor_tensor(f_kbg[:].rearrange("p t h -> p (t h)"), gcs[:, nt:2 * nt], gcs[:, 0:nt],
                                    ALU.subtract).then_inc(s["diffs"], 1)
                if i == 2:
                    dve.wait_ge(s["facs"], 1)
                    V.tensor_tensor(f_kbg[:], gate["beta"][:], f_cum[:], ALU.mult).then_inc(s["f_ready"], 1)

            def prep(t, i):
                c0, n = TILES[t]
                cols = slice(c0, c0 + n)
                p = t % 2
                b0, b1 = side_banks(t)
                if i == 4:
                    dve.wait_ge(s["qk_factor"], t + 1)
                    V.tensor_tensor(qkv[:, H:2 * H, cols], qkv[:, H:2 * H, cols], h4(work[:, 2 * p + 1, :], n), ALU.mult)
                    V.scalar_tensor_tensor(qkv[:, 0:H, cols], qkv[:, 0:H, cols], float(P) ** -0.5,
                                           h4(work[:, 2 * p, :], n), ALU.mult, ALU.mult).then_inc(s["qk_normed"], 1)
                    dve.wait_ge(s["gates_ps"], t + 1)
                    if t >= 2:
                        dve.wait_ge(s["es_ready"], t - 1)
                    for hd in range(H):
                        last = V.tensor_scalar(E_[p][0:n, hd, 0:n], heads(b0, n)[0:n, hd, :],
                                               gcs[0:n, H * t + hd:H * t + hd + 1], 0.0, ALU.subtract, ALU.min)
                    last.then_inc(s["d_diff"], 1)
                if i == 5:
                    V.tensor_tensor(ES[p][0:n, :, 0:n], heads(b1, n)[0:n], over_heads(tile_mask("strict", t), n),
                                    ALU.mult).then_inc(s["bs_ready"], 1)
                if i == 8:
                    dve.wait_ge(s["gram_ps"], t + 1)
                    dve.wait_ge(s["em_ready"], t + 1)
                    if t == 4:
                        dve.wait_ge(s["o_ps"], 1)
                    V.tensor_tensor(ATT[t % 4][0:n, :, 0:n], heads(b1, n)[0:n], E_[p][0:n, :, 0:n],
                                    ALU.mult).then_inc(s["att_ready"], 1)

            def tok(t, i):
                n = TILES[t][1]
                p = t % 2
                if i == 0:
                    return
                dve.wait_ge(s["tok_ps"], t + 1)
                if t == 0:
                    dve.wait_ge(s["f_ready"], 1)
                if t >= 2:
                    dve.wait_ge(s["wt_ps"], t - 1)
                    dve.wait_ge(s["s_ps"], t - 1)
                V.tensor_tensor(U_[p][0:n], heads(5, P)[0:n], over_cols(gate["beta"][0:n, t, :], P), ALU.mult)
                V.tensor_tensor(KBG[p][0:n], heads(4, P)[0:n], over_cols(f_kbg[0:n, t, :], P), ALU.mult)
                V.tensor_tensor(KG[p][0:n], heads(4, P)[0:n], over_cols(f_rest[0:n, t, :], P),
                                ALU.mult).then_inc(s["tok_ready"], 1)

            def start(t, i):
                n = TILES[t][1]
                p, a, b, ly, lx = chain_at(t)
                if i:
                    return
                dve.wait_ge(s["kk_ps"], t + 1)
                dve.wait_ge(s["es_ready"], t + 1)
                V.tensor_tensor(AT[p][0:n, :, 0:n], heads(a, n)[0:n], ES[p][0:n, :, 0:n], ALU.mult).then_inc(s["at_ready"], 1)
                dve.wait_ge(s["at_ready"], t + 1)
                link(V.tensor_tensor(T1[p][0:n, :, 0:n], AT[p][0:n, :, 0:n], over_heads(m("levels", n, 0), n), ALU.mult))
                if t == 2 or t == 3:
                    dve.wait_ge(s["u_ps"], t - 1)
                if t == 4:
                    dve.wait_ge(s["u_ps"], 3)
                V.tensor_tensor(Y_[p][0:n, :, 0:n], over_heads(m("ident", n), n), T1[p][0:n, :, 0:n],
                                ALU.subtract).then_inc(s["y_ready"][p], 1)

            def level(t, i):
                l, i = i // 2, i % 2
                n = TILES[t][1]
                p, a, b, ly, lx = chain_at(t)
                if i == 1:
                    dve.wait_ge(s["p_ps"][p], lx + l)
                    dve.wait_ge(s["x_inv"][p], lx + l)
                    if l < LEVELS[t] - 1:
                        V.tensor_tensor(X_[p][0:n, :, 0:n], X_[p][0:n, :, 0:n], heads(b, n)[0:n],
                                        ALU.subtract).then_inc(s["x_inv"][p], 1)
                    dve.wait_ge(s["y_ready"][p], ly + l)
                    V.tensor_tensor(Y_[p][0:n, :, 0:n], Y_[p][0:n, :, 0:n], heads(a, n)[0:n],
                                    ALU.subtract).then_inc(s["y_ready"][p], 1)
                    conv_taps(2 if t < 2 else 1)

            def end(t, i):
                n = TILES[t][1]
                p, a, b, ly, lx = chain_at(t)
                if t < 4:
                    dve.wait_ge(s["u_ps"], t + 1)
                    V.tensor_copy(U_[p][0:n], heads(b, P)[0:n]).then_inc(s["u_ready"], 1)

            def scan(t, i):
                c0, n = TILES[t]
                cols = slice(c0, c0 + n)
                p = t % 2
                if i == 1:
                    dve.wait_ge(s["u_ready"], t + 1)
                    if t == 0:
                        V.tensor_copy(VN[:], U_[p][:]).then_inc(s["vn_ready"], 1)
                    else:
                        dve.wait_ge(s["vn_ps"], t)
                        dve.wait_ge(s["s_ps"], t)
                        V.tensor_tensor(VN[:], U_[p][:], heads(6, P), ALU.add).then_inc(s["vn_ready"], 1)
                if i == 3:
                    dve.wait_ge(s["s_ps"], t + 1)
                    if t == 0:
                        V.tensor_copy(S[:, :, 0, :], heads(6, P)).then_inc(s["s_ready"], 1)
                    else:
                        dve.wait_ge(s["s_ready"], t)
                        for hd in range(H):
                            last = V.scalar_tensor_tensor(S[:, hd, 0, :], S[:, hd, 0, :], f_all[:, t, hd:hd + 1],
                                                          heads(6, P)[:, hd, :], ALU.mult, ALU.add)
                        last.then_inc(s["s_ready"], 1)
                if i == 6:
                    dve.wait_ge(s["o_factor"], t + 1)
                    V.tensor_tensor(qkv[:, 0:H, cols], qkv[:, 0:H, cols], h4(work[:, 3, :], n),
                                    ALU.mult).then_inc(s["o_ready"], 1)

            def conv(c, _):
                if c == 0:
                    conv_taps(CW)
                if c == 4:
                    dve.wait_ge(c_factor, 2)
                    for i in range(NC_):
                        V.tensor_tensor(work[:, 4 + i, 0:TOK], work[:, 4 + i, 0:TOK], ssum[:], ALU.mult).then_inc(c_scaled, 1)

            def mixed(cols):
                for i in range(H):
                    V.scalar_tensor_tensor(qkv[:, i, cols], qkv[:, i, cols], v("o_norm"), z[:, i, cols], ALU.mult,
                                           ALU.mult).then_inc(mix_ready, 1)

            def final(_, i):
                t, (c0, n) = 4, TILES[4]
                cols = slice(c0, c0 + n)
                if i == 1:
                    dve.wait_ge(s["vn4_ps"], 1)
                    V.tensor_copy(VN[0:n], heads(2, P)[0:n]).then_inc(s["vn_ready"], 1)
                if i == 2:
                    dve.wait_ge(s["os_ready"], 1)
                    dve.wait_ge(s["att4_ps"], 1)
                    V.tensor_tensor(qkv[:, 0:H, cols], heads(3, n), h4(work[:, 2, :], n), ALU.add).then_inc(s["o_evac"], 1)
                if i == 5:
                    dve.wait_ge(s["o_factor"], t + 1)
                    V.tensor_tensor(qkv[:, 0:H, cols], qkv[:, 0:H, cols], h4(work[:, 3, :], n),
                                    ALU.mult).then_inc(s["o_ready"], 1)
                    dve.wait_ge(z_ready, H)
                    dve.wait_ge(s["o_ready"], NT)
                    mixed(slice(0, TOK))
                if 3 <= i < 3 + H:
                    hd = i - 3
                    dve.wait_ge(s["s_scaled"], hd + 1)
                    dve.wait_ge(s["s4_ps"], hd + 1)
                    V.tensor_tensor(S[:, hd, 0:8, :], S[:, hd, 0:8, :],
                                    ps[:, 2].rearrange("p a (g c) -> p (a g) c", g=4), ALU.add)
                    V.tensor_tensor(S[:, hd, 8, :], S[:, hd, 8, :], bank(6)[:, 0:P], ALU.add).then_inc(s["s4_ready"], 1)

            def weights_split(j, _):
                if j == 0:
                    dve.wait_ge(s["wt_ps"], NT)
                split_lo(U_OUT + j, j)

            steps = {"gates": gates, "prep": prep, "tok": tok, "start": start, "level": level, "end": end, "scan": scan,
                     "conv": conv, "final": final, "weights": weights_split}
            for name, t, i in delta_schedule():
                steps[name](t, i)

            dve.wait_ge(s["s4_ps"], H)
            for i in range(2 * H):
                dve.wait_ge(x_hi_ready, 16 + i + 1)
                src = qkv[:, i, :] if i < H else work[:, i, 0:TOK]
                V.tensor_tensor(x_lo[:, i, :], src, x_hi[:, i, :].bitcast(F32), ALU.subtract).then_inc(x_ready, 1)

            for k in range(KT):
                add_to_h(U_OUT + k, k % 4, k, 1.0)
                split_lo(U_OUT + k + 4, k % 4)
            for k in range(KT):
                rest_of_x(k, "ffn2_norm", 24)
            rms_factor(2)
            ffn(U_FFN2, FT, None, 0)
            rms_factor(3)
            for k in range(KT):
                dve.wait_ge(y_gain, k + 1)
                V.tensor_tensor(h[:, k, :], h[:, k, :], rstd[:], ALU.mult).then_inc(y_ready, 1)

        @block.gpsimd
        def _(pool):
            G = nc.gpsimd
            count = [0]

            def link(ins):
                count[0] += 1
                ins.then_inc(pool_s, 1)
                pool.wait_ge(pool_s, count[0])

            def sum_squares(stage):
                for k in range(KT):
                    pool.wait_ge(sq_ready, 8 * stage + k + 1)
                    if k == 0:
                        if stage:
                            pool.wait_ge(stats_done, stage)
                        G.tensor_copy(ssum[:], sq[:, 0, :]).then_inc(ssum_step, 1)
                    else:
                        pool.wait_ge(ssum_step, 8 * stage + k)
                        G.tensor_tensor(ssum[:], ssum[:], sq[:, k % 2, :], ALU.add).then_inc(ssum_step, 1)

            sum_squares(0)
            sum_squares(1)

            pool.wait_ge(vec_in, 16)
            pool.wait_ge(hist_in, 16 * (2 + NC_))
            pool.wait_ge(pads_set, 1)
            pool.wait_ge(stats_done, 2)
            for c in range(3):
                pool.wait_ge(c_in_ready, c + 1)
                out = work[:, 4 + c, :]
                G.tensor_scalar(out[:, 0:L], c_ext[:, c, 0:L], v("conv_w", CW * c), v("conv_b", c), ALU.mult, ALU.add)
                link(G.tensor_scalar(out[:, L:TOK].rearrange("p (b w) -> p b w", b=NB),
                                     c_ext[:, c, CP:CE].rearrange("p (b w) -> p b w", b=NB)[:, :, 0:LB],
                                     v("conv_w", CW * c), v("conv_b", c), ALU.mult, ALU.add))
                for j in range(1, CW):
                    t = (CW - 1) * c + j - 1
                    pool.wait_ge(tap_ready, t + 1)
                    if j > 1:
                        pool.wait_ge(tap_added, t)
                    last = G.tensor_tensor(out[:, 0:TOK], out[:, 0:TOK], tap_place(t)[:, 0:TOK], ALU.add)
                    last.then_inc(tap_added, 1)

            def gates(_, i):
                if i == 0:
                    n = TILES[4][1]
                    pool.wait_ge(gates_ready, 1)
                    pool.wait_ge(psum_free, U_OUT)
                    G.tensor_tensor(gx[0:n], over_cols(gate["g"][0:n, 4, :], NG), over_heads(mask[0:n, MASK["group"]], n),
                                    ALU.mult).then_inc(s["gx_ready"], 1)

            def prep(t, i):
                c0, n = TILES[t]
                p = t % 2
                if i == 0:
                    if t >= 2:
                        pool.wait_ge(s["gates_ps"], t - 1)
                    G.tensor_copy(G_B[p][0:n], over_cols(gate["g"][0:n, t, :], P))
                    G.tensor_copy(B_B[p][0:n], over_cols(gate["beta"][0:n, t, :], P)).then_inc(s["gates_b"], 1)
                if i == 6:
                    pool.wait_ge(s["e_ready"], t + 1)
                    G.tensor_tensor(E_[p][0:n, :, 0:n], E_[p][0:n, :, 0:n], over_heads(tile_mask("incl", t), n),
                                    ALU.mult).then_inc(s["em_ready"], 1)
                    pool.wait_ge(s["em_ready"], t + 1)
                    pool.wait_ge(s["bs_ready"], t + 1)
                    G.tensor_tensor(ES[p][0:n, :, 0:n], ES[p][0:n, :, 0:n], E_[p][0:n, :, 0:n],
                                    ALU.mult).then_inc(s["es_ready"], 1)
                if i == 7:
                    e = EG[t % 4]
                    pool.wait_ge(s["eg_ready"], t + 1)
                    pool.wait_ge(s["qk_normed"], t + 1)
                    G.tensor_tensor(e[:, :, 0:n], e[:, :, 0:n], qkv[:, 0:H, c0:c0 + n], ALU.mult).then_inc(s["qg_ready"], 1)

            def tok(t, i):
                pass

            def blocks(t, l):
                n = TILES[t][1]
                p = t % 2
                G.tensor_tensor(BM[p][0:n, :, 0:n], AT[p][0:n, :, 0:n], over_heads(m("levels", n, l), n),
                                ALU.mult).then_inc(s["b_ready"][p], 1)

            def start(t, i):
                if i == 0:
                    pool.wait_ge(s["at_ready"], t + 1)
                    blocks(t, 1)

            def level(t, i):
                l, i = i // 2, i % 2
                p, a, b, ly, lx = chain_at(t)
                if i == 1 and l + 1 < LEVELS[t]:
                    pool.wait_ge(s["t1_ps"][p], lx + l)
                    blocks(t, l + 1)

            def end(t, i):
                pass

            def scan(t, i):
                pass

            def conv(c, _):
                pass

            def final(_, i):
                n = TILES[4][1]
                if i == 0:
                    pool.wait_ge(s["os_ps"], 1)
                    for hd in range(H):
                        G.tensor_tensor(S[:, hd], S[:, hd], over_cols(f_group[:, NG * hd:NG * (hd + 1)], P),
                                        ALU.mult).then_inc(s["s_scaled"], 1)
                if 3 <= i < 3 + H:
                    hd = i - 3
                    pool.wait_ge(s["vn_ready"], 5)
                    if hd:
                        pool.wait_ge(s["s4_ps"], hd)
                    G.tensor_tensor(VX3, VN[0:n, hd, :].unsqueeze(1).to_broadcast([n, NG, P]),
                                    mask[0:n, MASK["group"]].unsqueeze(2).to_broadcast([n, NG, P]),
                                    ALU.mult).then_inc(s["vx_ready"], 1)

            def weights_split(j, _):
                pass

            steps = {"gates": gates, "prep": prep, "tok": tok, "start": start, "level": level, "end": end, "scan": scan,
                     "conv": conv, "final": final, "weights": weights_split}
            for name, t, i in delta_schedule():
                steps[name](t, i)
            sum_squares(2)
            sum_squares(3)


_OUTS = {"y_t": (P, KT, TOK), "new_state": (P, H, NG, P), "last_q": (P, NQ, 27), "last_c": (P, NC_, 270)}


def feature_tiles(a):
    return np.ascontiguousarray(a.T.reshape(-1, P, a.shape[0]).transpose(1, 0, 2))


def unit_list(i):
    w_in = i["w_in"][0]
    qkv_z = NQ * P + H * P
    glu = qkv_z + 2 * H
    units = np.zeros((U_END, P, KT, P), np.float32)
    at = [0]

    def add(w, r0, rows, c0):
        block = w[r0 * P:(r0 + rows) * P, c0:c0 + P]
        units[at[0], :, 0:rows, :] = block.reshape(rows, P, P).transpose(1, 0, 2)
        at[0] += 1

    def ffn(w1, w3, w2):
        g = 0
        for n in PARTS:
            for f in range(g, g + n):
                add(w1, 0, KT, f * P)
                add(w3, 0, KT, f * P)
            for k in range(KT):
                add(w2, g, n, k * P)
            g += n

    ffn(i["ffn1_w1"][0], i["ffn1_w3"][0], i["ffn1_w2"][0])
    for c in range(NC_):
        add(w_in, 0, KT, glu + c * P)
        add(w_in, 0, KT, glu + (NC_ + c) * P)
    for c in range(NQ + H):
        add(w_in, 0, KT, c * P)
    for k in range(KT):
        add(i["w_out"][0], 0, KT, k * P)
    ffn(i["ffn2_w1"][0], i["ffn2_w3"][0], i["ffn2_w2"][0])
    assert at[0] == U_END
    return units


def kernel(**inputs):
    import concourse.bacc as bacc
    from concourse.bass_utils import run_bass_kernel_spmd

    i = {k: np.asarray(a) for k, a in inputs.items()}
    x = np.concatenate([i["meta_tokens"], i["x_prompt"][0], i["x_sample"].reshape(NB * LB, D)])
    vecs = np.zeros((P, NV), np.float32)
    for name in ("ffn1_norm", "mix_norm", "ffn2_norm", "conv_b", "conv_norm", "o_norm"):
        vecs[:, VEC[name]] = i[name][0].reshape(-1, P).T
    vecs[:, VEC["final_norm"]] = i["final_norm"].reshape(-1, P).T
    for name, w in (("qkv_conv_w", SC), ("conv_w", CW)):
        vecs[:, VEC[name]] = i[name][0].T.reshape(-1, P, w).transpose(1, 0, 2).reshape(P, -1)
    vecs[:, VEC["dt_bias"]] = i["dt_bias"][0]
    vecs[:, VEC["a_log"]] = i["a_log"][0]
    ba = i["w_in"][0][:, (NQ + H) * P:(NQ + H) * P + 2 * H]
    vecs[:, VEC["w_ba"]] = ba.reshape(KT, P, 2 * H).transpose(1, 0, 2).reshape(P, -1)
    arrays = {
        "weights": unit_list(i),
        "x_t": feature_tiles(x),
        "vecs": vecs,
        "masks": shape_masks(),
        "hist_q": feature_tiles(i["state_qkv_conv"][0].reshape(NB * (SC - 1), NQ * P)),
        "hist_c": np.ascontiguousarray(
            feature_tiles(i["state_conv"][0].reshape(NB * (CW - 1), NC_ * P)).reshape(P, NC_, NB, CW - 1)),
        "states": np.ascontiguousarray(i["state_delta"][0].transpose(2, 1, 0, 3)),
    }
    nc = bacc.Bacc("TRN2", target_bir_lowering=False, num_devices=1)
    args = [nc.dram_tensor(n, a.shape, mybir.dt.from_np(a.dtype), kind="ExternalInput").ap() for n, a in arrays.items()]
    args += [nc.dram_tensor(n, shape, F32, kind="ExternalOutput").ap() for n, shape in _OUTS.items()]
    build(nc, *args)
    r = run_bass_kernel_spmd(nc, [arrays], core_ids=[0]).results[0]
    y = r["y_t"].transpose(2, 1, 0).reshape(TOK, D)
    st = r["new_state"].transpose(1, 2, 0, 3)
    lq = r["last_q"].transpose(2, 1, 0).reshape(27, NQ * P)
    lc = r["last_c"].transpose(2, 1, 0).reshape(270, NC_ * P)
    c = np.ascontiguousarray
    return (c(y[N_META:L][None]), c(y[L:].reshape(NB, LB, D)), c(st[:, 0][None, None]),
            c(lq[0:3][None, None]), c(lc[0:30][None, None]), c(st[:, 1:].transpose(1, 0, 2, 3)[None]),
            c(lq[3:].reshape(1, NB, SC - 1, NQ * P)), c(lc[30:].reshape(1, NB, CW - 1, NC_ * P)))
```

```python
from contextlib import ExitStack

import numpy as np
import concourse.bass as bass
from concourse import mybir

F32 = mybir.dt.float32
F32R = mybir.dt.float32r
ACT = mybir.ActivationFunctionType
ALU = mybir.AluOpType

P = 128
D = 1024
KT = D // P
SEQ_LEN, N_META = 512, 16
L = SEQ_LEN + N_META
NB, LB = 8, 8
TOK = L + NB * LB
HALF = TOK // 2
FT = 2816 // P
PARTS = [8, 8, 6]
H = 4
NQ = 3 * H
NC_ = 4
SC, CW = 4, 31
POOL_TAPS = 3 * (CW - 1)
EARLY_TAPS = 8 * 3 + 3 * NQ + H
EPS = 1e-6

U_FFN1 = 0
FFN_UNITS = 2 * FT + 8 * len(PARTS)
U_GLU = U_FFN1 + FFN_UNITS
U_QKV = U_GLU + 2 * NC_
U_Z = U_QKV + NQ
U_OUT = U_Z + H
U_FFN2 = U_OUT + 8
U_END = U_FFN2 + FFN_UNITS
assert all(u % 4 == 0 for u in (U_FFN1, U_GLU, U_QKV, U_Z, U_OUT, U_FFN2, U_END))

QP = SC - 1 + L
QS = SC - 1 + LB
QE = QP + NB * QS
QO = QE - (SC - 1)
CP = CW - 1 + L
CS = CW - 1 + LB
CE = CP + NB * CS

TILES = [(128 * t, 128) for t in range(4)] + [(512, 80)]
NT = len(TILES)
NG = 1 + NB
GROUPS = [(0, 16)] + [(16 + LB * b, LB) for b in range(NB)]
LEVELS = [7, 7, 7, 7, 4]
LVO = [0, 0, 7, 7, 14]


def merge(a, b):
    if len(b) > len(a):
        a, b = b, a
    out, taken = [], 0
    for i, x in enumerate(a):
        out.append(x)
        while taken * len(a) < (i + 1) * len(b):
            out.append(b[taken])
            taken += 1
    return out


def delta_schedule():
    prep = [[("prep", t, i) for i in range(9)] for t in range(NT)]
    tok = [[("tok", t, i) for i in range(2)] for t in range(NT)]
    scan = [[("scan", t, i) for i in range(7)] for t in range(4)]
    chain = [[("start", t, i) for i in range(2)] + [("level", t, 2 * l + i) for l in range(1, LEVELS[t]) for i in range(2)]
             + [("end", t, 0)] for t in range(NT)]
    final = [("final", 4, i) for i in range(8)]
    taps = [("taps", 0, i) for i in range((POOL_TAPS - EARLY_TAPS + 1) // 2)]
    out = [("gates", 0, i) for i in range(3)] + merge(merge(prep[0], prep[1]), taps[0:4])
    lag1, lag3 = 10, 10
    out += merge(merge(merge(chain[0], chain[1][:lag1]), tok[0] + tok[1] + prep[2]), taps[4:])
    out += merge(merge(chain[1][lag1:], chain[2][:4]), prep[3])
    out += merge(merge(chain[2][4:], chain[3][:lag3]), merge(scan[0] + scan[1], prep[4]) + tok[2] + tok[3])
    out += merge(chain[3][lag3:], merge(chain[4][:4], scan[2]))
    out += merge(merge(tok[4] + scan[3], chain[4][4:]),
                 [("samples", hd, 0) for hd in range(H)] + [("conv", c, 0) for c in range(NC_)])
    out += final[0:2] + [("weights", 0, 0)] + final[2:4] + [("conv", 4, 0)] + final[4:5] + [("weights", 1, 0)] + final[5:]
    return out

VEC = {}
_at = 0
for _n, _w in (("ffn1_norm", 8), ("mix_norm", 8), ("ffn2_norm", 8), ("final_norm", 8), ("qkv_conv_w", NQ * SC),
               ("conv_w", NC_ * CW), ("conv_b", NC_), ("conv_norm", NC_), ("o_norm", 1), ("dt_bias", H),
               ("a_log", H), ("w_ba", KT * 2 * H)):
    VEC[_n] = slice(_at, _at + _w)
    _at += _w
NV = _at

MASK = {}
_at = 0
for _n, _w in (("ident", P), ("incl", P), ("strict", P), ("incl4", P), ("strict4", P), ("same4", P),
               ("levels", 7 * P), ("group", NG)):
    MASK[_n] = slice(_at, _at + _w)
    _at += _w
NM = _at


def shape_masks():
    m = np.zeros((P, NM), np.float32)
    s, c = np.arange(P)[:, None], np.arange(P)[None, :]
    seq = np.where(np.arange(P) < 16, 0, 1 + (np.arange(P) - 16) // LB)
    seq[80:] = 99
    same = (seq[:, None] == seq[None, :]) & (s < 80) & (c < 80)
    m[:, MASK["ident"]] = s == c
    m[:, MASK["incl"]] = s <= c
    m[:, MASK["strict"]] = s < c
    m[:, MASK["incl4"]] = (s <= c) & same
    m[:, MASK["strict4"]] = (s < c) & same
    m[:, MASK["same4"]] = same
    for l in range(7):
        w = 1 << l
        a = MASK["levels"].start + l * P
        m[:, a:a + P] = (s // (2 * w) == c // (2 * w)) & (s % (2 * w) < w) & (c % (2 * w) >= w)
    m[:, MASK["group"]] = seq[:, None] == np.arange(NG)[None, :]
    return m


def build(nc, weights, x_t, vecs, masks, hist_q, hist_c, states, y_t, new_state, last_q, last_c):
    ctx = ExitStack()
    with ctx:
        def sb(name, shape, dt=F32, where=ctx):
            return where.enter_context(nc.sbuf_tensor(name, shape, dt))

        def sem(name):
            return ctx.enter_context(nc.semaphore(name))

        h = sb("h", [P, KT, TOK])
        raw = sb("raw", [P, 2, KT, P])
        rstd = sb("rstd", [P, TOK])
        ssum = sb("ssum", [P, TOK])
        sq = sb("sq", [P, 2, TOK])
        work = sb("work", [P, 8, QE])
        vec = sb("vec", [P, NV])
        mask = sb("mask", [P, NM])
        mean_d = sb("mean_d", [P, P])
        mean_c = sb("mean_c", [P, P])
        ones = sb("ones", [P, P])
        eps = sb("eps", [P, 1])
        c_ext = sb("c_ext", [P, NC_, CE])
        hq = sb("hq", [P, NQ, NB * (SC - 1)])
        lastq = sb("lastq", [P, NQ, (1 + NB) * (SC - 1)])
        wba_hi = sb("wba_hi", [P, KT, 2 * H], F32R)
        wba_lo = sb("wba_lo", [P, KT, 2 * H], F32R)
        gate = {n: sb("gate_" + n, [P, NT, H]) for n in ("beta", "g", "t1", "t2", "t3")}
        ba = sb("ba", [P, NT, 2 * H])
        expa = sb("expa", [P, H])
        gcs = sb("gcs", [P, 2 * NT * H + H * NG])
        f_cum, f_rest, f_all, f_kbg = [sb("f_" + n, [P, NT, H]) for n in ("cum", "rest", "all", "kbg")]
        f_group = sb("f_group", [P, H * NG])
        gx = sb("gx", [P, H, NG])
        zone = ExitStack()
        w_hi = sb("w_hi", [P, 4, KT, P], F32R, zone)
        w_lo = sb("w_lo", [P, 4, KT, P], F32R, zone)
        x_hi = sb("x_hi", [P, KT, TOK], F32R, zone)
        x_lo = sb("x_lo", [P, KT, TOK], F32R, zone)
        zone.close()
        zone = ExitStack()

        def ring(name, n):
            return [sb(f"d_{name}{i}", [P, H, P], F32, zone) for i in range(n)]

        G_B, B_B, E_, ES, AT, BM, X_, T1 = [ring(n, 2) for n in ("g_b", "beta_b", "decay", "decay_strict", "a_t", "b",
                                                                  "inv", "t1")]
        Y_ = ring("inv_t", 2)
        ATT = ring("att_t", 4)
        EG = sb("d_egrow", [P, 4, H, P], F32, zone)
        NWT, U_, KBG = ring("neg_w_t", 2), ring("u", 2), ring("kbg", 2)
        KG = ring("kg", 2)
        VN = ring("v_new", 1)[0]
        ctx.enter_context(zone)
        zone2 = ExitStack()
        g_hi = sb("g_hi", [P, 8, TOK], F32R, zone2)
        g_lo = sb("g_lo", [P, 8, TOK], F32R, zone2)
        zone2.close()
        qkv = sb("qkv", [P, NQ, TOK], F32, zone2)
        S = sb("S", [P, H, NG, P], F32, zone2)
        z = sb("z", [P, H, TOK], F32, zone2)
        ctx.enter_context(zone2)

        ps = ctx.enter_context(nc.psum_tensor("ps", [P, 4, 2, 512], F32))

        def bank(j):
            return ps[:, j // 2, j % 2, :]

        def heads(j, n):
            return bank(j).rearrange("p (h c) -> p h c", h=H)[:, :, 0:n]

        def v(name, i=0, n=1):
            return vec[:, VEC[name].start + i:VEC[name].start + i + n]

        def m(name, n=P, i=0):
            a = MASK[name].start + i * P
            return mask[0:n, a:a + n]

        def chain_at(t):
            p = t % 2
            return p, 2 * p, 2 * p + 1, LVO[t], LVO[t] - t // 2

        def side_banks(t):
            return (6, 7) if t == 1 else (4, 5)

        def tile_mask(name, t, i=0, cols=None):
            n = TILES[t][1]
            a = MASK[name + "4" if t == 4 and name in ("incl", "strict") else name].start + i * P
            return mask[0:n, a:a + (cols or n)]

        def h4(ap, n):
            return ap[:, 0:H * n].rearrange("p (h c) -> p h c", h=H)

        n4 = TILES[4][1]
        VX = [work[0:n4, 0:2, :].rearrange("p a b -> p (a b)")[:, 0:NG * P],
              sq[0:n4].rearrange("p a b -> p (a b)")[:, 0:NG * P]]
        S4_BANKS = [(4, 5, 6), (2, 3, 7)]

        def over_heads(ap, n):
            return ap.unsqueeze(1).to_broadcast([n, H, ap.shape[1]])

        def over_cols(ap, c):
            return ap.unsqueeze(2).to_broadcast([ap.shape[0], ap.shape[1], c])

        raw_in = [sem(f"raw_in{i}") for i in range(2)]
        w_hi_ready = sem("w_hi_ready")
        w_lo_ready = sem("w_lo_ready")
        unit_done = sem("unit_done")
        psum_free = sem("psum_free")
        x_in = sem("x_in"); vec_in = sem("vec_in"); hist_in = sem("hist_in"); state_in = sem("state_in")
        ones_set = sem("ones_set")
        sq_ready = sem("sq_ready"); ssum_step = sem("ssum_step"); stats_done = sem("stats_done")
        rstd_ready = sem("rstd_ready")
        x_hi_ready = sem("x_hi_ready"); x_ready = sem("x_ready")
        silu_done = sem("silu_done"); sr_ready = sem("sr_ready")
        g_hi_ready = sem("g_hi_ready"); g_ready = sem("g_ready")
        wba_hi_ready = sem("wba_hi_ready"); wba_ready = sem("wba_ready")
        pads_set = sem("pads_set")
        link_s = sem("dve_link")
        pool_s = sem("pool_link")
        ab_ready = sem("ab_ready"); ba_ps = sem("ba_ps"); ba_scaled = sem("ba_scaled"); ba_tok_ps = sem("ba_tok_ps"); gate_act = sem("gate_act"); gates_ready = sem("gates_ready")
        gate_in = sem("gate_in"); sig_ready = sem("sig_ready"); c_in_ready = sem("c_in_ready")
        tap_ready = sem("tap_ready"); tap_added = sem("tap_added"); conv3_step = sem("conv3_step")
        lastq_saved = sem("lastq_saved"); q_conv = sem("q_conv"); q_ready = sem("q_ready")
        names = ("qk_sq norms_ps qk_log qk_factor o_log o_factor qk_normed gates_b gates_ps d_diff e_ready eg_ready "
                 "bs_ready em_ready es_ready qg_ready diffs facs f_ready tok_ps tok_ready gram_ps kk_ps at_ready "
                 "att_ready x1_ps wt_ps u_ps nwt_ready u_ready vn_ps vn_ready o_ps o_evac s_ps s_ready osq_ready on_ps "
                 "o_ready vnt_ps vnt_ready os_ps os_ready vn4_ps att4_ps gx_ready gsum_ps ek_ready ss_ps rhs_ready neg_vn_ps vx_ready s4_ps s4_ready "
                 "s_scaled").split()
        s = {n: sem(n) for n in names}
        for n in ("b_ready", "y_ready", "x_inv", "t1_ps", "t1_ready", "p_ps"):
            s[n] = [sem(f"{n}{i}") for i in range(2)]
        z_ready = sem("z_ready"); mix_ready = sem("mix_ready")
        csq_ready = sem("csq_ready"); cn_ps = sem("cn_ps"); c_factor = sem("c_factor"); log_done = sem("log_done"); root_done = sem("root_done"); c_scaled = sem("c_scaled"); c_act = sem("c_act")
        y_ready = sem("y_out_ready"); y_gain = sem("y_gain")
        out_s = sem("out_s"); state_out = sem("state_out")

        block = ctx.enter_context(nc.Block())

        def parts(base, g0):
            u, g = base, g0
            for n in PARTS:
                yield u, n, g
                u += 2 * n + 8
                g += n

        @block.sync
        def _(sp):
            sp.dma_start(vec[:], vecs).then_inc(vec_in, 16)
            sp.dma_start(h[:, 0:4], x_t[:, 0:4]).then_inc(x_in, 16)
            sp.dma_start(raw[:, 0], weights[0]).then_inc(raw_in[0], 16)
            sp.wait_ge(x_in, 16)
            sp.dma_start(h[:, 4:8], x_t[:, 4:8]).then_inc(x_in, 16)
            sp.dma_start(raw[:, 1], weights[1]).then_inc(raw_in[1], 16)
            sp.dma_start(mask[:], masks).then_inc(hist_in, 16)
            sp.dma_start(hq[:], hist_q).then_inc(hist_in, 16)
            for c in range(NC_):
                sp.dma_start(c_ext[:, c, CP:CE].rearrange("p (b w) -> p b w", b=NB)[:, :, 0:CW - 1],
                             hist_c[:, c]).then_inc(hist_in, 16)

            def load_pair(u):
                for j in range(2):
                    sp.wait_ge(w_lo_ready, u + j - 1)
                    sp.dma_start(raw[:, j], weights[u + j]).then_inc(raw_in[j], 16)

            with sp.Fori(0, (U_QKV + 4 - 2) // 2) as i:
                load_pair(2 * i + 2)
            sp.wait_ge(unit_done, U_GLU)
            sp.dma_start(S[:, :, 1:NG, :], states).then_inc(state_in, 16)
            with sp.Fori(0, (U_END - U_QKV - 4) // 2) as i:
                load_pair(2 * i + U_QKV + 4)
            sp.wait_ge(lastq_saved, NQ)
            sp.dma_start(last_q, lastq[:]).then_inc(out_s, 16)
            sp.wait_ge(c_in_ready, NC_)
            for c in range(NC_):
                sp.dma_start(last_c[:, c, 0:30], c_ext[:, c, L:L + 30]).then_inc(out_s, 16)
                sp.dma_start(last_c[:, c, 30:270].rearrange("p (b w) -> p b w", b=NB),
                             c_ext[:, c, CP:CE].rearrange("p (b w) -> p b w", b=NB)[:, :, LB:CS]).then_inc(out_s, 16)
            for k in range(KT):
                sp.wait_ge(y_ready, k + 1)
                sp.dma_start(y_t[:, k], h[:, k]).then_inc(out_s, 16)
            sp.wait_ge(out_s, 16 * (1 + 2 * NC_ + KT))

        @block.tensor
        def _(pe):
            def product(u, slot, kt, xh, xl, k_sem=None, k_base=0):
                pe.wait_ge(w_lo_ready, u + 1)
                for k in range(kt):
                    if k_sem is not None:
                        pe.wait_ge(k_sem, k_base + k + 1)
                    for n, (w, x) in enumerate(((w_hi, xh), (w_hi, xl), (w_lo, xh))):
                        for half in range(2):
                            last = nc.tensor.matmul(ps[:, slot, half, 0:HALF], w[:, slot, k, :],
                                                    x[:, k, half * HALF:(half + 1) * HALF],
                                                    start=(k == 0 and n == 0), stop=(k == kt - 1 and n == 2))
                last.then_inc(unit_done, 1)

            def mean_square(stage, u):
                pe.wait_ge(ssum_step, 8 * (stage + 1))
                if u:
                    pe.wait_ge(psum_free, u)
                for half in range(2):
                    last = nc.tensor.matmul(ps[:, 3, half, 0:HALF], mean_d[:], ssum[:, half * HALF:(half + 1) * HALF],
                                            start=True, stop=True)
                return last

            def ffn(stage, base, g0, k_base):
                for p, (u0, n, g) in enumerate(parts(base, g0)):
                    if p == 0:
                        for j in range(4):
                            u = u0 + j
                            if j == 3:
                                pe.wait_ge(rstd_ready, stage + 1)
                            elif u >= 4:
                                pe.wait_ge(psum_free, u - 3)
                            product(u, j, KT, x_hi, x_lo, x_ready if j == 0 else None, k_base)
                            if j == 1:
                                mean_square(stage, u0).then_inc(stats_done, 1)
                    with pe.Fori(1 if p == 0 else 0, n // 2) as i:
                        for j in range(4):
                            pe.wait_ge(psum_free, 4 * i + (u0 + j - 3))
                            product(4 * i + (u0 + j), j, KT, x_hi, x_lo)
                    d0 = u0 + 2 * n
                    with pe.Fori(0, 2) as i:
                        for j in range(4):
                            pe.wait_ge(psum_free, 4 * i + (d0 + j - 3))
                            product(4 * i + (d0 + j), j, n, g_hi, g_lo, g_ready if j == 0 else None, g)

            pe.wait_ge(ones_set, 1)
            ffn(0, U_FFN1, 0, 0)

            for j in range(4):
                u = U_GLU + j
                if j == 3:
                    pe.wait_ge(wba_ready, 1)
                    pe.wait_ge(rstd_ready, 2)
                    for k in range(KT):
                        for r, (w, x) in enumerate(((wba_hi, x_hi), (wba_hi, x_lo), (wba_lo, x_hi))):
                            for half in range(2):
                                last = nc.tensor.matmul(ps[0:2 * H, 3, half, 0:HALF], w[:, k, :],
                                                        x[:, k, half * HALF:(half + 1) * HALF],
                                                        start=(k == 0 and r == 0), stop=(k == 7 and r == 2))
                    last.then_inc(ba_ps, 1)
                    pe.wait_ge(ba_scaled, 1)
                    for t, (c0, n) in enumerate(TILES):
                        last = nc.tensor.transpose(ps[0:n, 3, 0, 8 * t:8 * t + 8], work[0:2 * H, 7, c0:c0 + n],
                                                   mask[0:2 * H, 0:2 * H])
                    last.then_inc(ba_tok_ps, 1)
                    pe.wait_ge(ab_ready, 1)
                else:
                    pe.wait_ge(psum_free, u - 3)
                product(u, j, KT, x_hi, x_lo, x_ready if j == 0 else None, 8)
                if j == 1:
                    mean_square(1, U_GLU).then_inc(stats_done, 1)
            with pe.Fori(1, (U_Z - U_GLU) // 4) as i:
                for j in range(4):
                    pe.wait_ge(psum_free, 4 * i + (U_GLU + j - 3))
                    product(4 * i + (U_GLU + j), j, KT, x_hi, x_lo)
            for j in range(4):
                pe.wait_ge(psum_free, U_Z + j - 3)
                product(U_Z + j, j, KT, x_hi, x_lo)

            def mm(out, lhsT, rhs, start=True, stop=True):
                return nc.tensor.matmul(out, lhsT, rhs, start=start, stop=stop, skip_group_check=True)

            ident = m("ident")

            def gates(_, i):
                if i:
                    return
                pe.wait_ge(psum_free, U_OUT)
                pe.wait_ge(s["gx_ready"], 1)
                for t, (c0, n) in enumerate(TILES):
                    g = gate["g"][0:n, t, :]
                    mm(bank(3)[:, H * t:H * (t + 1)], tile_mask("incl", t, cols=P), g)
                    mm(bank(3)[:, H * (NT + t):H * (NT + t + 1)], ones[:] if t < 4 else mask[0:n, MASK["same4"]], g)
                n = TILES[4][1]
                mm(bank(3)[:, 2 * NT * H:2 * NT * H + H * NG], ones[0:n, :],
                   gx[0:n].rearrange("p h g -> p (h g)")).then_inc(s["gsum_ps"], 1)

            def prep(t, i):
                c0, n = TILES[t]
                cols = slice(c0, c0 + n)
                b0, b1 = side_banks(t)
                if i == 1:
                    pe.wait_ge(s["qk_sq"], t + 1)
                    if t >= 2:
                        pe.wait_ge(s["att_ready"], t)
                        pe.wait_ge(s["eg_ready"], t)
                        pe.wait_ge(s["tok_ready"], 2)
                    mm(heads(b0, n), ones[:], h4(work[:, 2 * (t % 2), :], n))
                    mm(heads(b1, n), ones[:], h4(work[:, 2 * (t % 2) + 1, :], n)).then_inc(s["norms_ps"], 1)
                if i == 3:
                    pe.wait_ge(s["gates_b"], t + 1)
                    pe.wait_ge(s["qk_log"], t + 1)
                    for hd in range(H):
                        mm(heads(b0, n)[:, hd, :], G_B[t % 2][0:n, hd, :], tile_mask("incl", t))
                    for hd in range(H):
                        last = mm(heads(b1, n)[:, hd, :], B_B[t % 2][0:n, hd, :], m("ident", n))
                    last.then_inc(s["gates_ps"], 1)
                if i == 6:
                    pe.wait_ge(s["qk_normed"], t + 1)
                    pe.wait_ge(s["bs_ready"], t + 1)
                    for hd in range(H):
                        last = mm(heads(b1, n)[0:n, hd, :], qkv[:, H + hd, cols], qkv[:, hd, cols])
                    last.then_inc(s["gram_ps"], 1)

            def tok(t, i):
                if i:
                    return
                c0, n = TILES[t]
                cols = slice(c0, c0 + n)
                done = (2, 2, 5, 5, 5)[t]
                pe.wait_ge(s["qk_normed"], done)
                pe.wait_ge(s["att_ready"], done)
                pe.wait_ge(s["eg_ready"], done)
                if t:
                    pe.wait_ge(s["tok_ready"], t)
                for hd in range(H):
                    nc.tensor.transpose(bank(4)[0:n, hd * P:(hd + 1) * P], qkv[:, H + hd, cols], ident)
                for hd in range(H):
                    last = nc.tensor.transpose(bank(5)[0:n, hd * P:(hd + 1) * P], qkv[:, 2 * H + hd, cols], ident)
                last.then_inc(s["tok_ps"], 1)

            def start(t, i):
                c0, n = TILES[t]
                cols = slice(c0, c0 + n)
                p, a, b, ly, lx = chain_at(t)
                if i == 0:
                    pe.wait_ge(s["qk_normed"], t + 1)
                    if t >= 2:
                        pe.wait_ge(s["nwt_ready"], t - 1)
                    else:
                        pe.wait_ge(s["diffs"], 1)
                    for hd in range(H):
                        last = mm(heads(a, n)[0:n, hd, :], qkv[:, H + hd, cols], qkv[:, H + hd, cols])
                    last.then_inc(s["kk_ps"], 1)
                else:
                    pe.wait_ge(s["y_ready"][p], ly + 1)
                    if t >= 2:
                        pe.wait_ge(s["u_ready"], t - 1)
                    for hd in range(H):
                        last = nc.tensor.transpose(bank(b)[0:n, hd * P:hd * P + n], Y_[p][0:n, hd, 0:n], m("ident", n))
                    last.then_inc(s["x1_ps"], 1)

            def level(t, i):
                l, i = i // 2, i % 2
                n = TILES[t][1]
                p, a, b, ly, lx = chain_at(t)
                if i == 0:
                    pe.wait_ge(s["b_ready"][p], lx + l)
                    pe.wait_ge(s["x_inv"][p], lx + l)
                    pe.wait_ge(s["y_ready"][p], ly + l)
                    for hd in range(H):
                        last = mm(heads(a, n)[0:n, hd, :], BM[p][0:n, hd, 0:n], X_[p][0:n, hd, 0:n])
                    last.then_inc(s["t1_ps"][p], 1)
                else:
                    pe.wait_ge(s["t1_ready"][p], lx + l)
                    for hd in range(H if l < LEVELS[t] - 1 else 0):
                        mm(heads(b, n)[0:n, hd, :], Y_[p][0:n, hd, 0:n], T1[p][0:n, hd, 0:n])
                    for hd in range(H):
                        last = mm(heads(a, n)[0:n, hd, :], T1[p][0:n, hd, 0:n], Y_[p][0:n, hd, 0:n])
                    last.then_inc(s["p_ps"][p], 1)

            def end(t, i):
                n = TILES[t][1]
                p, a, b, ly, lx = chain_at(t)
                if t == 4:
                    return
                pe.wait_ge(s["y_ready"][p], ly + LEVELS[t])
                pe.wait_ge(s["tok_ready"], t + 1)
                for hd in range(H):
                    last = mm(heads(a, n)[:, hd, :], KBG[p][0:n, hd, :], Y_[p][0:n, hd, 0:n])
                last.then_inc(s["wt_ps"], 1)
                for hd in range(H):
                    last = mm(bank(b)[0:n, hd * P:(hd + 1) * P], Y_[p][0:n, hd, 0:n], U_[p][0:n, hd, :])
                last.then_inc(s["u_ps"], 1)

            def scan(t, i):
                n = TILES[t][1]
                p = t % 2
                if i == 0 and t:
                    pe.wait_ge(s["nwt_ready"], t + 1)
                    pe.wait_ge(s["s_ready"], t)
                    for hd in range(H):
                        last = mm(bank(6)[0:n, hd * P:(hd + 1) * P], NWT[p][:, hd, 0:n], S[:, hd, 0, :])
                    last.then_inc(s["vn_ps"], 1)
                if i == 2:
                    pe.wait_ge(s["vn_ready"], t + 1)
                    pe.wait_ge(s["qg_ready"], t + 1)
                    pe.wait_ge(s["att_ready"], max(t + 1, 2))
                    pe.wait_ge(s["eg_ready"], max(t + 1, 2))
                    if t:
                        pe.wait_ge(s["o_log"], t)
                    for hd in range(H):
                        if t:
                            mm(heads(7, n)[:, hd, :], S[:, hd, 0, :], EG[:, t % 4][:, hd, 0:n], stop=False)
                        last = mm(heads(7, n)[:, hd, :], VN[0:n, hd, :], ATT[t % 4][0:n, hd, 0:n], start=(t == 0))
                    last.then_inc(s["o_ps"], 1)
                    for hd in range(H):
                        last = mm(bank(6)[:, hd * P:(hd + 1) * P], KG[p][0:n, hd, :], VN[0:n, hd, :])
                    last.then_inc(s["s_ps"], 1)
                if i == 4:
                    pe.wait_ge(s["osq_ready"], t + 1)
                    mm(heads(7, n), ones[:], h4(work[:, 2, :], n)).then_inc(s["on_ps"], 1)

            def conv(c, _):
                if c == 4:
                    return
                pe.wait_ge(csq_ready, c + 1)
                if c == 0:
                    pe.wait_ge(s["tok_ready"], 5)
                for half in range(2):
                    last = mm(ps[:, 2, half, 0:HALF], mean_c[:], sq[:, c % 2, half * HALF:(half + 1) * HALF],
                              start=(c == 0), stop=(c == NC_ - 1))
                last.then_inc(cn_ps, 1)

            def state_products(hd, gi):
                a, w = GROUPS[gi]
                out = bank(2 + hd // 2)[:, 160 * (hd % 2):160 * (hd % 2) + 160].rearrange("p (x c) -> p x c", x=2)
                return mm(out[:, :, a:a + w], S[:, hd, gi, :], EG[:, 0:2, hd, a:a + w])

            def samples(hd, _):
                if hd == 0:
                    pe.wait_ge(state_in, 16)
                    pe.wait_ge(s["ek_ready"], 1)
                    pe.wait_ge(s["qg_ready"], 5)
                    pe.wait_ge(s["nwt_ready"], 4)
                    pe.wait_ge(s["u_ready"], 4)
                for gi in range(1, NG):
                    last = state_products(hd, gi)
                last.then_inc(s["ss_ps"], 1)

            def taps_step(_, i):
                pass

            def final(_, i):
                t, n = 4, TILES[4][1]
                if i == 0:
                    pe.wait_ge(s["s_ready"], 4)
                    for hd in range(H):
                        last = state_products(hd, 0)
                    last.then_inc(s["os_ps"], 1)
                if i == 1:
                    pe.wait_ge(s["vnt_ready"], 1)
                    pe.wait_ge(s["y_ready"][0], LVO[4] + LEVELS[4])
                    for hd in range(H):
                        last = nc.tensor.transpose(bank(1)[0:n, hd * P:(hd + 1) * P],
                                                   work[:, 3, hd * n:(hd + 1) * n], ident)
                    last.then_inc(s["vn4_ps"], 1)
                if i == 2:
                    pe.wait_ge(s["rhs_ready"], 1)
                    for hd in range(H):
                        last = mm(bank(0)[0:n, hd * P:(hd + 1) * P], Y_[0][0:n, hd, 0:n], U_[0][0:n, hd, :])
                    last.then_inc(s["neg_vn_ps"], 1)
                if i == 3:
                    pe.wait_ge(s["vn_ready"], 5)
                    pe.wait_ge(s["os_ready"], 1)
                    for hd in range(H):
                        last = mm(heads(3, n)[:, hd, :], VN[0:n, hd, :], ATT[0][0:n, hd, 0:n])
                    last.then_inc(s["att4_ps"], 1)
                if 4 <= i < 4 + H:
                    hd = i - 4
                    if hd == 0:
                        pe.wait_ge(s["osq_ready"], 5)
                        mm(heads(2, n), ones[:], h4(work[:, 3, :], n)).then_inc(s["on_ps"], 1)
                    pe.wait_ge(s["vx_ready"], hd + 1)
                    if hd == 0:
                        pe.wait_ge(c_factor, 1)
                    if hd == 1:
                        pe.wait_ge(s["o_log"], 5)
                    if hd >= 2:
                        pe.wait_ge(s["s4_ready"], hd - 1)
                    for b, (a, w) in zip(S4_BANKS[hd % 2], ((0, 512), (512, 512), (1024, 128))):
                        last = mm(bank(b)[:, 0:w], KG[0][0:n, hd, :], VX[hd % 2][:, a:a + w])
                    last.then_inc(s["s4_ps"], 1)

            def weights_split(j, _):
                pass

            steps = {"gates": gates, "prep": prep, "tok": tok, "start": start, "level": level, "end": end, "scan": scan,
                     "conv": conv, "samples": samples, "final": final, "weights": weights_split, "taps": taps_step}
            for name, t, i in delta_schedule():
                steps[name](t, i)

            for j in range(4):
                if j == 1:
                    pe.wait_ge(s["s4_ready"], H)
                product(U_OUT + j, j, KT, x_hi, x_lo, x_ready if j == 0 else None, 16)
            for j in range(4):
                pe.wait_ge(psum_free, U_OUT + 1 + j)
                product(U_OUT + 4 + j, j, KT, x_hi, x_lo)

            ffn(2, U_FFN2, FT, 24)
            pe.wait_ge(ssum_step, 32)
            pe.wait_ge(psum_free, U_END - 3)
            for half in range(2):
                last = nc.tensor.matmul(ps[:, 0, half, 0:HALF], mean_d[:], ssum[:, half * HALF:(half + 1) * HALF],
                                        start=True, stop=True)
            last.then_inc(stats_done, 1)

        def square_place(k):
            return sq[:, k, :] if k < 2 else work[:, k - 2, 0:TOK]

        def tap_place(t):
            return (ssum, sq[:, 0, :], sq[:, 1, :])[t % 3]

        def both(slot):
            return ps[:, slot, :, 0:HALF]

        def two(ap):
            return ap.rearrange("p (a b) -> p a b", a=2)

        @block.scalar
        def _(act):
            def split_hi(u, slot, first=False):
                if not isinstance(u, int):
                    act.wait_ge(raw_in[slot % 2], u * 8 + (16 - 8 * (slot % 2)))
                else:
                    act.wait_ge(raw_in[slot % 2], 16 * (u // 2 + 1))
                if not first:
                    act.wait_ge(unit_done, u - 3)
                nc.scalar.copy(w_hi[:, slot], raw[:, slot % 2]).then_inc(w_hi_ready, 1)

            def prepare(stage, norm, ready, split=True):
                for k in range(KT):
                    ready(k)
                    nc.scalar.activation(square_place(k), h[:, k, :], ACT.Square).then_inc(sq_ready, 1)
                    if split:
                        nc.scalar.activation(x_hi[:, k, :], h[:, k, :], ACT.Copy, scale=v(norm, k)).then_inc(x_hi_ready, 1)

            def root(stage, slot=3):
                if stage == 3:
                    act.wait_ge(stats_done, stage + 1)
                    nc.scalar.activation(two(rstd[:]), both(slot), ACT.Sqrt, bias=eps[:]).then_inc(root_done, 1)
                    return
                nc.scalar.preload_act_table_set("natural_log_exp_and_others")
                act.wait_ge(stats_done, stage + 1)
                nc.scalar.activation(two(rstd[:]), both(slot), ACT.Ln, bias=eps[:]).then_inc(log_done, 1)
                act.wait_ge(log_done, stage + 1)
                nc.scalar.activation(rstd[:], rstd[:], ACT.Exp, scale=-0.5).then_inc(rstd_ready, 1)

            def hidden(ua, f, gslot, j):
                act.wait_ge(psum_free, ua + 1)
                nc.scalar.activation(work[:, 2 + j, 0:TOK], work[:, j, 0:TOK], ACT.Silu).then_inc(silu_done, 1)
                split_hi(ua + 4, (2 * j) % 4)
                act.wait_ge(psum_free, ua + 2)
                nc.scalar.copy(g_hi[:, gslot, :], work[:, 6 + j, 0:TOK]).then_inc(g_hi_ready, 1)
                split_hi(ua + 5, (2 * j + 1) % 4)

            def ffn(base, g0, finish):
                for p, (u0, n, g) in enumerate(parts(base, g0)):
                    with act.Fori(0, n // 2) as i:
                        for j in range(2):
                            hidden(4 * i + (u0 + 2 * j), 2 * i + (g + j), 2 * i + j, j)
                    d0 = u0 + 2 * n
                    if p < len(PARTS) - 1:
                        with act.Fori(0, 2) as i:
                            for j in range(4):
                                split_hi(4 * i + (d0 + j + 4), j)
                    else:
                        finish(d0)

            act.wait_ge(vec_in, 16)
            act.wait_ge(ones_set, 1)
            nc.scalar.copy(wba_hi[:], v("w_ba", 0, KT * 2 * H).rearrange("p (k c) -> p k c", k=KT)).then_inc(wba_hi_ready, 1)
            nc.scalar.activation(expa[:], v("a_log", 0, H), ACT.Exp)

            def x_tile(k):
                act.wait_ge(x_in, 16 * (1 + k // 4))

            split_hi(0, 0, True)
            prepare(0, "ffn1_norm", x_tile)
            split_hi(1, 1, True)
            split_hi(2, 2, True)
            split_hi(3, 3, True)
            root(0)

            def finish_with(stage, norm, lookahead):
                def finish(d0):
                    def ready(k):
                        if d0 + k + 4 < U_END:
                            split_hi(d0 + k + 4, k % 4)
                        act.wait_ge(psum_free, d0 + k + 1)
                    prepare(stage, norm, ready, norm is not None)
                return finish

            ffn(U_FFN1, 0, finish_with(1, "mix_norm", True))

            root(1)
            taps = [0]

            def conv_taps(n):
                for t in range(taps[0], min(taps[0] + n, POOL_TAPS)):
                    c, j = t // (CW - 1), 1 + t % (CW - 1)
                    act.wait_ge(c_in_ready, c + 1)
                    if t >= 3:
                        act.wait_ge(tap_added, t - 2)
                    o = tap_place(t)
                    nc.scalar.activation(o[:, 0:L], c_ext[:, c, j:j + L], ACT.Copy, scale=v("conv_w", CW * c + j))
                    nc.scalar.activation(o[:, L:TOK].rearrange("p (b w) -> p b w", b=NB),
                                         c_ext[:, c, CP:CE].rearrange("p (b w) -> p b w", b=NB)[:, :, j:j + LB],
                                         ACT.Copy, scale=v("conv_w", CW * c + j)).then_inc(tap_ready, 1)
                taps[0] += n

            act.wait_ge(pads_set, 1)
            act.wait_ge(hist_in, 16 * (2 + NC_))
            for c in range(NC_):
                u = U_GLU + 2 * c
                split_hi(u + 4, (u + 4) % 4)
                if c:
                    conv_taps(8)
                if c == 1:
                    act.wait_ge(ab_ready, 1)
                    nc.scalar.activation(gate["beta"][:], ba[:, :, 0:H], ACT.Sigmoid).then_inc(gate_act, 1)
                    nc.scalar.activation(gate["t2"][:], gate["t1"][:], ACT.Exp, scale=-1.0).then_inc(gate_act, 1)
                    act.wait_ge(gate_act, 2)
                    nc.scalar.activation(gate["t3"][:], gate["t2"][:], ACT.Ln, bias=1.0).then_inc(gate_act, 1)
                act.wait_ge(psum_free, u + 2)
                nc.scalar.activation(work[:, 1 + 2 * (c % 2), 0:TOK], work[:, 1 + 2 * (c % 2), 0:TOK],
                                     ACT.Sigmoid).then_inc(sig_ready, 1)
                split_hi(u + 5, (u + 5) % 4)
            for i in range(NQ):
                u = U_QKV + i
                split_hi(u + 4, (u + 4) % 4)
                conv_taps(3)
                act.wait_ge(psum_free, u + 1)
                e = work[:, i % 2, :]
                nc.scalar.copy(lastq[:, i, 0:3], e[:, L:L + 3])
                nc.scalar.copy(lastq[:, i, 3:27].rearrange("p (b w) -> p b w", b=NB),
                               e[:, QP:QE].rearrange("p (b w) -> p b w", b=NB)[:, :, LB:QS]).then_inc(lastq_saved, 1)
                act.wait_ge(q_conv, i + 1)
                a = work[:, 2 + i % 2, :]
                nc.scalar.activation(qkv[:, i, 0:L], a[:, 0:L], ACT.Silu)
                nc.scalar.activation(qkv[:, i, L:TOK].rearrange("p (b w) -> p b w", b=NB),
                                     a[:, QP:QE].rearrange("p (b w) -> p b w", b=NB)[:, :, 0:LB],
                                     ACT.Silu).then_inc(q_ready, 1)
            for i in range(H):
                u = U_Z + i
                conv_taps(1)
                act.wait_ge(psum_free, u + 1)
                nc.scalar.activation(z[:, i, :], z[:, i, :], ACT.Silu).then_inc(z_ready, 1)

            def gates(_, i):
                if i == 0:
                    nc.scalar.preload_act_table_set("natural_log_exp_and_others")
                if i == 2:
                    act.wait_ge(s["diffs"], 1)
                    nt = NT * H
                    nc.scalar.activation(f_cum[:].rearrange("p t h -> p (t h)"), gcs[:, 0:nt], ACT.Exp)
                    nc.scalar.activation(f_all[:].rearrange("p t h -> p (t h)"), gcs[:, nt:2 * nt], ACT.Exp)
                    nc.scalar.activation(f_group[:], gcs[:, 2 * nt:2 * nt + H * NG], ACT.Exp)
                    nc.scalar.activation(f_rest[:], f_kbg[:], ACT.Exp).then_inc(s["facs"], 1)

            def prep(t, i):
                c0, n = TILES[t]
                cols = slice(c0, c0 + n)
                p = t % 2
                b0, b1 = side_banks(t)
                r = work[:, 2 * p:2 * p + 2, 0:H * n]
                if i == 0:
                    act.wait_ge(q_ready, NQ)
                    if t >= 2:
                        act.wait_ge(s["qk_normed"], t - 1)
                    for q in range(2):
                        last = nc.scalar.activation(h4(work[:, 2 * p + q, :], n), qkv[:, H * q:H * (q + 1), cols], ACT.Square)
                    last.then_inc(s["qk_sq"], 1)
                if i == 2:
                    act.wait_ge(s["norms_ps"], t + 1)
                    for q, b in enumerate((b0, b1)):
                        last = nc.scalar.activation(h4(work[:, 2 * p + q, :], n), heads(b, n), ACT.Ln, bias=eps[:])
                    last.then_inc(s["qk_log"], 1)
                if i == 3:
                    act.wait_ge(s["qk_log"], t + 1)
                    nc.scalar.activation(r, r, ACT.Exp, scale=-0.5).then_inc(s["qk_factor"], 1)
                if i == 5:
                    act.wait_ge(s["d_diff"], t + 1)
                    nc.scalar.activation(E_[p][0:n, :, 0:n], E_[p][0:n, :, 0:n], ACT.Exp).then_inc(s["e_ready"], 1)
                    if t == 4:
                        act.wait_ge(s["o_ps"], 1)
                    nc.scalar.activation(EG[:, t % 4][:, :, 0:n], heads(b0, n), ACT.Exp).then_inc(s["eg_ready"], 1)

            def tok(t, i):
                pass

            def start(t, i):
                n = TILES[t][1]
                p, a, b, ly, lx = chain_at(t)
                if i == 1:
                    act.wait_ge(s["x1_ps"], t + 1)
                    nc.scalar.copy(X_[p][0:n, :, 0:n], heads(b, n)[0:n]).then_inc(s["x_inv"][p], 1)

            def level(t, i):
                l, i = i // 2, i % 2
                n = TILES[t][1]
                p, a, b, ly, lx = chain_at(t)
                if i == 0:
                    act.wait_ge(s["t1_ps"][p], lx + l)
                    nc.scalar.copy(T1[p][0:n, :, 0:n], heads(a, n)[0:n]).then_inc(s["t1_ready"][p], 1)

            def end(t, i):
                n = TILES[t][1]
                p, a, b, ly, lx = chain_at(t)
                if t == 4:
                    return
                act.wait_ge(s["wt_ps"], t + 1)
                if t >= 3:
                    act.wait_ge(s["vn_ps"], t - 2)
                nc.scalar.activation(NWT[p][:, :, 0:n], heads(a, n), ACT.Copy, scale=-1.0).then_inc(s["nwt_ready"], 1)

            def o_norm(t, b, n):
                r = h4(work[:, 3, :], n)
                act.wait_ge(s["on_ps"], t + 1)
                nc.scalar.activation(r, heads(b, n), ACT.Ln, bias=eps[:], scale=1.0 / P).then_inc(s["o_log"], 1)
                act.wait_ge(s["o_log"], t + 1)
                nc.scalar.activation(r, r, ACT.Exp, scale=-0.5).then_inc(s["o_factor"], 1)

            def scan(t, i):
                c0, n = TILES[t]
                cols = slice(c0, c0 + n)
                if i == 3:
                    act.wait_ge(s["o_ps"], t + 1)
                    nc.scalar.copy(qkv[:, 0:H, cols], heads(7, n)).then_inc(s["o_evac"], 1)
                    act.wait_ge(s["o_evac"], t + 1)
                    if t == 0:
                        act.wait_ge(s["qk_normed"], 4)
                    else:
                        act.wait_ge(s["on_ps"], t)
                    nc.scalar.activation(h4(work[:, 2, :], n), qkv[:, 0:H, cols], ACT.Square).then_inc(s["osq_ready"], 1)
                if i == 5:
                    if t:
                        act.wait_ge(s["o_ready"], t)
                    o_norm(t, 7, n)

            def conv(c, _):
                if c < 4:
                    if c == 0:
                        act.wait_ge(tap_added, POOL_TAPS)
                    if c < 3:
                        act.wait_ge(tap_added, (CW - 1) * (c + 1))
                    else:
                        act.wait_ge(conv3_step, CW)
                    if c >= 2:
                        act.wait_ge(cn_ps, c - 1)
                    nc.scalar.activation(sq[:, c % 2, :], work[:, 4 + c, 0:TOK], ACT.Square).then_inc(csq_ready, 1)
                    if c < 3:
                        return
                    act.wait_ge(cn_ps, NC_)
                    nc.scalar.activation(two(ssum[:]), both(2), ACT.Ln, bias=eps[:]).then_inc(c_factor, 1)
                    act.wait_ge(c_factor, 1)
                    nc.scalar.activation(ssum[:], ssum[:], ACT.Exp, scale=-0.5).then_inc(c_factor, 1)

            def samples(hd, _):
                pass

            def taps_step(_, i):
                conv_taps(2)

            def final(_, i):
                t, (c0, n) = 4, TILES[4]
                sums = ps[:, 1, :, 0:4 * n].rearrange("p b (h x c) -> p b h x c", h=2, x=2)
                if i == 0:
                    act.wait_ge(s["os_ps"], 1)
                    act.wait_ge(s["o_ready"], 4)
                    nc.scalar.copy(h4(work[:, 3, :], n).rearrange("p (b h) c -> p b h c", b=2),
                                   sums[:, :, :, 1, :]).then_inc(s["vnt_ready"], 1)
                    nc.scalar.copy(h4(work[:, 2, :], n).rearrange("p (b h) c -> p b h c", b=2),
                                   sums[:, :, :, 0, :]).then_inc(s["os_ready"], 1)
                if i == 2:
                    act.wait_ge(s["neg_vn_ps"], 1)
                    nc.scalar.activation(VN[0:n], heads(0, P)[0:n], ACT.Copy, scale=-1.0).then_inc(s["vn_ready"], 1)
                if i == 4:
                    act.wait_ge(s["o_evac"], NT)
                    nc.scalar.activation(h4(work[:, 3, :], n), qkv[:, 0:H, c0:c0 + n], ACT.Square).then_inc(s["osq_ready"], 1)
                if i == 5:
                    o_norm(4, 2, n)

            def weights_split(j, _):
                if j == 0:
                    act.wait_ge(s["p_ps"][0], LVO[4] - 2 + LEVELS[4] - 1)
                split_hi(U_OUT + j, j)

            steps = {"gates": gates, "prep": prep, "tok": tok, "start": start, "level": level, "end": end, "scan": scan,
                     "conv": conv, "samples": samples, "final": final, "weights": weights_split, "taps": taps_step}
            for name, t, i in delta_schedule():
                steps[name](t, i)

            act.wait_ge(s["att4_ps"], 1)
            for i in range(H):
                act.wait_ge(mix_ready, i + 1)
                nc.scalar.copy(x_hi[:, i, :], qkv[:, i, :]).then_inc(x_hi_ready, 1)
            for c in range(NC_):
                act.wait_ge(c_scaled, c + 1)
                nc.scalar.activation(work[:, 4 + c, 0:TOK], work[:, 4 + c, 0:TOK], ACT.Silu,
                                     scale=v("conv_norm", c)).then_inc(c_act, 1)
                act.wait_ge(c_act, c + 1)
                nc.scalar.copy(x_hi[:, H + c, :], work[:, 4 + c, 0:TOK]).then_inc(x_hi_ready, 1)
            split_hi(U_OUT + 2, 2)
            split_hi(U_OUT + 3, 3)
            act.wait_ge(s["s4_ready"], H)
            act.dma_start(new_state, S[:]).then_inc(state_out, 16)

            def out_tile(k):
                split_hi(U_OUT + 4 + k, k % 4)
                act.wait_ge(psum_free, U_OUT + k + 1)
            prepare(2, None, out_tile, split=False)
            act.wait_ge(unit_done, U_FFN2)
            for k in range(KT):
                nc.scalar.activation(x_hi[:, k, :], h[:, k, :], ACT.Copy,
                                     scale=v("ffn2_norm", k)).then_inc(x_hi_ready, 1)
            root(2)
            act.wait_ge(state_out, 16)
            ffn(U_FFN2, FT, finish_with(3, None, False))
            root(3, 0)
            for k in range(KT):
                nc.scalar.activation(h[:, k, :], h[:, k, :], ACT.Copy, scale=v("final_norm", k)).then_inc(y_gain, 1)

        @block.vector
        def _(dve):
            V = nc.vector
            count = [0]

            def link(ins):
                count[0] += 1
                ins.then_inc(link_s, 1)
                dve.wait_ge(link_s, count[0])

            def split_lo(u, slot):
                dve.wait_ge(w_hi_ready, u + 1)
                V.tensor_tensor(w_lo[:, slot], raw[:, slot % 2], w_hi[:, slot].bitcast(F32),
                                ALU.subtract).then_inc(w_lo_ready, 1)

            def rest_of_x(k, norm, at):
                dve.wait_ge(x_hi_ready, at + k + 1)
                V.scalar_tensor_tensor(x_lo[:, k, :], h[:, k, :], v(norm, k), x_hi[:, k, :].bitcast(F32),
                                       ALU.mult, ALU.subtract).then_inc(x_ready, 1)

            def rms_factor(stage):
                if stage == 3:
                    dve.wait_ge(root_done, 1)
                    V.reciprocal(rstd[:], rstd[:]).then_inc(rstd_ready, 1)
                dve.wait_ge(rstd_ready, stage + 1)

            def scaled(out, u, slot):
                dve.wait_ge(unit_done, u + 1)
                return V.tensor_tensor(two(out), both(slot), two(rstd[:]), ALU.mult)

            def hidden(ua, f, gslot, j):
                scaled(work[:, j, 0:TOK], ua, 2 * j).then_inc(psum_free, 1)
                split_lo(ua + 4, 2 * j)
                dve.wait_ge(silu_done, f + 1)
                V.tensor_tensor(work[:, 4 + j, 0:TOK], work[:, 2 + j, 0:TOK], rstd[:], ALU.mult).then_inc(sr_ready, 1)
                dve.wait_ge(sr_ready, f + 1)
                dve.wait_ge(unit_done, ua + 2)
                V.tensor_tensor(two(work[:, 6 + j, 0:TOK]), both(2 * j + 1), two(work[:, 4 + j, 0:TOK]),
                                ALU.mult).then_inc(psum_free, 1)
                split_lo(ua + 5, 2 * j + 1)
                dve.wait_ge(g_hi_ready, f + 1)
                V.tensor_tensor(g_lo[:, gslot, :], work[:, 6 + j, 0:TOK], g_hi[:, gslot, :].bitcast(F32),
                                ALU.subtract).then_inc(g_ready, 1)

            def add_to_h(u, slot, k, factor):
                dve.wait_ge(unit_done, u + 1)
                dve.wait_ge(psum_free, u - 7)
                V.scalar_tensor_tensor(two(h[:, k, :]), both(slot), factor, two(h[:, k, :]), ALU.mult,
                                       ALU.add).then_inc(psum_free, 1)

            def ffn(base, g0, norm, at):
                for p, (u0, n, g) in enumerate(parts(base, g0)):
                    with dve.Fori(0, n // 2) as i:
                        for j in range(2):
                            hidden(4 * i + (u0 + 2 * j), 2 * i + (g + j), 2 * i + j, j)
                    d0 = u0 + 2 * n
                    if p < len(PARTS) - 1:
                        with dve.Fori(0, 2) as i:
                            for j in range(4):
                                add_to_h(4 * i + (d0 + j), j, 4 * i + j, 0.5)
                                split_lo(4 * i + (d0 + j + 4), j)
                    else:
                        for k in range(KT):
                            add_to_h(d0 + k, k % 4, k, 0.5)
                            if d0 + k + 4 < U_END:
                                split_lo(d0 + k + 4, k % 4)
                            if norm is not None:
                                rest_of_x(k, norm, at)

            V.memset(mean_d[:], 1.0 / D)
            V.memset(mean_c[:], 1.0 / (NC_ * P))
            V.memset(eps[:], EPS)
            V.memset(ones[:], 1.0).then_inc(ones_set, 1)
            V.memset(c_ext[:, :, 0:CW - 1], 0.0)
            V.memset(ba[:], 0.0).then_inc(pads_set, 1)
            dve.wait_ge(wba_hi_ready, 1)
            V.tensor_tensor(wba_lo[:], v("w_ba", 0, KT * 2 * H).rearrange("p (k c) -> p k c", k=KT),
                            wba_hi[:].bitcast(F32), ALU.subtract).then_inc(wba_ready, 1)
            split_lo(0, 0)
            for k in range(KT):
                rest_of_x(k, "ffn1_norm", 0)
            for u in range(1, 4):
                split_lo(u, u)
            rms_factor(0)
            ffn(U_FFN1, 0, "mix_norm", 8)

            rms_factor(1)
            dve.wait_ge(pads_set, 1)
            dve.wait_ge(hist_in, 16 * (2 + NC_))

            def gate_inputs():
                dve.wait_ge(ba_ps, 1)
                V.tensor_tensor(two(work[0:2 * H, 7, 0:TOK]), ps[0:2 * H, 3, :, 0:HALF], two(rstd[0:2 * H, :]),
                                ALU.mult).then_inc(ba_scaled, 1)
                dve.wait_ge(ba_tok_ps, 1)
                V.tensor_copy(ba[:, 0:4, :], ps[:, 3, 0, 0:32].rearrange("p (t c) -> p t c", t=4))
                link(V.tensor_copy(ba[0:80, 4, :], ps[0:80, 3, 0, 32:40]))
                link(V.tensor_tensor(gate["g"][:], ba[:, :, H:2 * H],
                                     v("dt_bias", 0, H).unsqueeze(1).to_broadcast([P, NT, H]), ALU.add))
                V.scalar_tensor_tensor(gate["t1"][:], gate["g"][:], -1.0, gate["g"][:], ALU.mult, ALU.max).then_inc(ab_ready, 1)

            for c in range(NC_):
                u = U_GLU + 2 * c
                a, b = work[:, 2 * (c % 2), :], work[:, 1 + 2 * (c % 2), :]
                scaled(a[:, 0:TOK], u, u % 4).then_inc(psum_free, 1)
                split_lo(u + 4, (u + 4) % 4)
                if c == 1:
                    gate_inputs()
                scaled(b[:, 0:TOK], u + 1, (u + 1) % 4).then_inc(psum_free, 1)
                split_lo(u + 5, (u + 5) % 4)
                dve.wait_ge(sig_ready, c + 1)
                dve.wait_ge(psum_free, u + 2)
                V.tensor_tensor(c_ext[:, c, CW - 1:CP], a[:, 0:L], b[:, 0:L], ALU.mult)
                V.tensor_tensor(c_ext[:, c, CP:CE].rearrange("p (b w) -> p b w", b=NB)[:, :, CW - 1:CS],
                                a[:, L:TOK].rearrange("p (b w) -> p b w", b=NB),
                                b[:, L:TOK].rearrange("p (b w) -> p b w", b=NB), ALU.mult).then_inc(c_in_ready, 1)
                if c == 2:
                    dve.wait_ge(gate_act, 3)
                    link(V.scalar_tensor_tensor(gate["t2"][:], gate["g"][:], 0.0, gate["t3"][:], ALU.max, ALU.add))
                    V.scalar_tensor_tensor(gate["g"][:], gate["t2"][:], -1.0,
                                           expa[:].unsqueeze(1).to_broadcast([P, NT, H]), ALU.mult,
                                           ALU.mult).then_inc(gates_ready, 1)

            dve.wait_ge(c_in_ready, NC_)
            for i in range(2):
                last = V.memset(work[:, i, 0:SC - 1], 0.0)
            link(last)
            for i in range(NQ):
                u = U_QKV + i
                e, a = work[:, i % 2, :], work[:, 2 + i % 2, :]
                if i >= 2:
                    dve.wait_ge(lastq_saved, i - 1)
                dve.wait_ge(unit_done, u + 1)
                V.tensor_copy(e[:, QP:QE].rearrange("p (b w) -> p b w", b=NB)[:, :, 0:SC - 1],
                              hq[:, i, :].rearrange("p (b w) -> p b w", b=NB))
                V.tensor_tensor(e[:, 3:3 + HALF], ps[:, u % 4, 0, 0:HALF], rstd[:, 0:HALF], ALU.mult)
                V.tensor_tensor(e[:, 3 + HALF:QP], ps[:, u % 4, 1, 0:L - HALF], rstd[:, HALF:L], ALU.mult)
                V.tensor_tensor(e[:, QP:QE].rearrange("p (b w) -> p b w", b=NB)[:, :, SC - 1:QS],
                                ps[:, u % 4, 1, L - HALF:HALF].rearrange("p (b w) -> p b w", b=NB),
                                rstd[:, L:TOK].rearrange("p (b w) -> p b w", b=NB), ALU.mult).then_inc(psum_free, 1)
                split_lo(u + 4, (u + 4) % 4)
                dve.wait_ge(psum_free, u + 1)
                if i >= 2:
                    dve.wait_ge(q_ready, i - 1)
                link(V.tensor_scalar(a[:, 0:QO], e[:, 0:QO], v("qkv_conv_w", SC * i), None, ALU.mult))
                for j in range(1, SC):
                    ins = V.scalar_tensor_tensor(a[:, 0:QO], e[:, j:j + QO], v("qkv_conv_w", SC * i + j), a[:, 0:QO],
                                                 ALU.mult, ALU.add)
                    if j < SC - 1:
                        link(ins)
                    else:
                        ins.then_inc(q_conv, 1)

            for i in range(H):
                u = U_Z + i
                scaled(z[:, i, :], u, u % 4).then_inc(psum_free, 1)

            taps = [0]

            def conv_taps(n):
                out, c = work[:, 7, :], 3
                parts = ((out[:, 0:L], lambda j: c_ext[:, c, j:j + L]),
                         (out[:, L:TOK].rearrange("p (b w) -> p b w", b=NB),
                          lambda j: c_ext[:, c, CP:CE].rearrange("p (b w) -> p b w", b=NB)[:, :, j:j + LB]))
                for j in range(taps[0], min(taps[0] + n, CW)):
                    if j:
                        dve.wait_ge(conv3_step, j)
                    for o, x in parts:
                        if j:
                            last = V.scalar_tensor_tensor(o, x(j), v("conv_w", CW * c + j), o, ALU.mult, ALU.add)
                        else:
                            last = V.tensor_scalar(o, x(j), v("conv_w", CW * c), v("conv_b", c), ALU.mult, ALU.add)
                    last.then_inc(conv3_step, 1)
                taps[0] += n

            def gates(_, i):
                if i == 1:
                    dve.wait_ge(s["gsum_ps"], 1)
                    link(V.tensor_copy(gcs[:], bank(3)[:, 0:2 * NT * H + H * NG]))
                    nt = NT * H
                    V.tensor_tensor(f_kbg[:].rearrange("p t h -> p (t h)"), gcs[:, nt:2 * nt], gcs[:, 0:nt],
                                    ALU.subtract).then_inc(s["diffs"], 1)
                if i == 2:
                    dve.wait_ge(s["facs"], 1)
                    V.tensor_tensor(f_kbg[:], gate["beta"][:], f_cum[:], ALU.mult).then_inc(s["f_ready"], 1)

            def prep(t, i):
                c0, n = TILES[t]
                cols = slice(c0, c0 + n)
                p = t % 2
                b0, b1 = side_banks(t)
                if i == 0:
                    dve.wait_ge(gates_ready, 1)
                    if t >= 2:
                        dve.wait_ge(s["gates_ps"], t - 1)
                    V.tensor_copy(G_B[p][0:n], over_cols(gate["g"][0:n, t, :], P))
                    V.tensor_copy(B_B[p][0:n], over_cols(gate["beta"][0:n, t, :], P)).then_inc(s["gates_b"], 1)
                if i == 4:
                    dve.wait_ge(s["qk_factor"], t + 1)
                    V.tensor_tensor(qkv[:, H:2 * H, cols], qkv[:, H:2 * H, cols], h4(work[:, 2 * p + 1, :], n), ALU.mult)
                    V.scalar_tensor_tensor(qkv[:, 0:H, cols], qkv[:, 0:H, cols], float(P) ** -0.5,
                                           h4(work[:, 2 * p, :], n), ALU.mult, ALU.mult).then_inc(s["qk_normed"], 1)
                    dve.wait_ge(s["gates_ps"], t + 1)
                    if t >= 2:
                        dve.wait_ge(s["es_ready"], t - 1)
                    for hd in range(H):
                        last = V.tensor_scalar(E_[p][0:n, hd, 0:n], heads(b0, n)[0:n, hd, :],
                                               gcs[0:n, H * t + hd:H * t + hd + 1], 0.0, ALU.subtract, ALU.min)
                    last.then_inc(s["d_diff"], 1)
                if i == 5:
                    V.tensor_tensor(ES[p][0:n, :, 0:n], heads(b1, n)[0:n], over_heads(tile_mask("strict", t), n),
                                    ALU.mult).then_inc(s["bs_ready"], 1)
                if i == 8:
                    dve.wait_ge(s["gram_ps"], t + 1)
                    dve.wait_ge(s["em_ready"], t + 1)
                    if t == 4:
                        dve.wait_ge(s["o_ps"], 1)
                    V.tensor_tensor(ATT[t % 4][0:n, :, 0:n], heads(b1, n)[0:n], E_[p][0:n, :, 0:n],
                                    ALU.mult).then_inc(s["att_ready"], 1)

            def tok(t, i):
                n = TILES[t][1]
                p = t % 2
                if i == 0:
                    return
                dve.wait_ge(s["tok_ps"], t + 1)
                if t == 0:
                    dve.wait_ge(s["f_ready"], 1)
                if t >= 2:
                    dve.wait_ge(s["wt_ps"], t - 1)
                    dve.wait_ge(s["s_ps"], t - 1)
                V.tensor_tensor(U_[p][0:n], heads(5, P)[0:n], over_cols(gate["beta"][0:n, t, :], P), ALU.mult)
                if t < 4:
                    V.tensor_tensor(KBG[p][0:n], heads(4, P)[0:n], over_cols(f_kbg[0:n, t, :], P), ALU.mult)
                V.tensor_tensor(KG[p][0:n], heads(4, P)[0:n], over_cols(f_rest[0:n, t, :], P),
                                ALU.mult).then_inc(s["tok_ready"], 1)

            def start(t, i):
                n = TILES[t][1]
                p, a, b, ly, lx = chain_at(t)
                if i:
                    return
                dve.wait_ge(s["kk_ps"], t + 1)
                dve.wait_ge(s["es_ready"], t + 1)
                V.tensor_tensor(AT[p][0:n, :, 0:n], heads(a, n)[0:n], ES[p][0:n, :, 0:n], ALU.mult).then_inc(s["at_ready"], 1)
                dve.wait_ge(s["at_ready"], t + 1)
                link(V.tensor_tensor(T1[p][0:n, :, 0:n], AT[p][0:n, :, 0:n], over_heads(m("levels", n, 0), n), ALU.mult))
                if t == 2 or t == 3:
                    dve.wait_ge(s["u_ps"], t - 1)
                if t == 4:
                    dve.wait_ge(s["u_ps"], 3)
                V.tensor_tensor(Y_[p][0:n, :, 0:n], over_heads(m("ident", n), n), T1[p][0:n, :, 0:n],
                                ALU.subtract).then_inc(s["y_ready"][p], 1)

            def level(t, i):
                l, i = i // 2, i % 2
                n = TILES[t][1]
                p, a, b, ly, lx = chain_at(t)
                if i == 1:
                    dve.wait_ge(s["p_ps"][p], lx + l)
                    dve.wait_ge(s["x_inv"][p], lx + l)
                    if l < LEVELS[t] - 1:
                        V.tensor_tensor(X_[p][0:n, :, 0:n], X_[p][0:n, :, 0:n], heads(b, n)[0:n],
                                        ALU.subtract).then_inc(s["x_inv"][p], 1)
                    dve.wait_ge(s["y_ready"][p], ly + l)
                    V.tensor_tensor(Y_[p][0:n, :, 0:n], Y_[p][0:n, :, 0:n], heads(a, n)[0:n],
                                    ALU.subtract).then_inc(s["y_ready"][p], 1)
                    conv_taps(2 if t < 2 else 1)

            def end(t, i):
                n = TILES[t][1]
                p, a, b, ly, lx = chain_at(t)
                if t < 4:
                    dve.wait_ge(s["u_ps"], t + 1)
                    V.tensor_copy(U_[p][0:n], heads(b, P)[0:n]).then_inc(s["u_ready"], 1)

            def scan(t, i):
                c0, n = TILES[t]
                cols = slice(c0, c0 + n)
                p = t % 2
                if i == 1:
                    dve.wait_ge(s["u_ready"], t + 1)
                    if t == 0:
                        V.tensor_copy(VN[:], U_[p][:]).then_inc(s["vn_ready"], 1)
                    else:
                        dve.wait_ge(s["vn_ps"], t)
                        dve.wait_ge(s["s_ps"], t)
                        V.tensor_tensor(VN[:], U_[p][:], heads(6, P), ALU.add).then_inc(s["vn_ready"], 1)
                if i == 3:
                    dve.wait_ge(s["s_ps"], t + 1)
                    if t == 0:
                        V.tensor_copy(S[:, :, 0, :], heads(6, P)).then_inc(s["s_ready"], 1)
                    else:
                        dve.wait_ge(s["s_ready"], t)
                        for hd in range(H):
                            last = V.scalar_tensor_tensor(S[:, hd, 0, :], S[:, hd, 0, :], f_all[:, t, hd:hd + 1],
                                                          heads(6, P)[:, hd, :], ALU.mult, ALU.add)
                        last.then_inc(s["s_ready"], 1)
                if i == 6:
                    dve.wait_ge(s["o_factor"], t + 1)
                    V.tensor_tensor(qkv[:, 0:H, cols], qkv[:, 0:H, cols], h4(work[:, 3, :], n),
                                    ALU.mult).then_inc(s["o_ready"], 1)

            def conv(c, _):
                if c == 0:
                    conv_taps(CW)
                if c == 4:
                    dve.wait_ge(c_factor, 2)
                    for i in range(NC_):
                        V.tensor_tensor(work[:, 4 + i, 0:TOK], work[:, 4 + i, 0:TOK], ssum[:], ALU.mult).then_inc(c_scaled, 1)

            def mixed(cols):
                for i in range(H):
                    V.scalar_tensor_tensor(qkv[:, i, cols], qkv[:, i, cols], v("o_norm"), z[:, i, cols], ALU.mult,
                                           ALU.mult).then_inc(mix_ready, 1)

            def samples(hd, _):
                pass

            def taps_step(_, i):
                pass

            def add_states(hd):
                b = S4_BANKS[hd % 2]
                dve.wait_ge(s["s_scaled"], hd + 1)
                dve.wait_ge(s["s4_ps"], hd + 1)
                V.scalar_tensor_tensor(S[:, hd, 0, :], S[:, hd, 0, :], f_group[:, NG * hd:NG * hd + 1],
                                       bank(b[0])[:, 0:P], ALU.mult, ALU.add)
                V.tensor_tensor(S[:, hd, 1:8, :], S[:, hd, 1:8, :],
                                ps[:, b[0] // 2].rearrange("p a (g c) -> p (a g) c", g=4)[:, 1:8], ALU.add)
                V.tensor_tensor(S[:, hd, 8, :], S[:, hd, 8, :], bank(b[2])[:, 0:P], ALU.add).then_inc(s["s4_ready"], 1)

            def final(_, i):
                t, (c0, n) = 4, TILES[4]
                cols = slice(c0, c0 + n)
                if i == 1:
                    dve.wait_ge(s["vn4_ps"], 1)
                    for hd in range(H):
                        last = V.scalar_tensor_tensor(U_[0][0:n, hd, :], bank(1)[0:n, hd * P:(hd + 1) * P],
                                                      gate["beta"][0:n, t, hd:hd + 1], U_[0][0:n, hd, :], ALU.mult,
                                                      ALU.subtract)
                    last.then_inc(s["rhs_ready"], 1)
                if i == 3:
                    dve.wait_ge(s["os_ready"], 1)
                    dve.wait_ge(s["att4_ps"], 1)
                    V.tensor_tensor(qkv[:, 0:H, cols], heads(3, n), h4(work[:, 2, :], n), ALU.add).then_inc(s["o_evac"], 1)
                if i == 6:
                    dve.wait_ge(s["o_factor"], t + 1)
                    V.tensor_tensor(qkv[:, 0:H, cols], qkv[:, 0:H, cols], h4(work[:, 3, :], n),
                                    ALU.mult).then_inc(s["o_ready"], 1)
                    dve.wait_ge(z_ready, H)
                    dve.wait_ge(s["o_ready"], NT)
                    mixed(slice(0, TOK))
                if i == 5 or i == 7:
                    add_states((i - 5) // 2)

            def weights_split(j, _):
                if j == 0:
                    dve.wait_ge(s["p_ps"][0], LVO[4] - 2 + LEVELS[4] - 1)
                split_lo(U_OUT + j, j)

            steps = {"gates": gates, "prep": prep, "tok": tok, "start": start, "level": level, "end": end, "scan": scan,
                     "conv": conv, "samples": samples, "final": final, "weights": weights_split, "taps": taps_step}
            for name, t, i in delta_schedule():
                steps[name](t, i)

            for i in range(2 * H):
                dve.wait_ge(x_hi_ready, 16 + i + 1)
                if i == 5:
                    dve.wait_ge(s["s4_ps"], H)
                src = qkv[:, i, :] if i < H else work[:, i, 0:TOK]
                V.tensor_tensor(x_lo[:, i, :], src, x_hi[:, i, :].bitcast(F32), ALU.subtract).then_inc(x_ready, 1)
            add_states(2)
            add_states(3)
            split_lo(U_OUT + 2, 2)
            split_lo(U_OUT + 3, 3)

            for k in range(KT):
                add_to_h(U_OUT + k, k % 4, k, 1.0)
                split_lo(U_OUT + k + 4, k % 4)
            for k in range(KT):
                rest_of_x(k, "ffn2_norm", 24)
            rms_factor(2)
            ffn(U_FFN2, FT, None, 0)
            rms_factor(3)
            for k in range(KT):
                dve.wait_ge(y_gain, k + 1)
                V.tensor_tensor(h[:, k, :], h[:, k, :], rstd[:], ALU.mult).then_inc(y_ready, 1)

        @block.gpsimd
        def _(pool):
            G = nc.gpsimd
            count = [0]

            def link(ins):
                count[0] += 1
                ins.then_inc(pool_s, 1)
                pool.wait_ge(pool_s, count[0])

            def sum_squares(stage):
                for k in range(KT):
                    pool.wait_ge(sq_ready, 8 * stage + k + 1)
                    if k == 0:
                        if stage:
                            pool.wait_ge(stats_done, stage)
                        G.tensor_copy(ssum[:], square_place(0)).then_inc(ssum_step, 1)
                    else:
                        pool.wait_ge(ssum_step, 8 * stage + k)
                        G.tensor_tensor(ssum[:], ssum[:], square_place(k), ALU.add).then_inc(ssum_step, 1)

            sum_squares(0)
            sum_squares(1)

            pool.wait_ge(vec_in, 16)
            pool.wait_ge(hist_in, 16 * (2 + NC_))
            pool.wait_ge(pads_set, 1)
            pool.wait_ge(stats_done, 2)
            def conv_taps(t0, t1):
                for t in range(t0, min(t1, POOL_TAPS)):
                    c, j = t // (CW - 1), 1 + t % (CW - 1)
                    out = work[:, 4 + c, :]
                    if j == 1:
                        pool.wait_ge(c_in_ready, c + 1)
                        G.tensor_scalar(out[:, 0:L], c_ext[:, c, 0:L], v("conv_w", CW * c), v("conv_b", c), ALU.mult, ALU.add)
                        link(G.tensor_scalar(out[:, L:TOK].rearrange("p (b w) -> p b w", b=NB),
                                             c_ext[:, c, CP:CE].rearrange("p (b w) -> p b w", b=NB)[:, :, 0:LB],
                                             v("conv_w", CW * c), v("conv_b", c), ALU.mult, ALU.add))
                    pool.wait_ge(tap_ready, t + 1)
                    if j > 1:
                        pool.wait_ge(tap_added, t)
                    G.tensor_tensor(out[:, 0:TOK], out[:, 0:TOK], tap_place(t)[:, 0:TOK], ALU.add).then_inc(tap_added, 1)

            conv_taps(0, EARLY_TAPS)

            def gates(_, i):
                if i == 0:
                    n = TILES[4][1]
                    pool.wait_ge(gates_ready, 1)
                    pool.wait_ge(psum_free, U_OUT)
                    G.tensor_tensor(gx[0:n], over_cols(gate["g"][0:n, 4, :], NG), over_heads(mask[0:n, MASK["group"]], n),
                                    ALU.mult).then_inc(s["gx_ready"], 1)

            def prep(t, i):
                c0, n = TILES[t]
                p = t % 2
                if i == 6:
                    pool.wait_ge(s["e_ready"], t + 1)
                    G.tensor_tensor(E_[p][0:n, :, 0:n], E_[p][0:n, :, 0:n], over_heads(tile_mask("incl", t), n),
                                    ALU.mult).then_inc(s["em_ready"], 1)
                    pool.wait_ge(s["em_ready"], t + 1)
                    pool.wait_ge(s["bs_ready"], t + 1)
                    G.tensor_tensor(ES[p][0:n, :, 0:n], ES[p][0:n, :, 0:n], E_[p][0:n, :, 0:n],
                                    ALU.mult).then_inc(s["es_ready"], 1)
                if i == 7:
                    e = EG[:, t % 4]
                    pool.wait_ge(s["eg_ready"], t + 1)
                    pool.wait_ge(s["qk_normed"], t + 1)
                    if t == 4:
                        pool.wait_ge(s["o_ps"], 2)
                        G.tensor_tensor(EG[:, 1][:, :, 0:n], e[:, :, 0:n], qkv[:, H:2 * H, c0:c0 + n],
                                        ALU.mult).then_inc(s["ek_ready"], 1)
                    G.tensor_tensor(e[:, :, 0:n], e[:, :, 0:n], qkv[:, 0:H, c0:c0 + n], ALU.mult).then_inc(s["qg_ready"], 1)

            def tok(t, i):
                pass

            def blocks(t, l):
                n = TILES[t][1]
                p = t % 2
                G.tensor_tensor(BM[p][0:n, :, 0:n], AT[p][0:n, :, 0:n], over_heads(m("levels", n, l), n),
                                ALU.mult).then_inc(s["b_ready"][p], 1)

            def start(t, i):
                if i == 0:
                    pool.wait_ge(s["at_ready"], t + 1)
                    blocks(t, 1)

            def level(t, i):
                l, i = i // 2, i % 2
                p, a, b, ly, lx = chain_at(t)
                if i == 1 and l + 1 < LEVELS[t]:
                    pool.wait_ge(s["t1_ps"][p], lx + l)
                    blocks(t, l + 1)

            def end(t, i):
                pass

            def scan(t, i):
                pass

            def conv(c, _):
                pass

            def samples(hd, _):
                pool.wait_ge(s["ss_ps"], hd + 1)
                G.tensor_tensor(S[:, hd, 1:NG], S[:, hd, 1:NG], over_cols(f_group[:, NG * hd + 1:NG * (hd + 1)], P),
                                ALU.mult).then_inc(s["s_scaled"], 1)

            def taps_step(_, i):
                conv_taps(EARLY_TAPS + 2 * i, EARLY_TAPS + 2 * i + 2)

            def final(_, i):
                n = TILES[4][1]
                if 4 <= i < 4 + H:
                    hd = i - 4
                    pool.wait_ge(s["vn_ready"], 5)
                    if hd == 1:
                        pool.wait_ge(cn_ps, NC_)
                    if hd >= 2:
                        pool.wait_ge(s["s4_ps"], hd - 1)
                    G.tensor_tensor(VX[hd % 2].rearrange("p (g c) -> p g c", g=NG),
                                    VN[0:n, hd, :].unsqueeze(1).to_broadcast([n, NG, P]),
                                    mask[0:n, MASK["group"]].unsqueeze(2).to_broadcast([n, NG, P]),
                                    ALU.mult).then_inc(s["vx_ready"], 1)

            def weights_split(j, _):
                pass

            steps = {"gates": gates, "prep": prep, "tok": tok, "start": start, "level": level, "end": end, "scan": scan,
                     "conv": conv, "samples": samples, "final": final, "weights": weights_split, "taps": taps_step}
            for name, t, i in delta_schedule():
                steps[name](t, i)
            sum_squares(2)
            sum_squares(3)


_OUTS = {"y_t": (P, KT, TOK), "new_state": (P, H, NG, P), "last_q": (P, NQ, 27), "last_c": (P, NC_, 270)}


def feature_tiles(a):
    return np.ascontiguousarray(a.T.reshape(-1, P, a.shape[0]).transpose(1, 0, 2))


def unit_list(i):
    w_in = i["w_in"][0]
    qkv_z = NQ * P + H * P
    glu = qkv_z + 2 * H
    units = np.zeros((U_END, P, KT, P), np.float32)
    at = [0]

    def add(w, r0, rows, c0):
        block = w[r0 * P:(r0 + rows) * P, c0:c0 + P]
        units[at[0], :, 0:rows, :] = block.reshape(rows, P, P).transpose(1, 0, 2)
        at[0] += 1

    def ffn(w1, w3, w2):
        g = 0
        for n in PARTS:
            for f in range(g, g + n):
                add(w1, 0, KT, f * P)
                add(w3, 0, KT, f * P)
            for k in range(KT):
                add(w2, g, n, k * P)
            g += n

    ffn(i["ffn1_w1"][0], i["ffn1_w3"][0], i["ffn1_w2"][0])
    for c in range(NC_):
        add(w_in, 0, KT, glu + c * P)
        add(w_in, 0, KT, glu + (NC_ + c) * P)
    for c in range(NQ + H):
        add(w_in, 0, KT, c * P)
    for k in range(KT):
        add(i["w_out"][0], 0, KT, k * P)
    ffn(i["ffn2_w1"][0], i["ffn2_w3"][0], i["ffn2_w2"][0])
    assert at[0] == U_END
    return units


def kernel(**inputs):
    import concourse.bacc as bacc
    from concourse.bass_utils import run_bass_kernel_spmd

    i = {k: np.asarray(a) for k, a in inputs.items()}
    x = np.concatenate([i["meta_tokens"], i["x_prompt"][0], i["x_sample"].reshape(NB * LB, D)])
    vecs = np.zeros((P, NV), np.float32)
    for name in ("ffn1_norm", "mix_norm", "ffn2_norm", "conv_b", "conv_norm", "o_norm"):
        vecs[:, VEC[name]] = i[name][0].reshape(-1, P).T
    vecs[:, VEC["final_norm"]] = i["final_norm"].reshape(-1, P).T
    for name, w in (("qkv_conv_w", SC), ("conv_w", CW)):
        vecs[:, VEC[name]] = i[name][0].T.reshape(-1, P, w).transpose(1, 0, 2).reshape(P, -1)
    vecs[:, VEC["dt_bias"]] = i["dt_bias"][0]
    vecs[:, VEC["a_log"]] = i["a_log"][0]
    ba = i["w_in"][0][:, (NQ + H) * P:(NQ + H) * P + 2 * H]
    vecs[:, VEC["w_ba"]] = ba.reshape(KT, P, 2 * H).transpose(1, 0, 2).reshape(P, -1)
    arrays = {
        "weights": unit_list(i),
        "x_t": feature_tiles(x),
        "vecs": vecs,
        "masks": shape_masks(),
        "hist_q": feature_tiles(i["state_qkv_conv"][0].reshape(NB * (SC - 1), NQ * P)),
        "hist_c": np.ascontiguousarray(
            feature_tiles(i["state_conv"][0].reshape(NB * (CW - 1), NC_ * P)).reshape(P, NC_, NB, CW - 1)),
        "states": np.ascontiguousarray(i["state_delta"][0].transpose(2, 1, 0, 3)),
    }
    nc = bacc.Bacc("TRN2", target_bir_lowering=False, num_devices=1)
    args = [nc.dram_tensor(n, a.shape, mybir.dt.from_np(a.dtype), kind="ExternalInput").ap() for n, a in arrays.items()]
    args += [nc.dram_tensor(n, shape, F32, kind="ExternalOutput").ap() for n, shape in _OUTS.items()]
    build(nc, *args)
    r = run_bass_kernel_spmd(nc, [arrays], core_ids=[0]).results[0]
    y = r["y_t"].transpose(2, 1, 0).reshape(TOK, D)
    st = r["new_state"].transpose(1, 2, 0, 3)
    lq = r["last_q"].transpose(2, 1, 0).reshape(27, NQ * P)
    lc = r["last_c"].transpose(2, 1, 0).reshape(270, NC_ * P)
    c = np.ascontiguousarray
    return (c(y[N_META:L][None]), c(y[L:].reshape(NB, LB, D)), c(st[:, 0][None, None]),
            c(lq[0:3][None, None]), c(lc[0:30][None, None]), c(st[:, 1:].transpose(1, 0, 2, 3)[None]),
            c(lq[3:].reshape(1, NB, SC - 1, NQ * P)), c(lc[30:].reshape(1, NB, CW - 1, NC_ * P)))
```
